# Optimizing a Trainium2 kernel written in Bass

```python
import math
import jax, jax.numpy as jnp
from jax import lax
import numpy as np

D_MODEL = 1024
BATCH = 1
SEQ = 1024
DEPTH = 1

GDN_HEADS = 8
GDN_DK = 128
GDN_DV = 128
CONV_K = 4
CHUNK = 64
DSA_HEADS = 8
DSA_DH = 128
KV_RANK = 256
IDX_HEADS = 8
IDX_DIM = 64
TOPK_MAX = 256
Q_BLOCK = 128
NUM_BUCKETS = 32
MAX_DISTANCE = 128
EPS = 1e-6

GDN_W = GDN_HEADS * GDN_DV
DSA_W = DSA_HEADS * DSA_DH
SPLITS = (GDN_HEADS * GDN_DK, GDN_HEADS * GDN_DK, GDN_W,
          GDN_W, GDN_HEADS, GDN_HEADS,
          DSA_W, KV_RANK, DSA_W,
          IDX_HEADS * IDX_DIM, IDX_DIM, IDX_HEADS,
          2 * D_MODEL)
PROJ_W = sum(SPLITS)

kernel_name = 'hybrid_gdn_dsa_gated_merge_block'

def _split_points(sizes):
    pts, acc = [], 0
    for s in sizes[:-1]:
        acc += s
        pts.append(acc)
    return pts

def rms_norm(x, g):
    xf = x.astype(jnp.float32)
    y = xf * lax.rsqrt(jnp.mean(xf * xf, axis=-1, keepdims=True) + EPS)
    return (y * g.astype(jnp.float32)).astype(x.dtype)

def l2norm(x):
    return x * lax.rsqrt(jnp.sum(x * x, axis=-1, keepdims=True) + EPS)

def causal_dwconv_silu(u, w):
    C = u.shape[-1]
    y = lax.conv_general_dilated(u, w[:, None, :].astype(u.dtype), window_strides=(1,),
                                 padding=[(CONV_K - 1, 0)],
                                 dimension_numbers=('NWC', 'WIO', 'NWC'),
                                 feature_group_count=C)
    return jax.nn.silu(y)

def gated_delta_rule(q, k, v, g, beta):
    B, T, H, DK = q.shape
    DV = v.shape[-1]
    N = T // CHUNK

    def chunks(a):
        return a.reshape(B, N, CHUNK, H, -1).transpose(0, 3, 1, 2, 4)

    q, k, v = chunks(q), chunks(k), chunks(v)
    g = g.reshape(B, N, CHUNK, H).transpose(0, 3, 1, 2)
    beta = beta.reshape(B, N, CHUNK, H).transpose(0, 3, 1, 2)
    decay = jnp.cumsum(g, axis=-1)
    pos = jnp.arange(CHUNK)
    causal = pos[:, None] >= pos[None, :]
    strict = pos[:, None] > pos[None, :]
    gamma = jnp.exp(jnp.where(causal, decay[..., :, None] - decay[..., None, :], -jnp.inf))
    kb = k * beta[..., None]
    a_mat = jnp.where(strict, jnp.einsum('bhnid,bhnjd->bhnij', kb, k) * gamma, 0.0)
    eye = jnp.eye(CHUNK, dtype=q.dtype)
    rhs = jnp.concatenate([v * beta[..., None], kb * jnp.exp(decay)[..., None]], axis=-1)
    sol = lax.linalg.triangular_solve(a_mat + eye, rhs, left_side=True, lower=True)
    u, w = sol[..., :DV], sol[..., DV:]
    attn = jnp.einsum('bhnid,bhnjd->bhnij', q, k) * gamma
    qg = q * jnp.exp(decay)[..., None]
    d_last = decay[..., -1]
    k_dec = k * jnp.exp(d_last[..., None] - decay)[..., None]

    def step(S, xs):
        u_n, w_n, qg_n, attn_n, kd_n, dl_n = xs
        v_new = u_n - jnp.einsum('bhcd,bhde->bhce', w_n, S)
        o = jnp.einsum('bhcd,bhde->bhce', qg_n, S) + jnp.einsum('bhij,bhje->bhie', attn_n, v_new)
        S = S * jnp.exp(dl_n)[..., None, None] + jnp.einsum('bhcd,bhce->bhde', kd_n, v_new)
        return S, o

    xs = tuple(jnp.moveaxis(a, 2, 0) for a in (u, w, qg, attn, k_dec, d_last))
    S0 = jnp.zeros((B, H, DK, DV), q.dtype)
    _, o = lax.scan(step, S0, xs)
    return o.transpose(1, 0, 3, 2, 4).reshape(B, T, H, DV)

def t5_bucket(dist):
    n = jnp.maximum(dist, 0)
    max_exact = NUM_BUCKETS // 2
    nf = jnp.maximum(n, 1).astype(jnp.float32)
    large = max_exact + (jnp.log(nf / max_exact) / math.log(MAX_DISTANCE / max_exact)
                         * (NUM_BUCKETS - max_exact)).astype(jnp.int32)
    large = jnp.minimum(large, NUM_BUCKETS - 1)
    return jnp.where(n < max_exact, n, large)

def dsa_attention(q_lat, c_kv, q_idx, k_idx, w_idx, rel_bias):
    B, T, H, DC = q_lat.shape
    S = c_kv.shape[1]
    k_sel = min(TOPK_MAX, S // 4)
    nb = T // Q_BLOCK
    f32 = jnp.float32

    def blocks(a):
        return jnp.moveaxis(a.reshape(B, nb, Q_BLOCK, *a.shape[2:]), 1, 0)

    key_pos = jnp.arange(S)
    k_idx32 = k_idx.astype(f32)

    def one_block(xs):
        ql, qi, wi, t0 = xs
        t = t0 + jnp.arange(Q_BLOCK)
        dots = jnp.einsum('bqhd,bsd->bqhs', qi.astype(f32), k_idx32)
        score = jnp.einsum('bqh,bqhs->bqs', wi.astype(f32), jax.nn.relu(dots))
        admissible = key_pos[None, :] <= t[:, None]
        score = jnp.where(admissible[None], score, -jnp.inf)
        _, sel = lax.top_k(score, k_sel)
        valid = sel <= t[None, :, None]
        kv = jax.vmap(lambda ck, ii: ck[ii])(c_kv, sel)
        logits = jnp.einsum('bqhc,bqkc->bqhk', ql, kv).astype(f32)
        bias = rel_bias[t5_bucket(t[None, :, None] - sel)]
        logits = logits + jnp.moveaxis(bias, -1, 2).astype(f32)
        logits = jnp.where(valid[:, :, None, :], logits, -jnp.inf)
        p = jax.nn.softmax(logits, axis=-1).astype(kv.dtype)
        return jnp.einsum('bqhk,bqkc->bqhc', p, kv)

    t0s = jnp.arange(nb) * Q_BLOCK
    o = lax.map(one_block, (blocks(q_lat), blocks(q_idx), blocks(w_idx), t0s))
    return jnp.moveaxis(o, 0, 1).reshape(B, T, H, DC)

def setup_inputs(seed: int = 0) -> dict:
    key = jax.random.key(seed)
    ks = jax.random.split(key, 20)
    nrm = jax.random.normal
    D = D_MODEL
    x = nrm(ks[0], (BATCH, SEQ, D), jnp.float32)
    c = nrm(ks[1], (BATCH, D), jnp.float32)
    norm_g = 1.0 + 0.02 * nrm(ks[2], (DEPTH, D), jnp.float32)
    w_ada = nrm(ks[3], (DEPTH, D, 3 * D), jnp.float32) * D ** -0.5
    b_ada = 0.01 * nrm(ks[4], (DEPTH, 3 * D), jnp.float32)
    w_in = nrm(ks[5], (DEPTH, D, PROJ_W), jnp.float32) * D ** -0.5
    conv_w = nrm(ks[6], (DEPTH, CONV_K, 2 * GDN_HEADS * GDN_DK + GDN_W), jnp.float32) * CONV_K ** -0.5
    a_log = jnp.log(jax.random.uniform(ks[7], (DEPTH, GDN_HEADS), jnp.float32, 1.0, 16.0))
    dt = jnp.exp(jax.random.uniform(ks[8], (DEPTH, GDN_HEADS), jnp.float32,
                                    math.log(1e-3), math.log(1e-1)))
    dt_bias = jnp.log(jnp.expm1(dt))
    gdn_norm_g = 1.0 + 0.02 * nrm(ks[9], (DEPTH, GDN_DV), jnp.float32)
    w_o_gdn = nrm(ks[10], (DEPTH, GDN_W, D), jnp.float32) * GDN_W ** -0.5
    kv_norm_g = 1.0 + 0.02 * nrm(ks[11], (DEPTH, KV_RANK), jnp.float32)
    w_uk = nrm(ks[12], (DEPTH, KV_RANK, DSA_HEADS, DSA_DH), jnp.float32) * KV_RANK ** -0.5
    w_uv = nrm(ks[13], (DEPTH, KV_RANK, DSA_HEADS, DSA_DH), jnp.float32) * KV_RANK ** -0.5
    w_o_dsa = nrm(ks[14], (DEPTH, DSA_W, D), jnp.float32) * DSA_W ** -0.5
    w_out = nrm(ks[15], (DEPTH, D, D), jnp.float32) * D ** -0.5
    rel_bias = 0.5 * nrm(ks[16], (NUM_BUCKETS, DSA_HEADS), jnp.float32)
    final_g = 1.0 + 0.02 * nrm(ks[17], (D,), jnp.float32)
    return {'x': x, 'c': c, 'norm_g': norm_g, 'w_ada': w_ada, 'b_ada': b_ada, 'w_in': w_in,
            'conv_w': conv_w, 'a_log': a_log, 'dt_bias': dt_bias, 'gdn_norm_g': gdn_norm_g,
            'w_o_gdn': w_o_gdn, 'kv_norm_g': kv_norm_g, 'w_uk': w_uk, 'w_uv': w_uv,
            'w_o_dsa': w_o_dsa, 'w_out': w_out, 'rel_bias': rel_bias, 'final_g': final_g}

def reference(x, c, norm_g, w_ada, b_ada, w_in, conv_w, a_log, dt_bias, gdn_norm_g, w_o_gdn,
              kv_norm_g, w_uk, w_uv, w_o_dsa, w_out, rel_bias, final_g):
    B, T, D = x.shape
    f32 = jnp.float32
    pts = _split_points(SPLITS)
    qkv_pts = [GDN_HEADS * GDN_DK, 2 * GDN_HEADS * GDN_DK]
    for l in range(DEPTH):
        mod = jax.nn.silu(c) @ w_ada[l] + b_ada[l]
        shift, scale, gate = jnp.split(mod, 3, axis=-1)
        h = rms_norm(x, norm_g[l]) * (1.0 + scale[:, None]) + shift[:, None]
        proj = h @ w_in[l]
        (qa, ka, va, za, aa, ba, qb, ckv, zb, qi, ki, wi, gl) = jnp.split(proj, pts, axis=-1)

        qkv = causal_dwconv_silu(jnp.concatenate([qa, ka, va], axis=-1), conv_w[l])
        qa, ka, va = jnp.split(qkv, qkv_pts, axis=-1)
        qa = l2norm(qa.reshape(B, T, GDN_HEADS, GDN_DK).astype(f32)) * GDN_DK ** -0.5
        ka = l2norm(ka.reshape(B, T, GDN_HEADS, GDN_DK).astype(f32))
        va = va.reshape(B, T, GDN_HEADS, GDN_DV).astype(f32)
        beta = jax.nn.sigmoid(ba.astype(f32))
        g = -jnp.exp(a_log[l].astype(f32)) * jax.nn.softplus(aa.astype(f32) + dt_bias[l].astype(f32))
        oa = gated_delta_rule(qa, ka, va, g, beta)
        oa = rms_norm(oa, gdn_norm_g[l]).astype(x.dtype).reshape(B, T, GDN_W) * jax.nn.silu(za)
        ya = oa @ w_o_gdn[l]

        ckv = rms_norm(ckv, kv_norm_g[l])
        qb = qb.reshape(B, T, DSA_HEADS, DSA_DH)
        q_lat = jnp.einsum('bthd,chd->bthc', qb, w_uk[l]) * DSA_DH ** -0.5
        qi = qi.reshape(B, T, IDX_HEADS, IDX_DIM)
        wi = wi * (IDX_HEADS ** -0.5 * IDX_DIM ** -0.5)
        o_lat = dsa_attention(q_lat, ckv, qi, ki, wi, rel_bias)
        ob = jnp.einsum('bthc,chd->bthd', o_lat, w_uv[l]).reshape(B, T, DSA_W) * jax.nn.silu(zb)
        yb = ob @ w_o_dsa[l]

        ga, gb = jnp.split(jax.nn.sigmoid(gl), 2, axis=-1)
        out = (ga * ya + gb * yb) @ w_out[l]
        x = x + gate[:, None] * out
    return rms_norm(x, final_g)


_drawn_inputs = setup_inputs


def setup_inputs(seed=0):
    import zlib

    import numpy as np

    out = dict(_drawn_inputs(seed))
    spreads = {}
    factors = {'norm_g': 5.61,
     'b_ada': 6.559,
     'gdn_norm_g': 28.98,
     'kv_norm_g': 8.0,
     'rel_bias': 3.61,
     'final_g': 7.96}
    for name, (base, spread) in spreads.items():
        noise = np.random.default_rng([zlib.crc32(name.encode()), seed]).standard_normal(out[name].shape)
        drawn = base * np.exp(spread * noise) if base else spread * noise
        out[name] = __import__('jax').numpy.asarray(drawn.astype(out[name].dtype))
    for name, factor in factors.items():
        out[name] = (out[name] * factor).astype(out[name].dtype)
    return out
```

```python
import concourse.bass as bass
from concourse import mybir
from contextlib import ExitStack
import numpy as np

F32 = mybir.dt.float32
F16 = mybir.dt.float16
BF16 = mybir.dt.bfloat16
ALU = mybir.AluOpType
ACT = mybir.ActivationFunctionType
AX = mybir.AxisListType

P = 128
T = 1024
D = 1024
NT = T // P
KD = D // P
H = 8
CHUNK = 64
IDX_DIM = 64
RANK = 256
TOPK = 256
NBUCKETS = 32
EPS = 1e-6
BANK = 512
HALVES = T // BANK

C_Q, C_K, C_V, C_ZA, C_AA, C_BA = 0, 1024, 2048, 3072, 4096, 4104
C_QB, C_CKV, C_ZB, C_QI, C_KI, C_WI, C_GL = 4112, 5136, 5392, 6416, 6928, 6992, 7000
UNIT = 256

BELOW = -3.0e38
TAKEN = float(np.finfo(np.float32).min)
CLOSED = -1.0e30

K_ID, K_FLIP, K_UPTO, K_AFTER, K_CH0, K_CH1, K_CAUSAL, K_LEVEL = 0, 128, 256, 384, 512, 640, 768, 896
K_ALL = K_LEVEL + 6 * 128
K_BUCKETS = 384


def constant_table():
    t = np.zeros((P, K_ALL), np.float32)
    i = np.arange(P)
    row, col = i[:, None], i[None, :]
    same = row // CHUNK == col // CHUNK
    t[:, K_ID:K_ID + P] = row == col
    t[:, K_FLIP:K_FLIP + P] = row + col == P - 1
    t[:, K_UPTO:K_UPTO + P] = same & (row <= col)
    t[:, K_AFTER:K_AFTER + P] = same & (row > col)
    t[:, K_CH0:K_CH0 + P] = row < CHUNK
    t[:, K_CH1:K_CH1 + P] = row >= CHUNK
    t[:, K_CAUSAL:K_CAUSAL + P] = np.where(col > row, BELOW, 0)
    for level in range(6):
        b = 1 << level
        m = (row // (2 * b) == col // (2 * b)) & (row % (2 * b) < b) & (col % (2 * b) >= b)
        t[:, K_LEVEL + level * P:K_LEVEL + (level + 1) * P] = m
    return t


def bucket_table():
    n = np.maximum(255 - np.arange(K_BUCKETS), 0)
    nf = np.maximum(n, 1).astype(np.float32)
    large = 16 + (np.log(nf / np.float32(16)) / np.float32(np.log(128 / 16)) * np.float32(16)).astype(np.int32)
    bucket = np.where(n < 16, n, np.minimum(large, NBUCKETS - 1))
    return (np.arange(NBUCKETS)[:, None] == bucket[None, :]).astype(np.float32)


class Tensors:
    pass


def three(pe, out, a_hi, a_lo, b_hi, b_lo, first, last):
    pe.matmul(out, a_hi, b_hi, start=first, stop=False)
    pe.matmul(out, a_hi, b_lo, start=False, stop=False)
    return pe.matmul(out, a_lo, b_hi, start=False, stop=last)


def phase_hidden(nc, g):
    with ExitStack() as ctx:
        sb = lambda n, s, d=F32: ctx.enter_context(nc.sbuf_tensor("a_" + n, s, d))
        sem = lambda n: nc.alloc_semaphore("a_" + n)
        x_sb = sb("x", [P, NT, D])
        w_ada = sb("w_ada", [P, KD, 3 * D])
        rows = sb("rows", [32, P])
        cols32 = sb("cols32", [P, 32])
        sc_col = sb("sc_col", [P, KD])
        b_gate = sb("b_gate", [P, D])
        mod = sb("mod", [P, 16])
        g1 = sb("g1", [P, KD])
        junk = sb("junk", [P, D])
        ss = sb("ss", [P, NT])
        rstd = sb("rstd", [P, 2, NT])
        h32 = sb("h32", [P, 2, BANK])
        gate = sb("gate", [P, D])
        small, x_in, ada_in = sem("small"), [sem(f"x_in{i}") for i in range(NT)], [sem(f"ada_in{k}") for k in range(KD)]
        silu, squares, root, inv, scaled = sem("silu"), sem("squares"), sem("root"), sem("inv"), sem("scaled")
        mod_mm, mod_ok, g1_ok, gscale = sem("mod_mm"), sem("mod_ok"), sem("g1_ok"), sem("gscale")
        turned, h_ok, hi_ok, lo_ok = sem("turned"), sem("h_ok"), sem("hi_ok"), sem("lo_ok")
        gate_mm, col_mm, col_ok, gate_ok, gate_sum, gate_out = sem("gate_mm"), sem("col_mm"), sem("col_ok"), sem("gate_ok"), sem("gate_sum"), sem("gate_out")
        bank = lambda k: g.ps[:, k * BANK:(k + 1) * BANK]
        block = ctx.enter_context(nc.Block())

        @block.sync
        def _(sp):
            sp.dma_start(rows[0:16, :], g.b_ada[0, 0:2 * D].rearrange("(k p) -> k p", p=P)).then_inc(small, 16)
            sp.dma_start(rows[16:24, :], g.c[0].rearrange("(k p) -> k p", p=P)).then_inc(small, 16)
            sp.dma_start(rows[24:32, :], g.norm_g[0].rearrange("(k p) -> k p", p=P)).then_inc(small, 16)
            sp.dma_start(g.const[:], g.const_dram).then_inc(small, 16)
            for i in range(NT):
                sp.dma_start(x_sb[:, i, :], g.x[0, i * P:(i + 1) * P, :]).then_inc(x_in[i], 16)
            sp.dma_start(b_gate[:], g.b_ada[0, 2 * D:3 * D].partition_broadcast(P)).then_inc(gate_ok, 16)
            sp.wait_ge(gate_sum, HALVES)
            sp.dma_start(g.gate_dram, gate[0:1, :]).then_inc(gate_out, 16)
            sp.wait_ge(gate_out, 16)

        @block.scalar
        def _(act):
            for k in range(KD):
                act.dma_start(w_ada[:, k, :], g.w_ada[0, k * P:(k + 1) * P, :]).then_inc(ada_in[k], 16)
            act.wait_ge(col_ok, 1)
            nc.scalar.activation(sc_col[:], cols32[:, 16:24], ACT.Silu).then_inc(silu, 1)
            for i in range(NT):
                act.wait_ge(x_in[i], 16)
                if i:
                    act.wait_ge(squares, i)
                nc.scalar.activation(junk[:], x_sb[:, i, :], ACT.Square, accum_out=ss[:, i:i + 1]).then_inc(squares, 1)
            act.wait_ge(inv, 1)
            nc.scalar.activation(rstd[:, 1, :], rstd[:, 0, :], ACT.Sqrt).then_inc(root, 1)
            act.wait_ge(g1_ok, 1)
            for n in range(KD * HALVES):
                k = n // HALVES
                act.wait_ge(turned, n + 1)
                if n >= 2:
                    act.wait_ge(lo_ok, n - 1)
                nc.scalar.activation(h32[:, n % 2, :], bank(n % 4), ACT.Identity, bias=mod[:, k:k + 1],
                                     scale=g1[:, k:k + 1]).then_inc(h_ok, 1)

        @block.vector
        def _(dve):
            dve.wait_ge(col_mm, 1)
            nc.vector.tensor_copy(cols32[:], g.ps[:, 7 * BANK:7 * BANK + 32]).then_inc(col_ok, 1)
            dve.wait_ge(squares, NT)
            nc.vector.tensor_scalar(rstd[:, 0, :], ss[:], 1.0 / D, EPS, ALU.mult, ALU.add).then_inc(inv, 1)
            dve.wait_ge(root, 1)
            nc.vector.reciprocal(ss[:], rstd[:, 1, :]).then_inc(inv, 1)
            dve.wait_ge(inv, 2)
            for i in range(NT):
                nc.vector.tensor_scalar(x_sb[:, i, :], x_sb[:, i, :], ss[:, i:i + 1], None, ALU.mult).then_inc(scaled, 1)
            dve.wait_ge(mod_mm, 1)
            nc.vector.tensor_tensor(mod[:], g.ps[:, 4 * BANK:4 * BANK + 16], cols32[:, 0:16], ALU.add).then_inc(mod_ok, 1)
            dve.wait_ge(mod_ok, 1)
            nc.vector.scalar_tensor_tensor(out=g1[:], in0=mod[:, KD:2 * KD], scalar=1.0, in1=cols32[:, 24:32],
                                           op0=ALU.add, op1=ALU.mult).then_inc(g1_ok, 1)
            for n in range(KD * HALVES):
                k, half = divmod(n, HALVES)
                dve.wait_ge(h_ok, n + 1)
                nc.vector.tensor_copy(g.h_hi[:, k, half * BANK:(half + 1) * BANK], h32[:, n % 2, :]).then_inc(hi_ok, 1)
            dve.wait_ge(gate_mm, 1)
            dve.wait_ge(gate_ok, 16)
            for half in range(HALVES):
                cols = slice(half * BANK, (half + 1) * BANK)
                nc.vector.tensor_tensor(gate[:, cols], bank(5 + half), b_gate[:, cols], ALU.add).then_inc(gate_sum, 1)

        @block.gpsimd
        def _(pool):
            for n in range(KD * HALVES):
                k, half = divmod(n, HALVES)
                cols = slice(half * BANK, (half + 1) * BANK)
                pool.wait_ge(hi_ok, n + 1)
                nc.gpsimd.tensor_tensor(g.h_lo[:, k, cols], h32[:, n % 2, :], g.h_hi[:, k, cols],
                                        ALU.subtract).then_inc(lo_ok, 1)

        @block.tensor
        def _(pe):
            pe.wait_ge(small, 64)
            nc.tensor.transpose(g.ps[:, 7 * BANK:7 * BANK + 32], rows[:], g.const[0:32, K_ID:K_ID + 32]).then_inc(col_mm, 1)
            pe.wait_ge(silu, 1)
            for k in range(KD):
                pe.wait_ge(ada_in[k], 16)
                for j in range(16):
                    last = nc.tensor.matmul(g.ps[:, 4 * BANK + j:4 * BANK + j + 1], w_ada[:, k, j * P:(j + 1) * P],
                                            sc_col[:, k:k + 1], start=(k == 0 and j == 0), stop=(k == KD - 1),
                                            skip_group_check=True)
            last.then_inc(mod_mm, 1)
            for half in range(HALVES):
                for k in range(KD):
                    last = nc.tensor.matmul(bank(5 + half), sc_col[:, k:k + 1].broadcast_to([P, P]),
                                            w_ada[:, k, 2 * D + half * BANK:2 * D + (half + 1) * BANK],
                                            start=(k == 0), stop=(k == KD - 1))
            last.then_inc(gate_mm, 1)
            pe.wait_ge(scaled, NT)
            for n in range(KD * HALVES):
                k, half = divmod(n, HALVES)
                if n >= 4:
                    pe.wait_ge(h_ok, n - 3)
                for j in range(4):
                    last = nc.tensor.transpose(g.ps[:, (n % 4) * BANK + j * P:(n % 4) * BANK + (j + 1) * P],
                                               x_sb[:, half * 4 + j, k * P:(k + 1) * P], g.const[:, K_ID:K_ID + P])
                last.then_inc(turned, 1)


def phase_index(nc, g):
    with ExitStack() as ctx:
        sb = lambda n, s, d=F32: ctx.enter_context(nc.sbuf_tensor("b_" + n, s, d))
        sem = lambda n: nc.alloc_semaphore("b_" + n)
        NS = 152
        s32, s_hi, s_lo = sb("s32", [P, KD, NS]), sb("s_hi", [P, KD, NS], F16), sb("s_lo", [P, KD, NS], BF16)
        w32, w_hi, w_lo = sb("w32", [P, 2, KD, UNIT]), sb("w_hi", [P, 2, KD, UNIT], F16), sb("w_lo", [P, 2, KD, UNIT], BF16)
        k_hi, k_lo = sb("k_hi", [P, 2, T], F16), sb("k_lo", [P, 2, T], F16)
        q_hi, q_lo = sb("q_hi", [P, 4, T], F16), sb("q_lo", [P, 4, T], F16)
        relu = sb("relu", [P, 4, T])
        s_in, w_in = sem("s_in"), [sem("w_in0"), sem("w_in1")]
        w_cast, w_ready = sem("w_cast"), sem("w_ready")
        proj, hi_ok, lo_ok, zero = sem("proj"), sem("hi_ok"), sem("lo_ok"), sem("zero")
        dots, relu_ok, acc, small_ok = sem("dots"), sem("relu_ok"), sem("acc"), sem("small_ok")
        bank = lambda k: g.ps[:, k * BANK:(k + 1) * BANK]
        win = g.w_in[0].rearrange("(k p) n -> p k n", p=P)
        block = ctx.enter_context(nc.Block())

        @block.sync
        def _(sp):
            for at, c0, n in ((0, C_KI, 64), (64, C_KI, 64), (128, C_WI, 8), (136, C_AA, 16)):
                sp.dma_start(s32[:, :, at:at + n], win[:, :, c0:c0 + n]).then_inc(s_in, 16)
            for u in range(2):
                sp.dma_start(w32[:, u], win[:, :, C_QI + u * UNIT:C_QI + (u + 1) * UNIT]).then_inc(w_in[u], 16)

        @block.gpsimd
        def _(pool):
            pool.wait_ge(s_in, 64)
            nc.gpsimd.tensor_copy(s_hi[:], s32[:]).then_inc(w_cast, 1)
            pool.wait_ge(w_cast, 1)
            nc.gpsimd.tensor_tensor(s_lo[:], s32[:], s_hi[:], ALU.subtract).then_inc(w_ready, 1)
            for u in range(2):
                pool.wait_ge(w_in[u], 16)
                nc.gpsimd.tensor_copy(w_hi[:, u], w32[:, u]).then_inc(w_cast, 1)
                pool.wait_ge(w_cast, 2 + u)
                nc.gpsimd.tensor_tensor(w_lo[:, u], w32[:, u], w_hi[:, u], ALU.subtract).then_inc(w_ready, 1)

        @block.tensor
        def _(pe):
            pe.wait_ge(w_ready, 1)
            for half in range(HALVES):
                cols = slice(half * BANK, (half + 1) * BANK)
                for k in range(KD):
                    last = three(nc.tensor, bank(half), s_hi[:, k, 0:P], s_lo[:, k, 0:P],
                                 g.h_hi[:, k, cols], g.h_lo[:, k, cols], k == 0, k == KD - 1)
                last.then_inc(proj, 1)
            for i in range(NT):
                for k in range(KD):
                    last = three(nc.tensor, g.ps[:, 2 * BANK + i * 24:2 * BANK + (i + 1) * 24],
                                 g.h_hi[:, k, i * P:(i + 1) * P], g.h_lo[:, k, i * P:(i + 1) * P],
                                 s_hi[:, k, P:NS], s_lo[:, k, P:NS], k == 0, k == KD - 1)
            last.then_inc(proj, 1)
            pe.wait_ge(w_ready, 3)
            with pe.Fori(0, 2) as u:
                for b in range(2):
                    for half in range(HALVES):
                        cols = slice(half * BANK, (half + 1) * BANK)
                        n = 2 * b + half
                        pe.wait_ge(lo_ok, u * (5 + n) + 1)
                        for k in range(KD):
                            last = three(nc.tensor, bank(3 + n), w_hi[:, bass.ds(u, 1), k, b * P:(b + 1) * P],
                                         w_lo[:, bass.ds(u, 1), k, b * P:(b + 1) * P],
                                         g.h_hi[:, k, cols], g.h_lo[:, k, cols], k == 0, k == KD - 1)
                        last.then_inc(proj, 1)
            pe.wait_ge(lo_ok, 8 + 4 + 1)
            for i in range(NT):
                width = (i + 1) * P
                with pe.Fori(0, 2) as turn:
                    for e in range(4):
                        pe.wait_ge(relu_ok, turn * 4 + (8 * i - 2 + e) if i else turn * (1 + e) + 1)
                        rows = (bass.ds(turn * 2 + e // 2, 1), slice(i * P, (i + 1) * P))
                        for c0 in range(0, width, BANK):
                            c1 = min(width, c0 + BANK)
                            last = three(nc.tensor, g.ps[:, e * T + c0:e * T + c1],
                                         q_hi[:, rows[0], rows[1]], q_lo[:, rows[0], rows[1]],
                                         k_hi[:, e % 2, c0:c1], k_lo[:, e % 2, c0:c1], True, True)
                        last.then_inc(dots, 1)

        @block.scalar
        def _(act):
            act.nop().then_inc(relu_ok, 1)
            act.wait_ge(zero, 1)
            for half in range(HALVES):
                cols = slice(half * BANK, (half + 1) * BANK)
                act.wait_ge(proj, half + 1)
                nc.scalar.copy(k_hi[0:64, 0, cols], bank(half)[0:64])
                nc.scalar.copy(k_hi[64:128, 1, cols], bank(half)[64:128]).then_inc(hi_ok, 1)
            act.wait_ge(proj, 3)
            nc.scalar.copy(g.small[:], g.ps[:, 2 * BANK:2 * BANK + NT * 24].rearrange("p (i n) -> p i n", n=24)).then_inc(small_ok, 1)
            with act.Fori(0, 2) as u:
                for b in range(2):
                    for half in range(HALVES):
                        n = 2 * b + half
                        act.wait_ge(proj, u * 4 + 4 + n)
                        nc.scalar.copy(q_hi[:, bass.ds(u * 2 + b, 1), half * BANK:(half + 1) * BANK],
                                       bank(3 + n)).then_inc(hi_ok, 1)
            for i in range(NT):
                with act.Fori(0, 2) as turn:
                    for e in range(4):
                        act.wait_ge(dots, turn * 4 + 8 * i + 1 + e)
                        act.wait_ge(acc, turn * 4 + (9 * i - 2 + e) if i else turn * (1 + e) + 1)
                        nc.scalar.activation(relu[:, e, 0:(i + 1) * P], g.ps[:, e * T:e * T + (i + 1) * P],
                                             ACT.Relu).then_inc(relu_ok, 1)

        @block.vector
        def _(dve):
            dve.nop().then_inc(lo_ok, 1)
            dve.nop().then_inc(acc, 1)
            nc.vector.memset(k_hi[64:128, 0, :], 0.0)
            nc.vector.memset(k_hi[0:64, 1, :], 0.0)
            nc.vector.memset(k_lo[64:128, 0, :], 0.0)
            nc.vector.memset(k_lo[0:64, 1, :], 0.0)
            nc.vector.memset(g.score[:], 0.0).then_inc(zero, 1)
            for half in range(HALVES):
                cols = slice(half * BANK, (half + 1) * BANK)
                dve.wait_ge(hi_ok, half + 1)
                nc.vector.tensor_tensor(k_lo[0:64, 0, cols], bank(half)[0:64], k_hi[0:64, 0, cols], ALU.subtract).then_inc(lo_ok, 1)
                nc.vector.tensor_tensor(k_lo[64:128, 1, cols], bank(half)[64:128], k_hi[64:128, 1, cols], ALU.subtract).then_inc(lo_ok, 1)
            dve.wait_ge(small_ok, 1)
            nc.vector.tensor_scalar(g.small[:, :, 0:8], g.small[:, :, 0:8], H ** -0.5 * IDX_DIM ** -0.5, None,
                                    ALU.mult).then_inc(small_ok, 1)
            with dve.Fori(0, 2) as u:
                for b in range(2):
                    for half in range(HALVES):
                        n = 2 * b + half
                        cols = slice(half * BANK, (half + 1) * BANK)
                        dve.wait_ge(hi_ok, u * 4 + 3 + n)
                        nc.vector.tensor_tensor(q_lo[:, bass.ds(u * 2 + b, 1), cols], bank(3 + n),
                                                q_hi[:, bass.ds(u * 2 + b, 1), cols], ALU.subtract).then_inc(lo_ok, 1)
            dve.wait_ge(small_ok, 2)
            dve.wait_ge(zero, 1)
            for i in range(NT):
                at = g.score[:, g.first[i]:g.first[i + 1]]
                with dve.Fori(0, 2) as turn:
                    for e in range(4):
                        dve.wait_ge(relu_ok, turn * 4 + 8 * i + 2 + e)
                        dve.wait_ge(acc, turn * 4 + 9 * i + e + 1)
                        nc.vector.scalar_tensor_tensor(out=at, in0=relu[:, e, 0:(i + 1) * P],
                                                       scalar=g.small[:, i, bass.ds(turn * 4 + e, 1)], in1=at,
                                                       op0=ALU.mult, op1=ALU.add).then_inc(acc, 1)
                dve.wait_ge(acc, 9 * i + 8 + 1)
                diag = g.score[:, g.first[i] + i * P:g.first[i + 1]]
                nc.vector.tensor_tensor(diag, diag, g.const[:, K_CAUSAL:K_CAUSAL + P], ALU.add).then_inc(acc, 1)


def phase_topk(nc, g):
    with ExitStack() as ctx:
        sb = lambda n, s, d=F32: ctx.enter_context(nc.sbuf_tensor("c_" + n, s, d))
        sem = lambda n: nc.alloc_semaphore("c_" + n)
        w32, w_hi, w_lo = sb("w32", [P, 2, KD, UNIT]), sb("w_hi", [P, 2, KD, UNIT], F16), sb("w_lo", [P, 2, KD, UNIT], BF16)
        stage = sb("stage", [P, 8, BANK])
        best = sb("best", [P, 2, 8])
        w_in, w_cast, w_ready = [sem("w_in0"), sem("w_in1")], sem("w_cast"), sem("w_ready")
        proj, gated, stored = sem("proj"), sem("gated"), [sem(f"stored{n}") for n in range(8)]
        top_ok, rep_ok, masked, mask_out = sem("top_ok"), sem("rep_ok"), sem("masked"), sem("mask_out")
        alone, pool_alone = sem("alone"), sem("pool_alone")
        bank = lambda k: g.ps[:, k * BANK:(k + 1) * BANK]
        win = g.w_in[0].rearrange("(k p) n -> p k n", p=P)
        columns = [C_ZA + n * UNIT for n in range(4)] + [C_ZB + n * UNIT for n in range(4)] + [C_GL + n * UNIT for n in range(8)]
        block = ctx.enter_context(nc.Block())

        @block.sync
        def _(sp):
            for u, c0 in enumerate(columns):
                if u >= 2:
                    sp.wait_ge(w_ready, u - 1)
                sp.dma_start(w32[:, u % 2], win[:, :, c0:c0 + UNIT]).then_inc(w_in[u % 2], 16)
            sp.wait_ge(masked, NT)
            sp.dma_start(g.mask_dram, g.mask[:]).then_inc(mask_out, 16)
            sp.wait_ge(mask_out, 16)
            for n in range(8):
                sp.wait_ge(stored[n], 16 * 10 + 1)

        @block.gpsimd
        def _(pool):
            def split(s, arrived, free, n):
                pool.wait_ge(w_in[s], arrived).then_inc(pool_alone, 1)
                pool.wait_ge(proj, free).then_inc(pool_alone, 1)
                nc.gpsimd.tensor_copy(w_hi[:, s], w32[:, s]).then_inc(w_cast, 1)
                pool.wait_ge(w_cast, n + 1)
                nc.gpsimd.tensor_tensor(w_lo[:, s], w32[:, s], w_hi[:, s], ALU.subtract).then_inc(w_ready, 1)

            with pool.Fori(0, 2) as t:
                for s in range(2):
                    split(s, t * 16 + 16, t * 16 + 8 * s, t * 2 + s)
            with pool.Fori(0, 6) as t:
                for s in range(2):
                    split(s, t * 16 + 48, t * 8 + 36 + 4 * s, t * 2 + 4 + s)

        @block.tensor
        def _(pe):
            pe.nop().then_inc(proj, 8)
            with pe.Fori(0, 2) as t:
                for s in range(2):
                    pe.wait_ge(w_ready, t * 2 + s + 1)
                    for i in range(NT):
                        pe.wait_ge(gated, t * 16 + s * 8 + i + 1)
                        for k in range(KD):
                            last = three(nc.tensor, g.ps[:, i * BANK:i * BANK + UNIT],
                                         g.h_hi[:, k, i * P:(i + 1) * P], g.h_lo[:, k, i * P:(i + 1) * P],
                                         w_hi[:, s, k], w_lo[:, s, k], k == 0, k == KD - 1)
                        last.then_inc(proj, 1)
            pe.wait_ge(gated, 40)
            with pe.Fori(0, 6) as t:
                for s in range(2):
                    pe.wait_ge(w_ready, t * 2 + 4 + s + 1)
                    for b in range(2):
                        for half in range(HALVES):
                            n = 4 * s + 2 * b + half
                            pe.wait_ge(gated, t * 8 + 33 + n)
                            cols = slice(half * BANK, (half + 1) * BANK)
                            for k in range(KD):
                                last = three(nc.tensor, bank(n), w_hi[:, s, k, b * P:(b + 1) * P], w_lo[:, s, k, b * P:(b + 1) * P],
                                             g.h_hi[:, k, cols], g.h_lo[:, k, cols], k == 0, k == KD - 1)
                            last.then_inc(proj, 1)

        @block.scalar
        def _(act):
            act.nop().then_inc(gated, 8)
            for i in range(8):
                act.nop().then_inc(stored[i], 1)
            with act.Fori(0, 4) as u:
                for i in range(NT):
                    act.wait_ge(proj, u * 8 + 8 + i + 1)
                    act.wait_ge(stored[i], u * 16 + 1)
                    nc.scalar.activation(stage[:, i, 0:UNIT], g.ps[:, i * BANK:i * BANK + UNIT], ACT.Silu).then_inc(gated, 1)
                    act.wait_ge(gated, u * 8 + 8 + i + 1)
                    act.dma_start(g.z_dram[i * P:(i + 1) * P, bass.ds(u * UNIT, UNIT)], stage[:, i, 0:UNIT]).then_inc(stored[i], 16)
            def gates(turns, function, before):
                with act.Fori(0, turns) as t:
                    for n in range(8):
                        channels, half = divmod(n, 2)
                        act.wait_ge(proj, t * 8 + 8 * before + 40 + n + 1)
                        act.wait_ge(stored[n], t * 16 + 16 * before + 64 + 1)
                        nc.scalar.activation(stage[:, n, :], bank(n), function).then_inc(gated, 1)
                        act.wait_ge(gated, t * 8 + 8 * before + 40 + n + 1)
                        act.dma_start(g.sig_dram[bass.ds(t * 4 * P + (before * 4 + channels) * P, P), half * BANK:(half + 1) * BANK],
                                      stage[:, n, :]).then_inc(stored[n], 16)

            gates(2, ACT.Silu, 0)
            gates(4, ACT.Sigmoid, 2)

        @block.vector
        def _(dve):
            dve.nop().then_inc(rep_ok, 2)
            for n, pair in enumerate(((7, 2), (6, 3), (5, 4))):
                tiles = [g.score[:, g.first[i]:g.first[i + 1]] for i in pair]
                with dve.Fori(0, TOPK // 8) as r:
                    for e, s in enumerate(tiles):
                        dve.wait_ge(rep_ok, r * 2 + 64 * n + e + 1).then_inc(alone, 1)
                        nc.vector.max(best[:, e], s).then_inc(top_ok, 1)
                    for e, s in enumerate(tiles):
                        dve.wait_ge(top_ok, r * 2 + 64 * n + 1 + e).then_inc(alone, 1)
                        nc.vector.match_replace(s, best[:, e], s, TAKEN).then_inc(rep_ok, 1)
                dve.wait_ge(rep_ok, 64 * (n + 1) + 2)
            for i in range(NT):
                s = g.score[:, g.first[i]:g.first[i + 1]]
                m = g.mask[:, g.first[i]:g.first[i + 1]]
                if (i + 1) * P <= TOPK:
                    nc.vector.tensor_scalar(m, s, BELOW * 0.9, CLOSED, ALU.is_le, ALU.mult).then_inc(masked, 1)
                else:
                    nc.vector.tensor_scalar(m, s, TAKEN, CLOSED, ALU.not_equal, ALU.mult).then_inc(masked, 1)


def phase_decay(nc, g):
    with ExitStack() as ctx:
        sb = lambda n, s, d=F32: ctx.enter_context(nc.sbuf_tensor("d_" + n, s, d))
        sem = lambda n: nc.alloc_semaphore("d_" + n)
        dt, al = sb("dt", [P, H]), sb("al", [P, H])
        y, neg, e, big = sb("y", [P, NT, H]), sb("neg", [P, NT, H]), sb("e", [P, NT, H]), sb("big", [P, NT, H])
        conv_rows = sb("conv_rows", [96, P])
        load, v, a, m = sem("load"), sem("v"), sem("a"), sem("m")
        everywhere = [P, NT, H]
        block = ctx.enter_context(nc.Block())

        @block.sync
        def _(sp):
            sp.dma_start(dt[:], g.dt_bias[0].partition_broadcast(P)).then_inc(load, 16)
            sp.dma_start(al[:], g.a_log[0].partition_broadcast(P)).then_inc(load, 16)
            sp.dma_start(conv_rows[:], g.conv_w[0].rearrange("j (b p) -> (j b) p", p=P)).then_inc(load, 16)

        @block.vector
        def _(dve):
            dve.wait_ge(load, 48)
            nc.vector.tensor_tensor(y[:], g.small[:, :, 8:16], dt[:].unsqueeze(1).broadcast_to(everywhere), ALU.add).then_inc(v, 1)
            dve.wait_ge(v, 1)
            nc.vector.tensor_scalar(neg[:], y[:], 0.0, None, ALU.max).then_inc(v, 1)
            dve.wait_ge(a, 3)
            dve.wait_ge(v, 2)
            nc.vector.tensor_tensor(y[:], neg[:], e[:], ALU.add).then_inc(v, 1)
            dve.wait_ge(v, 3)
            nc.vector.scalar_tensor_tensor(out=g.g[:], in0=y[:], scalar=-1.0, in1=al[:].unsqueeze(1).broadcast_to(everywhere),
                                           op0=ALU.mult, op1=ALU.mult).then_inc(v, 1)
            dve.wait_ge(a, 5)
            nc.vector.tensor_scalar(g.nbeta[:], g.beta[:], -1.0, None, ALU.mult)
            dve.wait_ge(m, 2)
            nc.vector.tensor_copy(g.taps[:], g.ps[:, BANK:BANK + 96])
            nc.vector.memset(g.eps[:], EPS)

        @block.scalar
        def _(act):
            act.wait_ge(v, 1)
            nc.scalar.activation(big[:], y[:], ACT.Abs).then_inc(a, 1)
            act.wait_ge(a, 1)
            nc.scalar.activation(e[:], big[:], ACT.Exp, scale=-1.0).then_inc(a, 1)
            nc.scalar.activation(al[:], al[:], ACT.Exp)
            act.wait_ge(a, 2)
            nc.scalar.activation(e[:], e[:], ACT.Ln, bias=1.0).then_inc(a, 1)
            nc.scalar.activation(g.beta[:], g.small[:, :, 16:24], ACT.Sigmoid).then_inc(a, 2)
            act.wait_ge(m, 1)
            sums = g.ps[:, 0:4 * NT * H].rearrange("p (n i h) -> p n i h", n=4, h=H)
            nc.scalar.activation(g.decays[:], sums, ACT.Exp)

        @block.tensor
        def _(pe):
            pe.wait_ge(v, 4)
            for n, mask in enumerate((K_UPTO, K_AFTER, K_CH0, K_CH1)):
                last = nc.tensor.matmul(g.ps[:, n * NT * H:(n + 1) * NT * H], g.const[:, mask:mask + P],
                                        g.g[:].rearrange("p i h -> p (i h)"), start=True, stop=True)
            last.then_inc(m, 1)
            pe.wait_ge(load, 48)
            nc.tensor.transpose(g.ps[:, BANK:BANK + 96], conv_rows[:], g.const[0:96, K_ID:K_ID + 96]).then_inc(m, 1)


GROUP = 4
LEVELS = 6


def phase_delta(nc, g):
    with ExitStack() as ctx:
        sb = lambda n, s, d=F32: ctx.enter_context(nc.sbuf_tensor("e_" + n, s, d))
        sem = lambda n: nc.alloc_semaphore("e_" + n)
        PAD = 4
        w32, w_hi, w_lo = sb("w32", [P, 3, KD, P]), sb("w_hi", [P, 3, KD, P], F16), sb("w_lo", [P, 3, KD, P], BF16)
        raw = sb("raw", [P, 2, PAD + T])
        y = sb("y", [P, 3, T])
        v_tok = sb("v_tok", [P, NT, P])
        k_dec = sb("k_dec", [P, NT, P])
        b1, b2 = sb("b1", [P, NT, P]), sb("b2", [P, NT, P])
        x = sb("x", [P, NT, P])
        gam = sb("gam", [P, NT, P])
        a_t = sb("a_t", [P, NT, P])
        m_t = sb("m_t", [P, 2, NT, P])
        g_col = sb("g_col", [P, NT])
        ones = sb("ones", [P, P])
        u_st, w_st, qg_st = sb("u_st", [P, GROUP, NT, P]), sb("w_st", [P, GROUP, T]), sb("qg_st", [P, GROUP, T])
        kd_st, at_st = sb("kd_st", [P, GROUP, NT, P]), sb("at_st", [P, GROUP, NT, P])
        s_st, v_new = sb("s_st", [P, GROUP, P]), sb("v_new", [P, GROUP, P])
        o_st = sb("o_st", [P, GROUP * P])
        each = dict(w_cast=3, w_ready=3, proj=6, raw_ok=6, conv=12, silu=3, sq=2, ssq=2, ln_ok=2, root=2, norm=2, gcol=1, glhs=1,
                    glhs_mm=1, gexp=1, gmask=1, beta_ok=1, decb=1, dexp=1, qg_ok=1, kk=1, qk=1, at=1, attn_ok=1, ktok=1, vtok=1,
                    ktok_r=1, vtok_r=1, mt=LEVELS, u0=1, m1=1, t_ok=10, u_ok=10, xm=10, x_ok=10, tx=10, uw=1, us_ok=1, ws_ok=1)
        s = {n: sem(n) for n in [*each, "alone", "pad", "wS", "qS", "o_mm", "kdv", "vn", "s_ok", "o_ok", "zero"]}

        def at(name, h, k):
            return s[name], h * each[name] + k + 1

        def start(engine, names):
            for n in names.split():
                engine.nop().then_inc(s[n], 1)

        w_in = [sem(f"w_in{n}") for n in range(3)]
        o_out = sem("o_out")
        bank = lambda k: g.ps[:, k * BANK:(k + 1) * BANK]
        pair = lambda k: g.ps[:, k * BANK:(k + 2) * BANK].rearrange("p (i n) -> p i n", n=P)
        tile_of = lambda k, i: g.ps[:, k * BANK + i * P:k * BANK + (i + 1) * P]
        win = g.w_in[0].rearrange("(k p) n -> p k n", p=P)
        upto = g.const[:, K_UPTO:K_UPTO + P]
        after = g.const[:, K_AFTER:K_AFTER + P]
        ident = g.const[:, K_ID:K_ID + P]
        full = [P, NT, P]
        over = lambda m: m.unsqueeze(1).broadcast_to(full)
        level = lambda l: over(g.const[:, K_LEVEL + l * P:K_LEVEL + (l + 1) * P])
        per = lambda t, h: t[:, :, bass.ds(h, 1)].broadcast_to(full)
        CHUNKS = T // CHUNK
        block = ctx.enter_context(nc.Block())

        @block.sync
        def _(sp):
            for h in range(H):
                for n in range(3):
                    if h:
                        sp.wait_ge(*at("w_ready", h - 1, n + 1))
                    c0 = (C_Q, C_K, C_V)[n] + h * P
                    sp.dma_start(w32[:, n], win[:, :, c0:c0 + P]).then_inc(w_in[n], 16)
            sp.wait_ge(o_out, 16 * NT * (H // GROUP))

        @block.gpsimd
        def _(pool):
            start(pool, "w_cast w_ready gcol glhs gmask beta_ok mt")

            def split(h, n):
                pool.wait_ge(w_in[n], h * 16 + 16).then_inc(s["alone"], 1)
                pool.wait_ge(*at("proj", h, 2 * n + 2 - each["proj"])).then_inc(s["alone"], 1)
                nc.gpsimd.tensor_copy(w_hi[:, n], w32[:, n]).then_inc(s["w_cast"], 1)
                pool.wait_ge(*at("w_cast", h, n + 1))
                nc.gpsimd.tensor_tensor(w_lo[:, n], w32[:, n], w_hi[:, n], ALU.subtract).then_inc(s["w_ready"], 1)

            def decays(h):
                pool.wait_ge(*at("decb", h, 0)).then_inc(s["alone"], 1)
                nc.gpsimd.tensor_copy(g_col[:], g.g[:, :, bass.ds(h, 1)].rearrange("p i o -> p (i o)")).then_inc(s["gcol"], 1)
                pool.wait_ge(*at("gcol", h, 1))
                pool.wait_ge(*at("xm", h, 8 - each["xm"]))
                nc.gpsimd.tensor_tensor(m_t[:, 0], over(after), g_col[:].unsqueeze(2).broadcast_to(full), ALU.mult).then_inc(s["glhs"], 1)
                pool.wait_ge(*at("gexp", h, 1))
                nc.gpsimd.tensor_tensor(gam[:], gam[:], over(upto), ALU.mult).then_inc(s["gmask"], 1)
                pool.wait_ge(*at("gmask", h, 1))
                pool.wait_ge(*at("mt", h, 0))
                nc.gpsimd.tensor_tensor(a_t[:], gam[:], per(g.beta, h), ALU.mult).then_inc(s["beta_ok"], 1)

            def head(h, front, more):
                for l in range(LEVELS):
                    if l == 0:
                        pool.wait_ge(*at("at", h, 1))
                        pool.wait_ge(*at("glhs_mm", h, 1))
                    elif l == 1:
                        pool.wait_ge(*at("qg_ok", h, 1))
                    elif l == 2:
                        pool.wait_ge(*at("u0", h, 1))
                        pool.wait_ge(*at("m1", h, 1))
                    else:
                        pool.wait_ge(*at("xm", h, 2 * (l - 2)))
                    nc.gpsimd.tensor_tensor(m_t[:, l % 2], a_t[:], level(l), ALU.mult).then_inc(s["mt"], 1)
                    if more and l >= 3:
                        split(h + 2, l - 3)
                if front:
                    decays(h + 1)

            for n in range(3):
                pool.wait_ge(w_in[n], 16)
                nc.gpsimd.tensor_copy(w_hi[:, n], w32[:, n]).then_inc(s["w_cast"], 1)
                pool.wait_ge(*at("w_cast", 0, n + 1))
                nc.gpsimd.tensor_tensor(w_lo[:, n], w32[:, n], w_hi[:, n], ALU.subtract).then_inc(s["w_ready"], 1)
            nc.gpsimd.tensor_copy(g_col[:], g.g[:, :, 0]).then_inc(s["gcol"], 1)
            pool.wait_ge(*at("gcol", 0, 1))
            nc.gpsimd.tensor_tensor(m_t[:, 0], over(after), g_col[:].unsqueeze(2).broadcast_to(full), ALU.mult).then_inc(s["glhs"], 1)
            for n in range(3):
                split(1, n)
            pool.wait_ge(*at("gexp", 0, 1))
            nc.gpsimd.tensor_tensor(gam[:], gam[:], over(upto), ALU.mult).then_inc(s["gmask"], 1)
            pool.wait_ge(*at("gmask", 0, 1))
            nc.gpsimd.tensor_tensor(a_t[:], gam[:], g.beta[:, :, 0:1].broadcast_to(full), ALU.mult).then_inc(s["beta_ok"], 1)
            with pool.Fori(0, H - 2) as h:
                head(h, True, True)
            head(H - 2, True, False)
            head(H - 1, False, False)

        @block.scalar
        def _(act):
            start(act, "raw_ok silu sq ln_ok root gexp dexp vtok_r x_ok ws_ok")
            squares = lambda n: (gam[:].rearrange("p i n -> p (i n)"), raw[:, 1, PAD:])[n]

            def project(h, n):
                for half in range(HALVES):
                    act.wait_ge(*at("proj", h, 2 * n + half + 1))
                    if half == 0:
                        act.wait_ge(*(at("conv", h, 0), at("norm", h, 0), at("conv", h, 4))[n])
                        act.wait_ge(s["pad"], 1)
                    nc.scalar.copy(raw[:, n % 2, PAD + half * BANK:PAD + (half + 1) * BANK], bank(half)).then_inc(s["raw_ok"], 1)

            def silu(h, n):
                act.wait_ge(*at("conv", h, 4 * n + 4))
                nc.scalar.activation(y[:, n], y[:, n], ACT.Silu).then_inc(s["silu"], 1)
                if n < 2:
                    act.wait_ge(*at("silu", h, n + 1))
                    act.wait_ge(*(at("attn_ok", h, 0), at("conv", h, 8))[n])
                    nc.scalar.activation(squares(n), y[:, n], ACT.Square).then_inc(s["sq"], 1)

            def root(h, n):
                act.wait_ge(*at("ssq", h, n + 1))
                nc.scalar.activation(squares(n), pair(0).rearrange("p i n -> p (i n)"), ACT.Ln, bias=g.eps[:]).then_inc(s["ln_ok"], 1)
                act.wait_ge(*at("ln_ok", h, n + 1))
                nc.scalar.activation(squares(n), squares(n), ACT.Exp, scale=-0.5).then_inc(s["root"], 1)

            def gamma(h):
                act.wait_ge(*at("glhs_mm", h, 1))
                act.wait_ge(*at("norm", h, 1))
                nc.scalar.activation(gam[:], pair(4), ACT.Exp).then_inc(s["gexp"], 1)

            def head(h, hh, front):
                act.wait_ge(*at("decb", h, 1))
                act.wait_ge(*at("xm", h, 0))
                nc.scalar.activation(m_t[:, 1], pair(6), ACT.Exp).then_inc(s["dexp"], 1)
                act.wait_ge(*at("vtok", h, 1))
                act.wait_ge(*at("uw", h, 0))
                nc.scalar.copy(v_tok[:], pair(0)).then_inc(s["vtok_r"], 1)
                for l in range(1, LEVELS):
                    for half in range(2):
                        act.wait_ge(*at("xm", h, 2 * l - 1 + half))
                        if l > 1:
                            act.wait_ge(*at("tx", h, 2 * (l - 1) - 1 + half))
                        else:
                            act.wait_ge(*at("uw", h, 0))
                        nc.scalar.copy(x[:, 4 * half:4 * half + 4], bank(2 + half).rearrange("p (i n) -> p i n", n=P)).then_inc(s["x_ok"], 1)
                    if front:
                        if 2 <= l < 5:
                            silu(h + 1, l - 2)
                        if l < 4:
                            project(h + 1, l - 1)
                        elif l == 4:
                            root(h + 1, 0)
                            root(h + 1, 1)
                        else:
                            gamma(h + 1)
                act.wait_ge(*at("uw", h, 1))
                nc.scalar.copy(w_st[:, bass.ds(hh, 1), :], pair(2).rearrange("p i n -> p (i n)").unsqueeze(1)).then_inc(s["ws_ok"], 1)

            def first():
                for n in range(3):
                    project(0, n)
                    if n:
                        silu(0, n - 1)
                silu(0, 2)
                root(0, 0)
                root(0, 1)
                gamma(0)

            def outputs(group):
                for n in range(CHUNKS):
                    rows = slice((n % 2) * CHUNK, (n % 2 + 1) * CHUNK)
                    act.wait_ge(s["o_mm"], group * CHUNKS + n + 1)
                    i = n // 2
                    if n % 2 == 0 and (group or i):
                        act.wait_ge(o_out, 16 * (group * NT + i))
                    nc.scalar.copy(o_st[rows], g.ps[rows, 2 * BANK:3 * BANK]).then_inc(s["o_ok"], 1)
                    if n % 2:
                        act.wait_ge(s["o_ok"], group * CHUNKS + n + 1)
                        act.dma_start(g.o_dram[i * P:(i + 1) * P, group * GROUP * P:(group + 1) * GROUP * P], o_st[:]).then_inc(o_out, 16)

            first()
            with act.Fori(0, GROUP) as h:
                head(h, h, True)
            outputs(0)
            with act.Fori(0, GROUP - 1) as hh:
                head(hh + GROUP, hh, True)
            head(H - 1, GROUP - 1, False)
            outputs(1)

        @block.vector
        def _(dve):
            nc.vector.memset(raw[:, :, 0:PAD], 0.0).then_inc(s["pad"], 1)
            nc.vector.memset(ones[:], 1.0).then_inc(s["pad"], 1)

            start(dve, "conv norm at qg_ok ktok_r u0 attn_ok t_ok u_ok us_ok")

            def convolve(h, n):
                for j in range(4):
                    tap = g.taps[:, bass.ds(h + 24 * j + 8 * n, 1)]
                    shifted = raw[:, n % 2, PAD - 3 + j:PAD - 3 + j + T]
                    if j == 0:
                        dve.wait_ge(*at("raw_ok", h, 2 * n + 2))
                        dve.wait_ge(*(at("qk", h, 0), at("qk", h, 0), at("vtok", h, 0))[n])
                        dve.wait_ge(*at("qg_ok", h, 0))
                        nc.vector.tensor_scalar(y[:, n], shifted, tap, None, ALU.mult).then_inc(s["conv"], 1)
                    else:
                        dve.wait_ge(*at("conv", h, 4 * n + j))
                        nc.vector.scalar_tensor_tensor(out=y[:, n], in0=shifted, scalar=tap, in1=y[:, n],
                                                       op0=ALU.mult, op1=ALU.add).then_inc(s["conv"], 1)

            def normalize(h, n):
                dve.wait_ge(*at("root", h, n + 1))
                nc.vector.scalar_tensor_tensor(out=y[:, n], in0=y[:, n], scalar=P ** -0.5 if n == 0 else 1.0,
                                               in1=(gam[:].rearrange("p i n -> p (i n)"), raw[:, 1, PAD:])[n],
                                               op0=ALU.mult, op1=ALU.mult).then_inc(s["norm"], 1)

            def head(h, hh, front):
                dve.wait_ge(*at("kk", h, 1))
                dve.wait_ge(*at("beta_ok", h, 1))
                nc.vector.tensor_tensor(a_t[:], pair(4), a_t[:], ALU.mult).then_inc(s["at"], 1)
                dve.wait_ge(*at("dexp", h, 1))
                nc.vector.tensor_tensor(qg_st[:, bass.ds(hh, 1)].rearrange("p o n -> p (o n)"), y[:, 0], m_t[:, 1].rearrange("p i n -> p (i n)"), ALU.mult).then_inc(s["qg_ok"], 1)
                dve.wait_ge(*at("mt", h, 1))
                dve.wait_ge(*at("uw", h, 0))
                nc.vector.tensor_tensor(b2[:], over(ident), m_t[:, 0], ALU.subtract).then_inc(s["u0"], 1)
                dve.wait_ge(*at("ktok", h, 1))
                nc.vector.tensor_tensor(k_dec[:], pair(2), per(g.decays[:, 0], h), ALU.mult)
                nc.vector.tensor_tensor(kd_st[:, bass.ds(hh, 1)].rearrange("p o i n -> p (o i) n"), pair(2), per(g.decays[:, 1], h), ALU.mult).then_inc(s["ktok_r"], 1)
                dve.wait_ge(*at("m1", h, 1))
                nc.vector.tensor_tensor(b1[:], over(ident), pair(0), ALU.subtract).then_inc(s["t_ok"], 2)
                dve.wait_ge(*at("qk", h, 1))
                nc.vector.tensor_tensor(at_st[:, bass.ds(hh, 1)].rearrange("p o i n -> p (o i) n"), pair(4), gam[:], ALU.mult).then_inc(s["attn_ok"], 1)
                for l in range(1, LEVELS):
                    for half in range(2):
                        t4 = slice(4 * half, 4 * half + 4)
                        part = lambda b, second: b[:, t4].rearrange("p i (c two w) -> p (i c) two w", two=2, w=1 << l)[:, :, second]
                        delta = lambda k: g.ps[:, k * BANK:k * BANK + BANK // 2].rearrange("p (c w) -> p c w", w=1 << l)
                        dve.wait_ge(*at("tx", h, 2 * l - 1 + half))
                        if l < LEVELS - 1:
                            dve.wait_ge(*at("t_ok", h, 2 * l if l == 1 else 2 * l - 1 + half))
                            nc.vector.tensor_tensor(part(b1, 0), part(b1, 0), delta(4 + half), ALU.subtract).then_inc(s["t_ok"], 1)
                        if l == 1:
                            dve.wait_ge(*at("u0", h, 1))
                        else:
                            dve.wait_ge(*at("u_ok", h, 2 * (l - 1) - 1 + half))
                        nc.vector.tensor_tensor(part(b2, 1), part(b2, 1), delta(6 + half), ALU.subtract).then_inc(s["u_ok"], 1)
                    if front:
                        if l < 4:
                            convolve(h + 1, l - 1)
                        elif l == 4:
                            normalize(h + 1, 0)
                            normalize(h + 1, 1)
                dve.wait_ge(*at("uw", h, 1))
                nc.vector.tensor_tensor(u_st[:, bass.ds(hh, 1)].rearrange("p o i n -> p (o i) n"), pair(0), per(g.beta, h), ALU.mult).then_inc(s["us_ok"], 1)

            def chunks(group):
                nc.vector.memset(s_st[:], 0.0).then_inc(s["zero"], 1)
                for n in range(CHUNKS):
                    i, c = divmod(n, 2)
                    rows = slice(c * CHUNK, (c + 1) * CHUNK)
                    done = (group * CHUNKS + n) * GROUP
                    for two in range(GROUP // 2):
                        dve.wait_ge(s["wS"], done // 2 + two + 1)
                        if done:
                            dve.wait_ge(s["kdv"], done // 2 - 1 + two)
                        for hh in (2 * two, 2 * two + 1):
                            h = group * GROUP + hh
                            nc.vector.scalar_tensor_tensor(
                                out=v_new[rows, hh], in0=g.ps[rows, two * BANK + hh * P:two * BANK + (hh + 1) * P],
                                scalar=g.nbeta[rows, i, h:h + 1], in1=u_st[rows, hh, i], op0=ALU.mult, op1=ALU.add).then_inc(s["vn"], 1)
                    for two in range(GROUP // 2):
                        dve.wait_ge(s["kdv"], done // 2 + two + 1)
                        if n:
                            dve.wait_ge(s["s_ok"], done - GROUP + 2 * two + 2)
                        else:
                            dve.wait_ge(s["zero"], group + 1)
                        for hh in (2 * two, 2 * two + 1):
                            h = group * GROUP + hh
                            nc.vector.scalar_tensor_tensor(
                                out=s_st[:, hh], in0=s_st[:, hh], scalar=g.decays[:, 2 + c, i, h:h + 1],
                                in1=tile_of(4 + two, hh), op0=ALU.mult, op1=ALU.add).then_inc(s["s_ok"], 1)

            for n in range(3):
                convolve(0, n)
            normalize(0, 0)
            normalize(0, 1)
            with dve.Fori(0, GROUP) as h:
                head(h, h, True)
            chunks(0)
            with dve.Fori(0, GROUP - 1) as hh:
                head(hh + GROUP, hh, True)
            head(H - 1, GROUP - 1, False)
            chunks(1)

        @block.tensor
        def _(pe):
            start(pe, "proj ssq glhs_mm decb kk qk ktok vtok m1 xm tx uw")
            mm = nc.tensor.matmul

            def project(h, n, half):
                if half == 0:
                    pe.wait_ge(*at("w_ready", h, n + 1))
                    if n == 0 and not (isinstance(h, int) and h == 0):
                        pe.wait_ge(*at("t_ok", h, 2 - each["t_ok"]))
                if n:
                    pe.wait_ge(*at("raw_ok", h, 2 * n + half - 1))
                cols = slice(half * BANK, (half + 1) * BANK)
                for k in range(KD):
                    last = three(nc.tensor, bank(half), w_hi[:, n, k], w_lo[:, n, k],
                                 g.h_hi[:, k, cols], g.h_lo[:, k, cols], k == 0, k == KD - 1)
                last.then_inc(s["proj"], 1)

            def sums(h, n):
                pe.wait_ge(*at("sq", h, n + 1))
                pe.wait_ge(*(at("raw_ok", h, 6), at("ln_ok", h, 1))[n])
                pe.wait_ge(s["pad"], 2)
                for half in range(HALVES):
                    src = (gam[:, 4 * half:4 * half + 4], raw[:, 1, PAD + half * BANK:PAD + (half + 1) * BANK])[n]
                    last = mm(bank(half), ones[:], src, start=True, stop=True)
                last.then_inc(s["ssq"], 1)

            def decays(h):
                pe.wait_ge(*at("glhs", h, 1))
                for i in range(NT):
                    last = mm(tile_of(4, i), m_t[:, 0, i], upto, start=True, stop=True)
                last.then_inc(s["glhs_mm"], 1)

            def between(h, slot):
                if slot < 6:
                    project(h, slot // 2, slot % 2)
                elif slot < 8:
                    sums(h, slot - 6)
                elif slot == 8:
                    pe.wait_ge(*at("t_ok", h, 0))
                    decays(h)

            def head(h, front):
                pe.wait_ge(*at("gcol", h, 1))
                pe.wait_ge(*at("u_ok", h, 0))
                for i in range(NT):
                    last = mm(tile_of(6, i), g_col[:, i:i + 1].broadcast_to([P, P]), upto, start=True, stop=True)
                last.then_inc(s["decb"], 1)
                pe.wait_ge(*at("norm", h, 2))
                pe.wait_ge(*at("gexp", h, 1))
                for i in range(NT):
                    tok = slice(i * P, (i + 1) * P)
                    last = mm(tile_of(4, i), y[:, 1, tok], y[:, 1, tok], start=True, stop=True)
                last.then_inc(s["kk"], 1)
                pe.wait_ge(*at("ws_ok", h, 0))
                for i in range(NT):
                    last = nc.tensor.transpose(tile_of(2, i), y[:, 1, i * P:(i + 1) * P], ident)
                last.then_inc(s["ktok"], 1)
                pe.wait_ge(*at("silu", h, 3))
                pe.wait_ge(*at("ln_ok", h, 2))
                pe.wait_ge(*at("us_ok", h, 0))
                for i in range(NT):
                    last = nc.tensor.transpose(tile_of(0, i), y[:, 2, i * P:(i + 1) * P], ident)
                last.then_inc(s["vtok"], 1)
                pe.wait_ge(*at("at", h, 1))
                for i in range(NT):
                    tok = slice(i * P, (i + 1) * P)
                    last = mm(tile_of(4, i), y[:, 1, tok], y[:, 0, tok], start=True, stop=True)
                last.then_inc(s["qk"], 1)
                pe.wait_ge(*at("mt", h, 1))
                pe.wait_ge(*at("vtok_r", h, 1))
                for i in range(NT):
                    last = nc.tensor.transpose(tile_of(0, i), m_t[:, 0, i], ident)
                last.then_inc(s["m1"], 1)
                for l in range(1, LEVELS):
                    pe.wait_ge(*at("mt", h, l + 1))
                    part = lambda b, i, second: b[:, i].rearrange("p (c two w) -> p c two w", two=2, w=1 << l)[:, :, second]
                    short = lambda k, i: g.ps[:, (k + i // 4) * BANK + i % 4 * CHUNK:(k + i // 4) * BANK + (i % 4 + 1) * CHUNK]
                    for half in range(2):
                        if l == 1:
                            pe.wait_ge(*at("t_ok", h, 2))
                            pe.wait_ge(*at("ktok_r", h, 1))
                        else:
                            pe.wait_ge(*at("t_ok", h, 2 * l - 1 + half))
                            pe.wait_ge(*at("x_ok", h, 2 * (l - 1) - 1 + half))
                        for i in range(4 * half, 4 * half + 4):
                            last = mm(tile_of(2, i), m_t[:, l % 2, i], b1[:, i], start=True, stop=True)
                        last.then_inc(s["xm"], 1)
                    if front:
                        between(h + 1, 2 * l - 2)
                    for half in range(2):
                        tiles = range(4 * half, 4 * half + 4)
                        pe.wait_ge(*at("x_ok", h, 2 * l - 1 + half))
                        if l == 1:
                            pe.wait_ge(*at("u0", h, 1))
                            pe.wait_ge(*at("attn_ok", h, 1))
                            pe.wait_ge(*at("dexp", h, 1))
                        else:
                            pe.wait_ge(*at("u_ok", h, 2 * (l - 1) - 1 + half))
                        if l < LEVELS - 1:
                            for i in tiles:
                                mm(short(4, i), b2[:, i], part(x, i, 0), start=True, stop=True)
                        for i in tiles:
                            last = mm(short(6, i), x[:, i], part(b2, i, 1), start=True, stop=True)
                        last.then_inc(s["tx"], 1)
                    if front:
                        between(h + 1, 2 * l - 1)
                pe.wait_ge(*at("u_ok", h, 10))
                if front:
                    pe.wait_ge(*at("ln_ok", h + 1, 2))
                for i in range(NT):
                    mm(tile_of(0, i), b2[:, i], v_tok[:, i], start=True, stop=True)
                for i in range(NT):
                    last = mm(tile_of(2, i), k_dec[:, i], b2[:, i], start=True, stop=True)
                last.then_inc(s["uw"], 1)

            def chunks(group):
                pe.wait_ge(*at("us_ok", GROUP * (group + 1), 0))
                pe.wait_ge(*at("ws_ok", GROUP * (group + 1), 0))
                if group + 1 < H // GROUP:
                    pe.wait_ge(*at("gexp", GROUP * (group + 1), 1))
                pe.wait_ge(s["zero"], group + 1)
                for n in range(CHUNKS):
                    i, c = divmod(n, 2)
                    rows = slice(c * CHUNK, (c + 1) * CHUNK)
                    tok = slice(n * CHUNK, (n + 1) * CHUNK)
                    done = (group * CHUNKS + n) * GROUP
                    if n >= 2 or group:
                        pe.wait_ge(s["o_ok"], group * CHUNKS + n - 1)
                    outs = g.ps[rows, 2 * BANK:3 * BANK]
                    for two in range(GROUP // 2):
                        both = (2 * two, 2 * two + 1)
                        for hh in both:
                            if n:
                                pe.wait_ge(s["s_ok"], done - GROUP + hh + 1)
                            last = mm(g.ps[rows, two * BANK + hh * P:two * BANK + (hh + 1) * P], w_st[:, hh, tok], s_st[:, hh],
                                      start=True, stop=True)
                        last.then_inc(s["wS"], 1)
                        for hh in both:
                            mm(outs[:, hh * P:(hh + 1) * P], qg_st[:, hh, tok], s_st[:, hh],
                               start=(hh == 0), stop=False, skip_group_check=True)
                    for two in range(GROUP // 2):
                        for hh in (2 * two, 2 * two + 1):
                            pe.wait_ge(s["vn"], done + hh + 1)
                            last = mm(outs[:, hh * P:(hh + 1) * P], at_st[rows, hh, i, rows], v_new[rows, hh],
                                      start=False, stop=True, skip_group_check=True)
                            if hh == GROUP - 1:
                                last.then_inc(s["o_mm"], 1)
                            last = mm(tile_of(4 + two, hh), kd_st[rows, hh, i], v_new[rows, hh], start=True, stop=True)
                        last.then_inc(s["kdv"], 1)
                pe.wait_ge(s["o_ok"], CHUNKS * (group + 1))
                pe.wait_ge(s["s_ok"], CHUNKS * GROUP * (group + 1))

            for slot in range(8):
                between(0, slot)
            decays(0)
            with pe.Fori(0, GROUP) as h:
                head(h, True)
            chunks(0)
            with pe.Fori(0, GROUP - 1) as hh:
                head(hh + GROUP, True)
            head(H - 1, False)
            chunks(1)


SHRINK = 1.0 / 16


def project_blocks(nc, pe, g, w_hi, w_lo, x_hi, x_lo, w_ready, proj, free):
    with pe.Fori(0, 2) as t:
        for s in range(2):
            pe.wait_ge(w_ready, t * 2 + s + 1)
            for b in range(2):
                for half in range(HALVES):
                    n = 4 * s + 2 * b + half
                    pe.wait_ge(free, t * 8 + n + 1)
                    cols = slice(half * BANK, (half + 1) * BANK)
                    for k in range(KD):
                        last = three(nc.tensor, g.ps[:, n * BANK:(n + 1) * BANK],
                                     w_hi[:, s, k, b * P:(b + 1) * P], w_lo[:, s, k, b * P:(b + 1) * P],
                                     x_hi[:, k, cols], x_lo[:, k, cols], k == 0, k == KD - 1)
                    last.then_inc(proj, 1)


def split_block(nc, pool, w32, w_hi, w_lo, s, cast, n):
    nc.gpsimd.tensor_copy(w_hi[:, s], w32[:, s]).then_inc(cast, 1)
    pool.wait_ge(cast, n + 1)
    return nc.gpsimd.tensor_tensor(w_lo[:, s], w32[:, s], w_hi[:, s], ALU.subtract)


def phase_delta_out(nc, g):
    with ExitStack() as ctx:
        sb = lambda n, s, d=F32: ctx.enter_context(nc.sbuf_tensor("f_" + n, s, d))
        sem = lambda n: nc.alloc_semaphore("f_" + n)
        w32, w_hi, w_lo = sb("w32", [P, 2, KD, UNIT]), sb("w_hi", [P, 2, KD, UNIT], F16), sb("w_lo", [P, 2, KD, UNIT], BF16)
        o, z = sb("o", [P, NT, D]), sb("z", [P, 2, D])
        sq = sb("sq", [P, 2, D])
        gn = sb("gn", [P, P])
        ss, rstd = sb("ss", [P, NT, H]), sb("rstd", [P, NT, H])
        a_hi, a_lo = sb("a_hi", [P, H, T], F16), sb("a_lo", [P, H, T], F16)
        ga, m1 = sb("ga", [P, 4, BANK]), sb("m1", [P, 4, BANK])
        w_in, w_cast, w_ready = [sem("w_in0"), sem("w_in1")], sem("w_cast"), sem("w_ready")
        o_in, z_in, gn_in = [sem(f"o_in{i}") for i in range(NT)], [sem(f"z_in{i}") for i in range(2)], sem("gn_in")
        sq_ok, ss_ok, mean, root, inv = sem("sq_ok"), sem("ss_ok"), sem("mean"), sem("root"), sem("inv")
        normed, zg, gated, turned, hi_ok, lo_ok = sem("normed"), sem("zg"), sem("gated"), sem("turned"), sem("hi_ok"), sem("lo_ok")
        proj, free = sem("proj"), sem("free")
        ga_in, m_out = [sem(f"ga_in{i}") for i in range(4)], [sem(f"m_out{i}") for i in range(4)]
        wo = g.w_o_gdn[0].rearrange("(k p) n -> p k n", p=P)
        block = ctx.enter_context(nc.Block())

        def low(dve, i):
            dve.wait_ge(hi_ok, i + 1)
            cols = slice(i * P, (i + 1) * P)
            nc.vector.scalar_tensor_tensor(out=a_lo[:, :, cols], in0=g.ps[:, (i % 2) * T:(i % 2 + 1) * T].rearrange("p (h t) -> p h t", t=P),
                                           scalar=SHRINK, in1=a_hi[:, :, cols], op0=ALU.mult, op1=ALU.subtract).then_inc(lo_ok, 1)

        def product(n):
            return g.m_dram[(n // 2) * P:(n // 2 + 1) * P, (n % 2) * BANK:(n % 2 + 1) * BANK]

        @block.sync
        def _(sp):
            sp.dma_start(gn[:], g.gdn_norm_g[0].partition_broadcast(P)).then_inc(gn_in, 16)
            for i in range(NT):
                sp.dma_start(o[:, i], g.o_dram[i * P:(i + 1) * P, :]).then_inc(o_in[i], 16)
            for u in range(2):
                sp.dma_start(w32[:, u], wo[:, :, u * UNIT:(u + 1) * UNIT]).then_inc(w_in[u], 16)
            for i in range(NT):
                if i >= 2:
                    sp.wait_ge(gated, i - 1)
                sp.dma_start(z[:, i % 2], g.z_dram[i * P:(i + 1) * P, :]).then_inc(z_in[i % 2], 16)
            for n in range(16):
                if n in (0, 4):
                    u = 2 + n // 4
                    sp.wait_ge(w_ready, u - 1)
                    sp.dma_start(w32[:, u % 2], wo[:, :, u * UNIT:(u + 1) * UNIT]).then_inc(w_in[u % 2], 16)
                if n >= 4:
                    sp.wait_ge(free, 8 + n - 3)
                    sp.dma_start(product(n - 4), m1[:, n % 4]).then_inc(m_out[n % 4], 16)
                sp.dma_start(ga[:, n % 4], g.sig_dram[D + (n // 2) * P:D + (n // 2 + 1) * P, (n % 2) * BANK:(n % 2 + 1) * BANK]).then_inc(ga_in[n % 4], 16)
            for n in range(12, 16):
                sp.wait_ge(free, 8 + n + 1)
                sp.dma_start(product(n), m1[:, n % 4]).then_inc(m_out[n % 4], 16)
            for n in range(4):
                sp.wait_ge(m_out[n], 16 * 4 + 1)

        @block.gpsimd
        def _(pool):
            pool.wait_ge(gn_in, 16)
            for u in range(2):
                pool.wait_ge(w_in[u], 16)
                split_block(nc, pool, w32, w_hi, w_lo, u, w_cast, u).then_inc(w_ready, 1)
            for i in range(NT):
                pool.wait_ge(z_in[i % 2], 16 * (i // 2 + 1))
                zt = z[:, i % 2].rearrange("p (h e) -> p h e", e=P)
                nc.gpsimd.tensor_tensor(zt, zt, gn[:].unsqueeze(1).broadcast_to([P, H, P]), ALU.mult).then_inc(zg, 1)
            for u in range(2, 4):
                pool.wait_ge(w_in[u % 2], 32)
                pool.wait_ge(proj, 4 * (u - 1))
                split_block(nc, pool, w32, w_hi, w_lo, u % 2, w_cast, u).then_inc(w_ready, 1)

        @block.scalar
        def _(act):
            for i in range(NT):
                act.wait_ge(o_in[i], 16)
                if i >= 2:
                    act.wait_ge(ss_ok, i - 1)
                nc.scalar.activation(sq[:, i % 2], o[:, i], ACT.Square).then_inc(sq_ok, 1)
            act.wait_ge(mean, 1)
            nc.scalar.activation(rstd[:], ss[:], ACT.Sqrt).then_inc(root, 1)
            for i in range(NT):
                act.wait_ge(turned, i + 1)
                nc.scalar.mul(a_hi[:, :, i * P:(i + 1) * P], g.ps[:, (i % 2) * T:(i % 2 + 1) * T].rearrange("p (h t) -> p h t", t=P),
                              SHRINK).then_inc(hi_ok, 1)

        @block.vector
        def _(dve):
            for i in range(NT):
                dve.wait_ge(sq_ok, i + 1)
                nc.vector.reduce_sum(ss[:, i], sq[:, i % 2].rearrange("p (h e) -> p h e", e=P), AX.X).then_inc(ss_ok, 1)
            dve.wait_ge(ss_ok, NT)
            nc.vector.tensor_scalar(ss[:], ss[:], 1.0 / P, EPS, ALU.mult, ALU.add).then_inc(mean, 1)
            dve.wait_ge(root, 1)
            nc.vector.reciprocal(rstd[:], rstd[:]).then_inc(inv, 1)
            dve.wait_ge(inv, 1)
            for i in range(NT):
                heads = o[:, i].rearrange("p (h e) -> p h e", e=P)
                nc.vector.tensor_tensor(heads, heads, rstd[:, i].unsqueeze(2).broadcast_to([P, H, P]), ALU.mult).then_inc(normed, 1)
                dve.wait_ge(normed, i + 1)
                dve.wait_ge(zg, i + 1)
                nc.vector.tensor_tensor(o[:, i], o[:, i], z[:, i % 2], ALU.mult).then_inc(gated, 1)
                if i:
                    low(dve, i - 1)
            low(dve, NT - 1)
            dve.nop().then_inc(free, 8)
            for n in range(4):
                dve.nop().then_inc(m_out[n], 1)
            with dve.Fori(0, 2) as t:
                for n in range(8):
                    dve.wait_ge(proj, t * 8 + n + 1)
                    dve.wait_ge(ga_in[n % 4], t * 32 + 16 * (n // 4 + 1))
                    dve.wait_ge(m_out[n % 4], t * 32 + 16 * (n // 4) + 1)
                    nc.vector.scalar_tensor_tensor(out=m1[:, n % 4], in0=g.ps[:, n * BANK:(n + 1) * BANK], scalar=1.0 / SHRINK,
                                                   in1=ga[:, n % 4], op0=ALU.mult, op1=ALU.mult).then_inc(free, 1)

        @block.tensor
        def _(pe):
            for i in range(NT):
                pe.wait_ge(gated, i + 1)
                if i >= 2:
                    pe.wait_ge(lo_ok, i - 1)
                for h in range(H):
                    last = nc.tensor.transpose(g.ps[:, (i % 2) * T + h * P:(i % 2) * T + (h + 1) * P], o[:, i, h * P:(h + 1) * P],
                                               g.const[:, K_ID:K_ID + P])
                last.then_inc(turned, 1)
            pe.wait_ge(lo_ok, NT)
            project_blocks(nc, pe, g, w_hi, w_lo, a_hi, a_lo, w_ready, proj, free)


def phase_merge(nc, g):
    with ExitStack() as ctx:
        sb = lambda n, s, d=F32: ctx.enter_context(nc.sbuf_tensor("i_" + n, s, d))
        sem = lambda n: nc.alloc_semaphore("i_" + n)
        w32, w_hi, w_lo = sb("w32", [P, 2, KD, UNIT]), sb("w_hi", [P, 2, KD, UNIT], F16), sb("w_lo", [P, 2, KD, UNIT], BF16)
        v_hi, v_lo = sb("v_hi", [P, KD, D], F16), sb("v_lo", [P, KD, D], BF16)
        b_hi, b_lo = sb("b_hi", [P, H, T], F16), sb("b_lo", [P, H, T], F16)
        m_hi, m_lo = sb("m_hi", [P, KD, T], F16), sb("m_lo", [P, KD, T], F16)
        gb, m1 = sb("gb", [P, 4, BANK]), sb("m1", [P, 4, BANK])
        x, y = sb("x", [P, 2, D]), sb("y", [P, 2, D])
        fg, gate = sb("fg", [P, D]), sb("gate", [P, D])
        ss = sb("ss", [P, 4])
        w_in, w_cast, w_ready = [sem("w_in0"), sem("w_in1")], sem("w_cast"), sem("w_ready")
        b_in, fg_in, proj, free = sem("b_in"), sem("fg_in"), sem("proj"), sem("free")
        gb_in, m_in = [sem(f"gb_in{i}") for i in range(4)], [sem(f"m_in{i}") for i in range(4)]
        prod, summed, hi_ok, lo_ok = sem("prod"), sem("summed"), sem("hi_ok"), sem("lo_ok")
        out_mm, gate_ok, res, sq_ok, mean, root, inv, done = (sem(n) for n in "out_mm gate_ok res sq_ok mean root inv done".split())
        x_in, y_out = [sem("x_in0"), sem("x_in1")], [sem("y_out0"), sem("y_out1")]
        wo, wv = g.w_o_dsa[0].rearrange("(k p) n -> p k n", p=P), g.w_out[0].rearrange("(k p) n -> p k n", p=P)
        block = ctx.enter_context(nc.Block())

        @block.sync
        def _(sp):
            for u in range(2):
                sp.dma_start(w32[:, u], wo[:, :, u * UNIT:(u + 1) * UNIT]).then_inc(w_in[u], 16)
            for half in range(HALVES):
                cols = slice(half * BANK, (half + 1) * BANK)
                for part, of in ((b_hi, g.bhi_dram), (b_lo, g.blo_dram)):
                    sp.dma_start(part[:, :, cols], of.rearrange("(h p) t -> p h t", p=P)[:, :, cols]).then_inc(b_in, 16)
            for i in range(2):
                sp.dma_start(x[:, i], g.x[0, i * P:(i + 1) * P, :]).then_inc(x_in[i], 16)
            sp.dma_start(fg[:], g.final_g.partition_broadcast(P)).then_inc(fg_in, 16)
            sp.dma_start(gate[:], g.gate_dram[0].partition_broadcast(P)).then_inc(fg_in, 16)
            for n in range(16):
                if n >= 4:
                    sp.wait_ge(summed, n - 3)
                at = (slice((n // 2) * P, (n // 2 + 1) * P), slice((n % 2) * BANK, (n % 2 + 1) * BANK))
                sp.dma_start(gb[:, n % 4], g.sig_dram[2 * D + (n // 2) * P:2 * D + (n // 2 + 1) * P, at[1]]).then_inc(gb_in[n % 4], 16)
                if n >= 4:
                    sp.wait_ge(hi_ok, n - 3)
                    sp.wait_ge(lo_ok, n - 3)
                sp.dma_start(m1[:, n % 4], g.m_dram[at[0], at[1]]).then_inc(m_in[n % 4], 16)
                if n % 2 == 1 and n // 2 < 6:
                    u = 2 + n // 2
                    sp.wait_ge(w_ready, u - 1)
                    src = wo[:, :, u * UNIT:(u + 1) * UNIT] if u < 4 else wv[:, :, (u - 4) * UNIT:(u - 3) * UNIT]
                    sp.dma_start(w32[:, u % 2], src).then_inc(w_in[u % 2], 16)
            for i in range(NT):
                sp.wait_ge(done, i + 1)
                sp.dma_start(g.out[0, i * P:(i + 1) * P, :], y[:, i % 2]).then_inc(y_out[i % 2], 16)
                if i + 2 < NT:
                    sp.dma_start(x[:, i % 2], g.x[0, (i + 2) * P:(i + 3) * P, :]).then_inc(x_in[i % 2], 16)
            for n in range(2):
                sp.wait_ge(y_out[n], 16 * NT // 2)

        @block.gpsimd
        def _(pool):
            for u in range(4):
                pool.wait_ge(w_in[u % 2], 16 * (u // 2 + 1))
                if u >= 2:
                    pool.wait_ge(proj, 4 * (u - 1))
                split_block(nc, pool, w32, w_hi, w_lo, u % 2, w_cast, u).then_inc(w_ready, 1)
            for u in range(4, 8):
                cols = slice((u - 4) * UNIT, (u - 3) * UNIT)
                pool.wait_ge(w_in[u % 2], 16 * (u // 2 + 1))
                nc.gpsimd.tensor_copy(v_hi[:, :, cols], w32[:, u % 2]).then_inc(w_cast, 1)
                pool.wait_ge(w_cast, u + 1)
                nc.gpsimd.tensor_tensor(v_lo[:, :, cols], w32[:, u % 2], v_hi[:, :, cols], ALU.subtract).then_inc(w_ready, 1)

        @block.tensor
        def _(pe):
            pe.wait_ge(b_in, 64)
            project_blocks(nc, pe, g, w_hi, w_lo, b_hi, b_lo, w_ready, proj, free)
            pe.wait_ge(w_ready, 8)
            pe.wait_ge(lo_ok, 16)
            with pe.Fori(0, NT // 2) as t:
                for e in range(2):
                    pe.wait_ge(gate_ok, t * 4 + 2 * e + 2)
                    for half in range(HALVES):
                        for k in range(KD):
                            tok = bass.ds((t * 2 + e) * P, P)
                            last = three(nc.tensor, g.ps[:, (2 * e + half) * BANK:(2 * e + half + 1) * BANK], m_hi[:, k, tok], m_lo[:, k, tok],
                                         v_hi[:, k, half * BANK:(half + 1) * BANK], v_lo[:, k, half * BANK:(half + 1) * BANK], k == 0, k == KD - 1)
                    last.then_inc(out_mm, 1)

        @block.scalar
        def _(act):
            with act.Fori(0, 2) as t:
                for n in range(8):
                    b, half = divmod(n, 2)
                    act.wait_ge(summed, t * 8 + n + 1)
                    nc.scalar.mul(m_hi[:, bass.ds(t * 4 + b, 1), half * BANK:(half + 1) * BANK], m1[:, n % 4].unsqueeze(1), SHRINK).then_inc(hi_ok, 1)
            for i in range(NT):
                act.wait_ge(res, i + 1)
                if i >= 2:
                    act.wait_ge(y_out[i % 2], 16 * (i // 2))
                nc.scalar.activation(y[:, i % 2], x[:, i % 2], ACT.Square, accum_out=ss[:, 2 * (i % 2):2 * (i % 2) + 1]).then_inc(sq_ok, 1)
                act.wait_ge(mean, i + 1)
                nc.scalar.activation(ss[:, 2 * (i % 2) + 1:2 * (i % 2) + 2], ss[:, 2 * (i % 2) + 1:2 * (i % 2) + 2], ACT.Sqrt).then_inc(root, 1)

        @block.vector
        def _(dve):
            dve.nop().then_inc(free, 8)
            with dve.Fori(0, 2) as t:
                for n in range(8):
                    b, half = divmod(n, 2)
                    dve.wait_ge(proj, t * 8 + n + 1)
                    dve.wait_ge(gb_in[n % 4], t * 32 + 16 * (n // 4 + 1))
                    nc.vector.tensor_tensor(gb[:, n % 4], g.ps[:, n * BANK:(n + 1) * BANK], gb[:, n % 4], ALU.mult).then_inc(free, 1)
                    dve.wait_ge(m_in[n % 4], t * 32 + 16 * (n // 4 + 1))
                    dve.wait_ge(free, t * 8 + 8 + n + 1)
                    nc.vector.tensor_tensor(m1[:, n % 4], m1[:, n % 4], gb[:, n % 4], ALU.add).then_inc(summed, 1)
                    dve.wait_ge(hi_ok, t * 8 + n + 1)
                    at = (slice(None), bass.ds(t * 4 + b, 1), slice(half * BANK, (half + 1) * BANK))
                    nc.vector.scalar_tensor_tensor(out=m_lo[at], in0=m1[:, n % 4].unsqueeze(1), scalar=SHRINK,
                                                   in1=m_hi[at], op0=ALU.mult, op1=ALU.subtract).then_inc(lo_ok, 1)
            dve.nop().then_inc(gate_ok, 4)
            dve.wait_ge(fg_in, 32)
            dve.wait_ge(lo_ok, 16)
            for i in range(NT):
                e = i % 2
                dve.wait_ge(out_mm, i + 1)
                if i >= 2:
                    dve.wait_ge(y_out[e], 16 * (i // 2))
                nc.vector.scalar_tensor_tensor(out=y[:, e], in0=g.ps[:, e * T:(e + 1) * T], scalar=1.0 / SHRINK, in1=gate[:],
                                               op0=ALU.mult, op1=ALU.mult).then_inc(gate_ok, 2)
                dve.wait_ge(x_in[e], 16 * (i // 2 + 1))
                dve.wait_ge(gate_ok, 4 + 2 * (i + 1))
                nc.vector.tensor_tensor(x[:, e], x[:, e], y[:, e], ALU.add).then_inc(res, 1)
                dve.wait_ge(sq_ok, i + 1)
                nc.vector.tensor_scalar(ss[:, 2 * e + 1:2 * e + 2], ss[:, 2 * e:2 * e + 1], 1.0 / D, EPS, ALU.mult, ALU.add).then_inc(mean, 1)
                dve.wait_ge(root, i + 1)
                nc.vector.reciprocal(ss[:, 2 * e:2 * e + 1], ss[:, 2 * e + 1:2 * e + 2]).then_inc(inv, 1)
                dve.wait_ge(inv, i + 1)
                nc.vector.scalar_tensor_tensor(out=y[:, e], in0=x[:, e], scalar=ss[:, 2 * e:2 * e + 1], in1=fg[:],
                                               op0=ALU.mult, op1=ALU.mult).then_inc(done, 1)


NEAR = 2 * P


def phase_attention(nc, g):
    with ExitStack() as ctx:
        sb = lambda n, s, d=F32: ctx.enter_context(nc.sbuf_tensor("j_" + n, s, d))
        sem = lambda n: nc.alloc_semaphore("j_" + n)
        q_hi, q_lo = sb("q_hi", [P, H, T], F16), sb("q_lo", [P, H, T], F16)
        c_hi, c_lo = sb("c_hi", [P, NT, RANK], F16), sb("c_lo", [P, NT, RANK], F16)
        ct_hi, ct_lo = sb("ct_hi", [P, 2, T], F16), sb("ct_lo", [P, 2, T], F16)
        uk_hi, uk_lo = sb("uk_hi", [P, H, RANK], F16), sb("uk_lo", [P, H, RANK], BF16)
        uv_hi, uv_lo = sb("uv_hi", [P, 2, D], F16), sb("uv_lo", [P, 2, D], BF16)
        bias_hi, bias_lo = sb("bias_hi", [P, H, NEAR], F16), sb("bias_lo", [P, H, NEAR], F16)
        mask = sb("mask", [P, g.first[NT]], BF16)
        ident_b, flip_h = sb("ident_b", [P, P], BF16), sb("flip_h", [P, P], F16)
        latents(nc, g, locals())
        attend(nc, g, locals())


def latents(nc, g, a):
    q_hi, q_lo, c_hi, c_lo, ct_hi, ct_lo = (a[n] for n in ("q_hi", "q_lo", "c_hi", "c_lo", "ct_hi", "ct_lo"))
    uk_hi, uk_lo, uv_hi, uv_lo, bias_hi, bias_lo = (a[n] for n in ("uk_hi", "uk_lo", "uv_hi", "uv_lo", "bias_hi", "bias_lo"))
    with ExitStack() as ctx:
        sb = lambda n, s, d=F32: ctx.enter_context(nc.sbuf_tensor("k_" + n, s, d))
        sem = lambda n: nc.alloc_semaphore("k_" + n)
        w32, w_hi, w_lo = sb("w32", [P, 2, KD, UNIT]), sb("w_hi", [P, 2, KD, UNIT], F16), sb("w_lo", [P, 2, KD, UNIT], BF16)
        uk32, uv32 = sb("uk32", [P, 2, D]), sb("uv32", [P, 2, D])
        kvg = sb("kvg", [P, RANK])
        onehot, rel, rows = sb("onehot", [NBUCKETS, K_BUCKETS]), sb("rel", [NBUCKETS, H]), sb("rows", [H, K_BUCKETS])
        rows2 = sb("rows2", [H, K_BUCKETS])
        bias32 = sb("bias32", [P, H, NEAR])
        c32, sq = sb("c32", [P, NT, RANK]), sb("sq", [P, NT, RANK])
        ss, r = sb("ss", [P, NT]), sb("r", [P, NT])
        w_in, w_cast, w_ready = [sem("w_in0"), sem("w_in1")], sem("w_cast"), sem("w_ready")
        (uk_in, uv_in, kv_in, mask_in, rel_in, rows_out, bias_in, raw, ss_ok, mean, root, inv, normed, proj, q_h, q_l,
         rows_mm, rows_ok, b_h, uk_mm, uk_h, uk_l, uv_h, ch, turned, ct_h, ct_l, const_ok) = (sem(n) for n in (
             "uk_in uv_in kv_in mask_in rel_in rows_out bias_in raw ss_ok mean root inv normed proj q_h q_l rows_mm rows_ok "
             "b_h uk_mm uk_h uk_l uv_h ch turned ct_h ct_l const_ok").split())
        bank = lambda k: g.ps[:, k * BANK:(k + 1) * BANK]
        win = g.w_in[0].rearrange("(k p) n -> p k n", p=P)
        order = [C_CKV] + [C_QB + u * UNIT for u in range(4)]
        block = ctx.enter_context(nc.Block())

        @block.sync
        def _(sp):
            for u in range(2):
                sp.dma_start(w32[:, u], win[:, :, order[u]:order[u] + UNIT]).then_inc(w_in[u], 16)
            sp.dma_start(kvg[:], g.kv_norm_g[0].partition_broadcast(P)).then_inc(kv_in, 16)
            sp.dma_start(onehot[:], g.buckets_dram).then_inc(rel_in, 16)
            sp.dma_start(rel[:], g.rel_bias).then_inc(rel_in, 16)
            sp.dma_start(uk32[:], g.w_uk[0].rearrange("(q p) h d -> p q (h d)", p=P)).then_inc(uk_in, 16)
            sp.dma_start(uv32[:], g.w_uv[0].rearrange("(q p) h d -> p q (h d)", p=P)).then_inc(uv_in, 16)
            sp.dma_start(a["mask"][:], g.mask_dram).then_inc(mask_in, 16)
            sp.wait_ge(rows_ok, 2)
            sp.dma_start(g.rows_dram, rows2[:]).then_inc(rows_out, 16)
            sp.wait_ge(rows_out, 16)
            sp.dma_start(bias32[:], bass.AP(g.rows_dram.tensor, 0, [[1, P], [K_BUCKETS, H], [1, NEAR]])).then_inc(bias_in, 16)
            for u in range(2, 5):
                sp.wait_ge(w_ready, u - 1)
                sp.dma_start(w32[:, u % 2], win[:, :, order[u]:order[u] + UNIT]).then_inc(w_in[u % 2], 16)
            sp.wait_ge(mask_in, 16)

        @block.gpsimd
        def _(pool):
            for u in range(5):
                pool.wait_ge(w_in[u % 2], 16 * (u // 2 + 1))
                if u == 2:
                    pool.wait_ge(raw, NT)
                elif u > 2:
                    pool.wait_ge(proj, 4 * (u - 2))
                split_block(nc, pool, w32, w_hi, w_lo, u % 2, w_cast, u).then_inc(w_ready, 1)
                if u == 1:
                    pool.wait_ge(uv_in, 16)
                    nc.gpsimd.tensor_copy(uv_hi[:], uv32[:]).then_inc(uv_h, 1)
                    pool.wait_ge(uv_h, 1)
                    nc.gpsimd.tensor_tensor(uv_lo[:], uv32[:], uv_hi[:], ALU.subtract)
                    pool.wait_ge(b_h, 1)
                    nc.gpsimd.tensor_tensor(bias_lo[:], bias32[:], bias_hi[:], ALU.subtract)
            pool.wait_ge(ch, 1)
            nc.gpsimd.tensor_tensor(c_lo[:], c32[:], c_hi[:], ALU.subtract)

        @block.tensor
        def _(pe):
            pe.wait_ge(w_ready, 1)
            for i in range(NT):
                for k in range(KD):
                    last = three(nc.tensor, g.ps[:, i * BANK:i * BANK + RANK], g.h_hi[:, k, i * P:(i + 1) * P], g.h_lo[:, k, i * P:(i + 1) * P],
                                 w_hi[:, 0, k], w_lo[:, 0, k], k == 0, k == KD - 1)
                last.then_inc(raw, 1)
            pe.wait_ge(rel_in, 32)
            pe.wait_ge(normed, 1)
            nc.tensor.matmul(g.ps[0:H, 0:K_BUCKETS], rel[:], onehot[:], start=True, stop=True).then_inc(rows_mm, 1)
            pe.wait_ge(uk_in, 16)
            for n in range(4):
                pe.wait_ge(normed, 2 * n + 3 if n < 3 else NT)
                for j in range(4):
                    h, q = 2 * n + j // 2, j % 2
                    last = nc.tensor.transpose(g.ps[:, (1 + n) * BANK + j * P:(1 + n) * BANK + (j + 1) * P], uk32[:, q, h * P:(h + 1) * P],
                                               g.const[:, K_ID:K_ID + P])
                last.then_inc(uk_mm, 1)
            pe.wait_ge(normed, NT)
            pe.wait_ge(rows_ok, 1)
            for u in range(4):
                pe.wait_ge(w_ready, u + 2)
                for b in range(2):
                    for half in range(HALVES):
                        n = 4 * u + 2 * b + half
                        if n >= 3:
                            pe.wait_ge(q_l, n - 2)
                        at = (0, 5, 6)[n % 3]
                        cols = slice(half * BANK, (half + 1) * BANK)
                        s = (u + 1) % 2
                        for k in range(KD):
                            last = three(nc.tensor, bank(at), w_hi[:, s, k, b * P:(b + 1) * P], w_lo[:, s, k, b * P:(b + 1) * P],
                                         g.h_hi[:, k, cols], g.h_lo[:, k, cols], k == 0, k == KD - 1)
                        last.then_inc(proj, 1)
            pe.wait_ge(normed, NT)
            pe.wait_ge(uk_l, 4)
            for n in range(4):
                q, half = divmod(n, HALVES)
                for j in range(4):
                    last = nc.tensor.transpose(g.ps[:, (1 + n) * BANK + j * P:(1 + n) * BANK + (j + 1) * P],
                                               c32[:, 4 * half + j, q * P:(q + 1) * P], g.const[:, K_ID:K_ID + P])
                last.then_inc(turned, 1)

        @block.scalar
        def _(act):
            for i in range(NT):
                act.wait_ge(raw, i + 1)
                nc.scalar.activation(sq[:, i], g.ps[:, i * BANK:i * BANK + RANK], ACT.Square, accum_out=ss[:, i:i + 1]).then_inc(ss_ok, 1)
            act.wait_ge(mean, 1)
            nc.scalar.activation(r[:], r[:], ACT.Sqrt).then_inc(root, 1)
            for n in range(4):
                act.wait_ge(uk_mm, n + 1)
                nc.scalar.copy(uk_hi[:, 2 * n:2 * n + 2], bank(1 + n).rearrange("p (h c) -> p h c", c=RANK)).then_inc(uk_h, 1)
            act.wait_ge(bias_in, 16)
            nc.scalar.copy(bias_hi[:], bias32[:]).then_inc(b_h, 1)
            for n in range(16):
                act.wait_ge(proj, n + 1)
                nc.scalar.copy(q_hi[:, n // 2, (n % 2) * BANK:(n % 2 + 1) * BANK], bank((0, 5, 6)[n % 3])).then_inc(q_h, 1)
                if n == 3:
                    act.wait_ge(normed, NT)
                    nc.scalar.copy(c_hi[:], c32[:]).then_inc(ch, 1)
            for n in range(4):
                act.wait_ge(turned, n + 1)
                nc.scalar.copy(ct_hi[:, n // 2, (n % 2) * BANK:(n % 2 + 1) * BANK], bank(1 + n)).then_inc(ct_h, 1)

        @block.vector
        def _(dve):
            nc.vector.tensor_copy(a["ident_b"][:], g.const[:, K_ID:K_ID + P])
            nc.vector.tensor_copy(a["flip_h"][:], g.const[:, K_FLIP:K_FLIP + P])
            dve.wait_ge(ss_ok, NT)
            nc.vector.tensor_scalar(r[:], ss[:], 1.0 / RANK, EPS, ALU.mult, ALU.add).then_inc(mean, 1)
            dve.wait_ge(root, 1)
            nc.vector.reciprocal(ss[:], r[:]).then_inc(inv, 1)
            dve.wait_ge(inv, 1)
            dve.wait_ge(kv_in, 16)
            for i in range(NT):
                nc.vector.scalar_tensor_tensor(out=c32[:, i], in0=g.ps[:, i * BANK:i * BANK + RANK], scalar=ss[:, i:i + 1],
                                               in1=kvg[:], op0=ALU.mult, op1=ALU.mult).then_inc(normed, 1)
            dve.wait_ge(rows_mm, 1)
            nc.vector.tensor_copy(rows[:], g.ps[0:H, 0:K_BUCKETS]).then_inc(rows_ok, 1)
            dve.wait_ge(rows_ok, 1)
            nc.vector.tensor_scalar(rows2[:], rows[:], rows[:, 0:1], None, ALU.subtract).then_inc(rows_ok, 1)
            for n in range(4):
                dve.wait_ge(uk_h, n + 1)
                nc.vector.tensor_tensor(uk_lo[:, 2 * n:2 * n + 2], bank(1 + n).rearrange("p (h c) -> p h c", c=RANK),
                                        uk_hi[:, 2 * n:2 * n + 2], ALU.subtract).then_inc(uk_l, 1)
            for n in range(16):
                dve.wait_ge(q_h, n + 1)
                at = (slice(None), n // 2, slice((n % 2) * BANK, (n % 2 + 1) * BANK))
                nc.vector.tensor_tensor(q_lo[at], bank((0, 5, 6)[n % 3]), q_hi[at], ALU.subtract).then_inc(q_l, 1)
            for n in range(4):
                dve.wait_ge(ct_h, n + 1)
                at = (slice(None), n // 2, slice((n % 2) * BANK, (n % 2 + 1) * BANK))
                nc.vector.tensor_tensor(ct_lo[at], bank(1 + n), ct_hi[at], ALU.subtract).then_inc(ct_l, 1)


def attend(nc, g, a):
    q_hi, q_lo, c_hi, c_lo, ct_hi, ct_lo = (a[n] for n in ("q_hi", "q_lo", "c_hi", "c_lo", "ct_hi", "ct_lo"))
    uk_hi, uk_lo, uv_hi, uv_lo, bias_hi, bias_lo = (a[n] for n in ("uk_hi", "uk_lo", "uv_hi", "uv_lo", "bias_hi", "bias_lo"))
    mask, ident_b, flip_h = a["mask"], a["ident_b"], a["flip_h"]
    with ExitStack() as ctx:
        sb = lambda n, s, d=F32: ctx.enter_context(nc.sbuf_tensor("l_" + n, s, d))
        sem = lambda n: nc.alloc_semaphore("l_" + n)
        lat_hi, lat_lo = sb("lat_hi", [P, 2, T], F16), sb("lat_lo", [P, 2, T], F16)
        p = sb("p", [P, 2, T])
        pt_hi, pt_lo = sb("pt_hi", [P, 2, NT, P], F16), sb("pt_lo", [P, 2, NT, P], F16)
        ol_hi, ol_lo = sb("ol_hi", [P, 2, 2, P], F16), sb("ol_lo", [P, 2, 2, P], F16)
        top, total, share = sb("top", [P, 2]), sb("total", [P, 2]), sb("share", [P, 2])
        z = sb("z", [P, 2, T])
        b32 = sb("b32", [P, 2, P])
        b_hi, b_lo = sb("b_hi", [P, 2, T], F16), sb("b_lo", [P, 2, T], F16)
        (lat, lat_h, lat_l, logit, top_ok, exp_ok, inv, shared, turned, pt_h, pt_l, pv, ol_h, ol_l, up, got, b_h, b_l) = (
            sem(n) for n in "lat lat_h lat_l logit top_ok exp_ok inv shared turned pt_h pt_l pv ol_h ol_l up got b_h b_l".split())
        z_in, b_out = [sem("z_in0"), sem("z_in1")], [sem("b_out0"), sem("b_out1")]
        block = ctx.enter_context(nc.Block())
        TURNS = H // 2
        steps = [(e, i) for e in range(2) for i in reversed(range(NT))]
        N = len(steps)
        wide = [(i + 1) * P for _, i in steps]
        bank = lambda k: g.ps[:, k * BANK:(k + 1) * BANK]

        def start(engine, *sems):
            for n in sems:
                engine.nop().then_inc(n, 1)

        @block.sync
        def _(sp):
            for t in range(TURNS):
                for e in range(2):
                    h = 2 * t + e
                    if t:
                        sp.wait_ge(got, N * (t - 1) + NT * (e + 1) + 1)
                    sp.dma_start(z[:, e], g.sig_dram[h * P:(h + 1) * P, :]).then_inc(z_in[e], 16)
            for e in range(2):
                sp.wait_ge(b_out[e], 32 * TURNS + 1)

        @block.tensor
        def _(pe):
            mm = nc.tensor.matmul

            def queries(t, e):
                for half in range(HALVES):
                    for q in range(2):
                        n = 2 * half + q
                        pe.wait_ge(exp_ok, t * N + e * NT + 1)
                        cols = slice(half * BANK, (half + 1) * BANK)
                        head = bass.ds(t * 2 + e, 1)
                        last = three(nc.tensor, bank(n), uk_hi[:, head, q * P:(q + 1) * P], uk_lo[:, head, q * P:(q + 1) * P],
                                     q_hi[:, head, cols], q_lo[:, head, cols], True, True)
                        last.then_inc(lat, 1)
                pe.wait_ge(lat_l, t * 8 + 4 * e + 4 + 1)

            def logits(t, n):
                e, i = steps[n]
                head = bass.ds(t * 2 + e, 1)
                if n >= 2 and n != NT:
                    pe.wait_ge(exp_ok, t * N + n - 1 + 1)
                tok = slice(i * P, (i + 1) * P)
                at = (n % 2) * T
                for c0 in range(0, wide[n], BANK):
                    c1 = min(wide[n], c0 + BANK)
                    out = g.ps[:, at + c0:at + c1]
                    for q in range(2):
                        three(nc.tensor, out, lat_hi[:, q, tok], lat_lo[:, q, tok], ct_hi[:, q, c0:c1], ct_lo[:, q, c0:c1], q == 0, False)
                    n0, n1 = max(c0, (i - 1) * P, 0), min(c1, (i + 1) * P)
                    if n0 < n1:
                        b0 = n0 - (i - 1) * P
                        for part in (bias_hi, bias_lo):
                            mm(g.ps[:, at + n0:at + n1], flip_h[:], part[:, head, b0:b0 + n1 - n0], start=False, stop=False)
                    last = mm(out, ident_b[:], mask[:, g.first[i] + c0:g.first[i] + c1], start=False, stop=True)
                last.then_inc(logit, 1)

            def turn(t, n):
                e, i = steps[n]
                pe.wait_ge(shared, t * N + n + 2)
                pe.wait_ge(pt_l, t * N + n + 1)
                for j in range(i + 1):
                    last = nc.tensor.transpose(g.ps[:, 4 * BANK + j * P:4 * BANK + (j + 1) * P], p[:, n % 2, j * P:(j + 1) * P],
                                               g.const[:, K_ID:K_ID + P])
                last.then_inc(turned, 1)

            def values(t, n):
                e, i = steps[n]
                pe.wait_ge(pt_l, t * N + n + 2)
                pe.wait_ge(ol_l, t * N + n + 1)
                for q in range(2):
                    for j in range(i + 1):
                        cs = slice(q * P, (q + 1) * P)
                        last = three(nc.tensor, g.ps[:, 6 * BANK + q * P:6 * BANK + (q + 1) * P], c_hi[:, j, cs], c_lo[:, j, cs],
                                     pt_hi[:, n % 2, j], pt_lo[:, n % 2, j], j == 0, j == i)
                last.then_inc(pv, 1)

            def lift(t, n):
                e, i = steps[n]
                pe.wait_ge(ol_l, t * N + n + 2)
                pe.wait_ge(got, t * N + n + 1)
                for q in range(2):
                    cols = bass.ds((t * 2 + e) * P, P)
                    last = three(nc.tensor, g.ps[:, 7 * BANK:7 * BANK + P], uv_hi[:, q, cols], uv_lo[:, q, cols],
                                 ol_hi[:, n % 2, q], ol_lo[:, n % 2, q], q == 0, q == 1)
                last.then_inc(up, 1)

            start(pe, lat, logit, turned, pv, up)
            with pe.Fori(0, TURNS) as t:
                for n in range(N + 3):
                    if n in (0, NT):
                        queries(t, n // NT)
                    if n < N:
                        logits(t, n)
                    if 0 <= n - 1 < N:
                        turn(t, n - 1)
                    if 0 <= n - 2 < N:
                        values(t, n - 2)
                    if 0 <= n - 3 < N:
                        lift(t, n - 3)

        @block.scalar
        def _(act):
            def queries(t, e):
                for n in range(4):
                    half, q = divmod(n, 2)
                    cols = slice(half * BANK, (half + 1) * BANK)
                    act.wait_ge(lat, t * 8 + 4 * e + n + 2)
                    nc.scalar.mul(lat_hi[:, q, cols], bank(n), P ** -0.5).then_inc(lat_h, 1)

            def soften(t, n):
                act.wait_ge(top_ok, t * N + n + 2)
                act.wait_ge(turned, (t * N + n - 1 if n >= 2 else t * N) + 1)
                nc.scalar.activation(p[:, n % 2, 0:wide[n]], g.ps[:, (n % 2) * T:(n % 2) * T + wide[n]], ACT.Exp,
                                     bias=top[:, n % 2:n % 2 + 1], accum_out=total[:, n % 2:n % 2 + 1]).then_inc(exp_ok, 1)

            def split_p(t, n):
                i = steps[n][1]
                act.wait_ge(turned, t * N + n + 2)
                act.wait_ge(pv, (t * N + n - 1 if n >= 2 else t * N) + 1)
                nc.scalar.copy(pt_hi[:, n % 2, 0:i + 1], g.ps[:, 4 * BANK:4 * BANK + wide[n]].rearrange("p (j t) -> p j t", t=P)).then_inc(pt_h, 1)

            def split_o(t, n):
                act.wait_ge(pv, t * N + n + 2)
                act.wait_ge(up, (t * N + n - 1 if n >= 2 else t * N) + 1)
                nc.scalar.copy(ol_hi[:, n % 2], g.ps[:, 6 * BANK:6 * BANK + RANK].rearrange("p (q t) -> p q t", t=P)).then_inc(ol_h, 1)

            def split_b(t, n):
                e, i = steps[n]
                act.wait_ge(got, t * N + n + 2)
                if i == NT - 1:
                    act.wait_ge(b_out[e], t * 32 + 1)
                nc.scalar.copy(b_hi[:, e, i * P:(i + 1) * P], b32[:, n % 2]).then_inc(b_h, 1)
                if i == 0:
                    act.wait_ge(b_l, t * N + n + 2)
                    act.wait_ge(b_h, t * N + n + 2)
                    rows = bass.ds((t * 2 + e) * P, P)
                    act.dma_start(g.bhi_dram[rows, :], b_hi[:, e]).then_inc(b_out[e], 16)
                    act.dma_start(g.blo_dram[rows, :], b_lo[:, e]).then_inc(b_out[e], 16)

            start(act, lat_h, exp_ok, pt_h, ol_h, b_h, *b_out)
            with act.Fori(0, TURNS) as t:
                for n in range(N + 4):
                    if n in (0, NT):
                        queries(t, n // NT)
                    if n < N:
                        soften(t, n)
                    if 0 <= n - 1 < N:
                        split_p(t, n - 1)
                    if 0 <= n - 2 < N:
                        split_o(t, n - 2)
                    if 0 <= n - 3 < N:
                        split_b(t, n - 3)

        @block.vector
        def _(dve):
            def queries(t, e):
                for n in range(4):
                    half, q = divmod(n, 2)
                    cols = slice(half * BANK, (half + 1) * BANK)
                    dve.wait_ge(lat_h, t * 8 + 4 * e + n + 2)
                    nc.vector.scalar_tensor_tensor(out=lat_lo[:, q, cols], in0=bank(n), scalar=P ** -0.5, in1=lat_hi[:, q, cols],
                                                   op0=ALU.mult, op1=ALU.subtract).then_inc(lat_l, 1)

            def peak(t, n):
                dve.wait_ge(logit, t * N + n + 2)
                dve.wait_ge(exp_ok, (t * N + n - 1 if n >= 2 else t * N) + 1)
                nc.vector.tensor_reduce(top[:, n % 2:n % 2 + 1], g.ps[:, (n % 2) * T:(n % 2) * T + wide[n]], AX.X, ALU.max,
                                        negate=True).then_inc(top_ok, 1)

            def norm(t, n):
                dve.wait_ge(exp_ok, t * N + n + 2)
                nc.vector.reciprocal(share[:, n % 2:n % 2 + 1], total[:, n % 2:n % 2 + 1]).then_inc(inv, 1)
                dve.wait_ge(inv, t * N + n + 2)
                nc.vector.tensor_scalar(p[:, n % 2, 0:wide[n]], p[:, n % 2, 0:wide[n]], share[:, n % 2:n % 2 + 1], None, ALU.mult).then_inc(shared, 1)

            def split_p(t, n):
                i = steps[n][1]
                dve.wait_ge(pt_h, t * N + n + 2)
                nc.vector.tensor_tensor(pt_lo[:, n % 2, 0:i + 1], g.ps[:, 4 * BANK:4 * BANK + wide[n]].rearrange("p (j t) -> p j t", t=P),
                                        pt_hi[:, n % 2, 0:i + 1], ALU.subtract).then_inc(pt_l, 1)

            def split_o(t, n):
                dve.wait_ge(ol_h, t * N + n + 2)
                nc.vector.tensor_tensor(ol_lo[:, n % 2], g.ps[:, 6 * BANK:6 * BANK + RANK].rearrange("p (q t) -> p q t", t=P),
                                        ol_hi[:, n % 2], ALU.subtract).then_inc(ol_l, 1)

            def gate(t, n):
                e, i = steps[n]
                dve.wait_ge(up, t * N + n + 2)
                dve.wait_ge(b_l, (t * N + n - 1 if n >= 2 else t * N) + 1)
                dve.wait_ge(z_in[e], t * 16 + 16)
                nc.vector.tensor_tensor(b32[:, n % 2], g.ps[:, 7 * BANK:7 * BANK + P], z[:, e, i * P:(i + 1) * P], ALU.mult).then_inc(got, 1)

            start(dve, lat_l, top_ok, inv, shared, pt_l, ol_l, got)
            with dve.Fori(0, TURNS) as t:
                for n in range(N + 4):
                    if n in (0, NT):
                        queries(t, n // NT)
                    if n < N:
                        peak(t, n)
                        norm(t, n)
                    if 0 <= n - 1 < N:
                        split_p(t, n - 1)
                    if 0 <= n - 2 < N:
                        split_o(t, n - 2)
                    if 0 <= n - 3 < N:
                        gate(t, n - 3)

        @block.gpsimd
        def _(pool):
            start(pool, b_l)
            with pool.Fori(0, TURNS) as t:
                for n, (e, i) in enumerate(steps):
                    pool.wait_ge(b_h, t * N + n + 2)
                    nc.gpsimd.tensor_tensor(b_lo[:, e, i * P:(i + 1) * P], b32[:, n % 2], b_hi[:, e, i * P:(i + 1) * P], ALU.subtract).then_inc(b_l, 1)


def program(nc, g):
    scratch = lambda n, s, d=F32: nc.dram_tensor(n, s, d, kind="Internal").ap()
    g.gate_dram = scratch("gate_row", [1, D])
    g.z_dram = scratch("delta_gate", [T, D])
    g.sig_dram = scratch("channel_gates", [3 * D, T])
    g.mask_dram = scratch("mask", [P, P * NT * (NT + 1) // 2], BF16)
    g.o_dram = scratch("delta_out", [T, D])
    g.m_dram = scratch("merge_half", [D, T])
    g.rows_dram = scratch("bias_rows", [H, K_BUCKETS])
    g.bhi_dram, g.blo_dram = scratch("attended_hi", [D, T], F16), scratch("attended_lo", [D, T], F16)
    g.first = [P * i * (i + 1) // 2 for i in range(NT + 1)]
    with ExitStack() as ctx:
        g.ps = ctx.enter_context(nc.psum_tensor("ps", [P, 8 * BANK], F32))
        sb = lambda n, s, d=F32: ctx.enter_context(nc.sbuf_tensor("g_" + n, s, d))
        g.const = sb("const", [P, K_ALL])
        g.eps = sb("eps", [P, 1])
        with ExitStack() as inner:
            sb = lambda n, s, d=F32: inner.enter_context(nc.sbuf_tensor("g_" + n, s, d))
            g.h_hi, g.h_lo = sb("h_hi", [P, KD, T], F16), sb("h_lo", [P, KD, T], F16)
            with ExitStack() as tables:
                sb = lambda n, s, d=F32: tables.enter_context(nc.sbuf_tensor("g_" + n, s, d))
                g.g, g.beta, g.nbeta = sb("g", [P, NT, H]), sb("beta", [P, NT, H]), sb("nbeta", [P, NT, H])
                g.decays = sb("decays", [P, 4, NT, H])
                g.taps = sb("taps", [P, 96])
                with nc.cleanup_on_exit():
                    phase_hidden(nc, g)
                    with ExitStack() as scores:
                        sb = lambda n, s, d=F32: scores.enter_context(nc.sbuf_tensor("g_" + n, s, d))
                        g.small = sb("small", [P, NT, 24])
                        g.score = sb("score", [P, g.first[NT]])
                        g.mask = sb("mask", [P, g.first[NT]], BF16)
                        phase_index(nc, g)
                        phase_topk(nc, g)
                        phase_decay(nc, g)
                with nc.cleanup_on_exit():
                    phase_delta(nc, g)
            with nc.cleanup_on_exit():
                phase_delta_out(nc, g)
                phase_attention(nc, g)
        with nc.cleanup_on_exit():
            phase_merge(nc, g)


INPUTS = ["x", "c", "norm_g", "w_ada", "b_ada", "w_in", "conv_w", "a_log", "dt_bias", "gdn_norm_g", "w_o_gdn",
          "kv_norm_g", "w_uk", "w_uv", "w_o_dsa", "w_out", "rel_bias", "final_g"]


def kernel(**inputs):
    import concourse.bacc as bacc
    from concourse.bass_utils import run_bass_kernel_spmd

    nc = bacc.Bacc("TRN2", target_bir_lowering=False, num_devices=1)
    g = Tensors()
    arrays = {"in_" + n: np.ascontiguousarray(inputs[n]) for n in INPUTS}
    arrays["in_const_dram"], arrays["in_buckets_dram"] = constant_table(), bucket_table()
    for n, a in arrays.items():
        g.__dict__[n.removeprefix("in_")] = nc.dram_tensor(n, a.shape, F32, kind="ExternalInput").ap()
    g.out = nc.dram_tensor("out", [1, T, D], F32, kind="ExternalOutput").ap()
    program(nc, g)
    r = run_bass_kernel_spmd(nc, [arrays], core_ids=[0])
    return r.results[0]["out"]
```

```python
import concourse.bass as bass
from concourse import mybir
from contextlib import ExitStack
import numpy as np

F32 = mybir.dt.float32
F16 = mybir.dt.float16
BF16 = mybir.dt.bfloat16
ALU = mybir.AluOpType
ACT = mybir.ActivationFunctionType
AX = mybir.AxisListType

P = 128
T = 1024
D = 1024
NT = T // P
KD = D // P
H = 8
CHUNK = 64
IDX_DIM = 64
RANK = 256
TOPK = 256
NBUCKETS = 32
EPS = 1e-6
BANK = 512
HALVES = T // BANK

C_Q, C_K, C_V, C_ZA, C_AA, C_BA = 0, 1024, 2048, 3072, 4096, 4104
C_QB, C_CKV, C_ZB, C_QI, C_KI, C_WI, C_GL = 4112, 5136, 5392, 6416, 6928, 6992, 7000
NS = 152
UNIT = 256

BELOW = -3.0e38
TAKEN = float(np.finfo(np.float32).min)
CLOSED = -1.0e30

K_ID, K_FLIP, K_UPTO, K_AFTER, K_CH0, K_CH1, K_CAUSAL, K_LEVEL = 0, 128, 256, 384, 512, 640, 768, 896
K_ALL = K_LEVEL + 6 * 128
K_BUCKETS = 384


def constant_table():
    t = np.zeros((P, K_ALL), np.float32)
    i = np.arange(P)
    row, col = i[:, None], i[None, :]
    same = row // CHUNK == col // CHUNK
    t[:, K_ID:K_ID + P] = row == col
    t[:, K_FLIP:K_FLIP + P] = row + col == P - 1
    t[:, K_UPTO:K_UPTO + P] = same & (row <= col)
    t[:, K_AFTER:K_AFTER + P] = same & (row > col)
    t[:, K_CH0:K_CH0 + P] = row < CHUNK
    t[:, K_CH1:K_CH1 + P] = row >= CHUNK
    t[:, K_CAUSAL:K_CAUSAL + P] = np.where(col > row, BELOW, 0)
    for level in range(6):
        b = 1 << level
        m = (row // (2 * b) == col // (2 * b)) & (row % (2 * b) < b) & (col % (2 * b) >= b)
        t[:, K_LEVEL + level * P:K_LEVEL + (level + 1) * P] = m
    return t


def bucket_table():
    n = np.maximum(255 - np.arange(K_BUCKETS), 0)
    nf = np.maximum(n, 1).astype(np.float32)
    large = 16 + (np.log(nf / np.float32(16)) / np.float32(np.log(128 / 16)) * np.float32(16)).astype(np.int32)
    bucket = np.where(n < 16, n, np.minimum(large, NBUCKETS - 1))
    return (np.arange(NBUCKETS)[:, None] == bucket[None, :]).astype(np.float32)


class Tensors:
    pass


def three(pe, out, a_hi, a_lo, b_hi, b_lo, first, last):
    pe.matmul(out, a_hi, b_hi, start=first, stop=False)
    pe.matmul(out, a_hi, b_lo, start=False, stop=False)
    return pe.matmul(out, a_lo, b_hi, start=False, stop=last)


def phase_hidden(nc, g):
    with ExitStack() as ctx:
        sb = lambda n, s, d=F32: ctx.enter_context(nc.sbuf_tensor("a_" + n, s, d))
        sem = lambda n: nc.alloc_semaphore("a_" + n)
        x_sb = sb("x", [P, NT, D])
        w_ada = sb("w_ada", [P, KD, 2 * D])
        rows = sb("rows", [32, P])
        cols32 = sb("cols32", [P, 32])
        sc_col = g.sc_col
        mod = sb("mod", [P, 16])
        g1 = sb("g1", [P, KD])
        ss = sb("ss", [P, NT])
        rstd = sb("rstd", [P, 2, NT])
        h32 = sb("h32", [P, 2, BANK])
        w_cast = sem("w_cast")
        small, x_in, ada_in = sem("small"), [sem(f"x_in{i}") for i in range(NT)], [sem(f"ada_in{k}") for k in range(KD)]
        s_in, w_in = sem("s_in"), sem("w_in")
        win = g.w_in[0].rearrange("(k p) n -> p k n", p=P)
        silu, squares, root, inv, scaled = sem("silu"), sem("squares"), sem("root"), sem("inv"), sem("scaled")
        mod_mm, mod_ok, g1_ok = sem("mod_mm"), sem("mod_ok"), sem("g1_ok")
        turned, h_ok, hi_ok, lo_ok = sem("turned"), sem("h_ok"), sem("hi_ok"), sem("lo_ok")
        col_mm, col_ok = sem("col_mm"), sem("col_ok")
        bank = lambda k: g.ps[:, k * BANK:(k + 1) * BANK]
        block = ctx.enter_context(nc.Block())

        @block.sync
        def _(sp):
            sp.dma_start(rows[0:16, :], g.b_ada[0, 0:2 * D].rearrange("(k p) -> k p", p=P)).then_inc(small, 16)
            sp.dma_start(rows[16:24, :], g.c[0].rearrange("(k p) -> k p", p=P)).then_inc(small, 16)
            sp.dma_start(rows[24:32, :], g.norm_g[0].rearrange("(k p) -> k p", p=P)).then_inc(small, 16)
            sp.dma_start(g.const[:], g.const_dram).then_inc(small, 16)
            for i in range(NT):
                sp.dma_start(x_sb[:, i, :], g.x[0, i * P:(i + 1) * P, :]).then_inc(x_in[i], 16)
            for at, c0, n in ((0, C_KI, 64), (64, C_KI, 64), (P, C_WI, 8), (P + 8, C_AA, 16)):
                sp.dma_start(g.s32[:, :, at:at + n], win[:, :, c0:c0 + n]).then_inc(s_in, 16)
            for u in range(2):
                sp.dma_start(g.w32[:, u], win[:, :, C_QI + u * UNIT:C_QI + (u + 1) * UNIT]).then_inc(w_in, 16)
            sp.wait_ge(w_in, 32)

        @block.scalar
        def _(act):
            for k in range(KD):
                act.dma_start(w_ada[:, k, :], g.w_ada[0, k * P:(k + 1) * P, 0:2 * D]).then_inc(ada_in[k], 16)
            act.wait_ge(col_ok, 1)
            nc.scalar.activation(sc_col[:], cols32[:, 16:24], ACT.Silu).then_inc(silu, 1)
            for i in range(NT):
                act.wait_ge(x_in[i], 16)
                if i:
                    act.wait_ge(squares, i)
                nc.scalar.activation(h32[:].rearrange("p s t -> p (s t)"), x_sb[:, i, :], ACT.Square, accum_out=ss[:, i:i + 1]).then_inc(squares, 1)
            act.wait_ge(inv, 1)
            nc.scalar.activation(rstd[:, 1, :], rstd[:, 0, :], ACT.Sqrt).then_inc(root, 1)
            act.wait_ge(g1_ok, 1)
            for n in range(KD * HALVES):
                k = n // HALVES
                act.wait_ge(turned, n + 1)
                if n >= 2:
                    act.wait_ge(lo_ok, n - 1)
                nc.scalar.activation(h32[:, n % 2, :], bank(n % 4), ACT.Identity, bias=mod[:, k:k + 1],
                                     scale=g1[:, k:k + 1]).then_inc(h_ok, 1)

        @block.vector
        def _(dve):
            dve.wait_ge(col_mm, 1)
            nc.vector.tensor_copy(cols32[:], g.ps[:, 7 * BANK:7 * BANK + 32]).then_inc(col_ok, 1)
            dve.wait_ge(squares, NT)
            nc.vector.tensor_scalar(rstd[:, 0, :], ss[:], 1.0 / D, EPS, ALU.mult, ALU.add).then_inc(inv, 1)
            dve.wait_ge(root, 1)
            nc.vector.reciprocal(ss[:], rstd[:, 1, :]).then_inc(inv, 1)
            dve.wait_ge(inv, 2)
            for i in range(NT):
                nc.vector.tensor_scalar(x_sb[:, i, :], x_sb[:, i, :], ss[:, i:i + 1], None, ALU.mult).then_inc(scaled, 1)
            dve.wait_ge(mod_mm, 1)
            nc.vector.tensor_tensor(mod[:], g.ps[:, 4 * BANK:4 * BANK + 16], cols32[:, 0:16], ALU.add).then_inc(mod_ok, 1)
            dve.wait_ge(mod_ok, 1)
            nc.vector.scalar_tensor_tensor(out=g1[:], in0=mod[:, KD:2 * KD], scalar=1.0, in1=cols32[:, 24:32],
                                           op0=ALU.add, op1=ALU.mult).then_inc(g1_ok, 1)
            for n in range(KD * HALVES):
                k, half = divmod(n, HALVES)
                dve.wait_ge(h_ok, n + 1)
                nc.vector.tensor_copy(g.h_hi[:, k, half * BANK:(half + 1) * BANK], h32[:, n % 2, :]).then_inc(hi_ok, 1)

        @block.gpsimd
        def _(pool):
            pool.wait_ge(s_in, 64)
            nc.gpsimd.tensor_copy(g.s_hi[:], g.s32[:]).then_inc(w_cast, 1)
            pool.wait_ge(w_cast, 1)
            nc.gpsimd.tensor_tensor(g.s_lo[:], g.s32[:], g.s_hi[:], ALU.subtract)
            for n in range(KD * HALVES):
                k, half = divmod(n, HALVES)
                cols = slice(half * BANK, (half + 1) * BANK)
                pool.wait_ge(hi_ok, n + 1)
                nc.gpsimd.tensor_tensor(g.h_lo[:, k, cols], h32[:, n % 2, :], g.h_hi[:, k, cols],
                                        ALU.subtract).then_inc(lo_ok, 1)

        @block.tensor
        def _(pe):
            pe.wait_ge(small, 64)
            nc.tensor.transpose(g.ps[:, 7 * BANK:7 * BANK + 32], rows[:], g.const[0:32, K_ID:K_ID + 32]).then_inc(col_mm, 1)
            pe.wait_ge(silu, 1)
            for k in range(KD):
                pe.wait_ge(ada_in[k], 16)
                for j in range(16):
                    last = nc.tensor.matmul(g.ps[:, 4 * BANK + j:4 * BANK + j + 1], w_ada[:, k, j * P:(j + 1) * P],
                                            sc_col[:, k:k + 1], start=(k == 0 and j == 0), stop=(k == KD - 1),
                                            skip_group_check=True)
            last.then_inc(mod_mm, 1)
            pe.wait_ge(scaled, NT)
            for n in range(KD * HALVES):
                k, half = divmod(n, HALVES)
                if n >= 4:
                    pe.wait_ge(h_ok, n - 3)
                for j in range(4):
                    last = nc.tensor.transpose(g.ps[:, (n % 4) * BANK + j * P:(n % 4) * BANK + (j + 1) * P],
                                               x_sb[:, half * 4 + j, k * P:(k + 1) * P], g.const[:, K_ID:K_ID + P])
                last.then_inc(turned, 1)


def phase_index(nc, g):
    with ExitStack() as ctx:
        sb = lambda n, s, d=F32: ctx.enter_context(nc.sbuf_tensor("b_" + n, s, d))
        sem = lambda n: nc.alloc_semaphore("b_" + n)
        s_hi, s_lo, w32, w_hi, w_lo = g.s_hi, g.s_lo, g.w32, g.w_hi, g.w_lo
        k_hi, k_lo = sb("k_hi", [P, 2, T], F16), sb("k_lo", [P, 2, T], F16)
        q_hi, q_lo = sb("q_hi", [P, 4, T], F16), sb("q_lo", [P, 4, T], F16)
        relu = sb("relu", [P, 4, T])
        w_in = [sem("w_in0"), sem("w_in1")]
        w_cast, w_ready = sem("w_cast"), sem("w_ready")
        proj, hi_ok, lo_ok, zero = sem("proj"), sem("hi_ok"), sem("lo_ok"), sem("zero")
        dots, relu_ok, acc, small_ok = sem("dots"), sem("relu_ok"), sem("acc"), sem("small_ok")
        bank = lambda k: g.ps[:, k * BANK:(k + 1) * BANK]
        win = g.w_in[0].rearrange("(k p) n -> p k n", p=P)
        block = ctx.enter_context(nc.Block())

        @block.sync
        def _(sp):
            for u in range(2):
                sp.wait_ge(w_ready, u + 1)
                sp.dma_start(w32[:, u], win[:, :, C_ZA + u * UNIT:C_ZA + (u + 1) * UNIT]).then_inc(w_in[u], 16)

        @block.gpsimd
        def _(pool):
            for n in range(4):
                u = n % 2
                if n >= 2:
                    pool.wait_ge(w_in[u], 16)
                    pool.wait_ge(proj, 3 + 4 * (u + 1))
                nc.gpsimd.tensor_copy(w_hi[:, u], w32[:, u]).then_inc(w_cast, 1)
                pool.wait_ge(w_cast, n + 1)
                nc.gpsimd.tensor_tensor(w_lo[:, u], w32[:, u], w_hi[:, u], ALU.subtract).then_inc(w_ready, 1)

        @block.tensor
        def _(pe):
            for half in range(HALVES):
                cols = slice(half * BANK, (half + 1) * BANK)
                for k in range(KD):
                    last = three(nc.tensor, bank(half), s_hi[:, k, 0:P], s_lo[:, k, 0:P],
                                 g.h_hi[:, k, cols], g.h_lo[:, k, cols], k == 0, k == KD - 1)
                last.then_inc(proj, 1)
            for i in range(NT):
                for k in range(KD):
                    last = three(nc.tensor, g.ps[:, 2 * BANK + i * 24:2 * BANK + (i + 1) * 24],
                                 g.h_hi[:, k, i * P:(i + 1) * P], g.h_lo[:, k, i * P:(i + 1) * P],
                                 s_hi[:, k, P:NS], s_lo[:, k, P:NS], k == 0, k == KD - 1)
            last.then_inc(proj, 1)
            pe.wait_ge(w_ready, 2)
            with pe.Fori(0, 2) as u:
                for b in range(2):
                    for half in range(HALVES):
                        cols = slice(half * BANK, (half + 1) * BANK)
                        n = 2 * b + half
                        pe.wait_ge(lo_ok, u * (5 + n) + 1)
                        for k in range(KD):
                            last = three(nc.tensor, bank(3 + n), w_hi[:, bass.ds(u, 1), k, b * P:(b + 1) * P],
                                         w_lo[:, bass.ds(u, 1), k, b * P:(b + 1) * P],
                                         g.h_hi[:, k, cols], g.h_lo[:, k, cols], k == 0, k == KD - 1)
                        last.then_inc(proj, 1)
            pe.wait_ge(lo_ok, 8 + 4 + 1)
            for i in range(NT):
                width = (i + 1) * P
                with pe.Fori(0, 2) as turn:
                    for e in range(4):
                        pe.wait_ge(relu_ok, turn * 4 + (8 * i - 2 + e) if i else turn * (1 + e) + 1)
                        rows = (bass.ds(turn * 2 + e // 2, 1), slice(i * P, (i + 1) * P))
                        for c0 in range(0, width, BANK):
                            c1 = min(width, c0 + BANK)
                            last = three(nc.tensor, g.ps[:, e * T + c0:e * T + c1],
                                         q_hi[:, rows[0], rows[1]], q_lo[:, rows[0], rows[1]],
                                         k_hi[:, e % 2, c0:c1], k_lo[:, e % 2, c0:c1], True, True)
                        last.then_inc(dots, 1)

        @block.scalar
        def _(act):
            act.nop().then_inc(relu_ok, 1)
            act.wait_ge(zero, 1)
            for half in range(HALVES):
                cols = slice(half * BANK, (half + 1) * BANK)
                act.wait_ge(proj, half + 1)
                nc.scalar.copy(k_hi[0:64, 0, cols], bank(half)[0:64])
                nc.scalar.copy(k_hi[64:128, 1, cols], bank(half)[64:128]).then_inc(hi_ok, 1)
            act.wait_ge(proj, 3)
            nc.scalar.copy(g.small[:], g.ps[:, 2 * BANK:2 * BANK + NT * 24].rearrange("p (i n) -> p i n", n=24)).then_inc(small_ok, 1)
            with act.Fori(0, 2) as u:
                for b in range(2):
                    for half in range(HALVES):
                        n = 2 * b + half
                        act.wait_ge(proj, u * 4 + 4 + n)
                        nc.scalar.copy(q_hi[:, bass.ds(u * 2 + b, 1), half * BANK:(half + 1) * BANK],
                                       bank(3 + n)).then_inc(hi_ok, 1)
            for i in range(NT):
                with act.Fori(0, 2) as turn:
                    for e in range(4):
                        act.wait_ge(dots, turn * 4 + 8 * i + 1 + e)
                        act.wait_ge(acc, turn * 4 + (9 * i - 2 + e) if i else turn * (1 + e) + 1)
                        nc.scalar.activation(relu[:, e, 0:(i + 1) * P], g.ps[:, e * T:e * T + (i + 1) * P],
                                             ACT.Relu).then_inc(relu_ok, 1)

        @block.vector
        def _(dve):
            dve.nop().then_inc(lo_ok, 1)
            dve.nop().then_inc(acc, 1)
            nc.vector.memset(k_hi[64:128, 0, :], 0.0)
            nc.vector.memset(k_hi[0:64, 1, :], 0.0)
            nc.vector.memset(k_lo[64:128, 0, :], 0.0)
            nc.vector.memset(k_lo[0:64, 1, :], 0.0)
            nc.vector.memset(g.score[:], 0.0).then_inc(zero, 1)
            for half in range(HALVES):
                cols = slice(half * BANK, (half + 1) * BANK)
                dve.wait_ge(hi_ok, half + 1)
                nc.vector.tensor_tensor(k_lo[0:64, 0, cols], bank(half)[0:64], k_hi[0:64, 0, cols], ALU.subtract).then_inc(lo_ok, 1)
                nc.vector.tensor_tensor(k_lo[64:128, 1, cols], bank(half)[64:128], k_hi[64:128, 1, cols], ALU.subtract).then_inc(lo_ok, 1)
            dve.wait_ge(small_ok, 1)
            nc.vector.tensor_scalar(g.small[:, :, 0:8], g.small[:, :, 0:8], H ** -0.5 * IDX_DIM ** -0.5, None,
                                    ALU.mult).then_inc(small_ok, 1)
            with dve.Fori(0, 2) as u:
                for b in range(2):
                    for half in range(HALVES):
                        n = 2 * b + half
                        cols = slice(half * BANK, (half + 1) * BANK)
                        dve.wait_ge(hi_ok, u * 4 + 3 + n)
                        nc.vector.tensor_tensor(q_lo[:, bass.ds(u * 2 + b, 1), cols], bank(3 + n),
                                                q_hi[:, bass.ds(u * 2 + b, 1), cols], ALU.subtract).then_inc(lo_ok, 1)
            dve.wait_ge(small_ok, 2)
            dve.wait_ge(zero, 1)
            for i in range(NT):
                at = g.score[:, g.first[i]:g.first[i + 1]]
                with dve.Fori(0, 2) as turn:
                    for e in range(4):
                        dve.wait_ge(relu_ok, turn * 4 + 8 * i + 2 + e)
                        dve.wait_ge(acc, turn * 4 + 9 * i + e + 1)
                        nc.vector.scalar_tensor_tensor(out=at, in0=relu[:, e, 0:(i + 1) * P],
                                                       scalar=g.small[:, i, bass.ds(turn * 4 + e, 1)], in1=at,
                                                       op0=ALU.mult, op1=ALU.add).then_inc(acc, 1)
                dve.wait_ge(acc, 9 * i + 8 + 1)
                diag = g.score[:, g.first[i] + i * P:g.first[i + 1]]
                nc.vector.tensor_tensor(diag, diag, g.const[:, K_CAUSAL:K_CAUSAL + P], ALU.add).then_inc(acc, 1)


def phase_topk(nc, g):
    with ExitStack() as ctx:
        sb = lambda n, s, d=F32: ctx.enter_context(nc.sbuf_tensor("c_" + n, s, d))
        sem = lambda n: nc.alloc_semaphore("c_" + n)
        w32, w_hi, w_lo = g.w32, g.w_hi, g.w_lo
        stage = sb("stage", [P, 8, BANK])
        best = sb("best", [P, 2, 8])
        w_in, w_cast, w_ready = [sem("w_in0"), sem("w_in1")], sem("w_cast"), sem("w_ready")
        proj, gated, stored = sem("proj"), sem("gated"), [sem(f"stored{n}") for n in range(8)]
        top_ok, rep_ok, masked, mask_out = sem("top_ok"), sem("rep_ok"), sem("masked"), sem("mask_out")
        alone, pool_alone = sem("alone"), sem("pool_alone")
        dt, al = sb("dt", [P, H]), sb("al", [P, H])
        y, neg, soft, big = sb("y", [P, NT, H]), sb("neg", [P, NT, H]), sb("soft", [P, NT, H]), sb("big", [P, NT, H])
        conv_rows = sb("conv_rows", [96, P])
        load, step_v, step_a, sums_mm, sums_ok = sem("load"), sem("step_v"), sem("step_a"), sem("sums_mm"), sem("sums_ok")
        everywhere = [P, NT, H]
        bank = lambda k: g.ps[:, k * BANK:(k + 1) * BANK]
        win = g.w_in[0].rearrange("(k p) n -> p k n", p=P)
        columns = [C_ZA + n * UNIT for n in range(4)] + [C_ZB + n * UNIT for n in range(4)] + [C_GL + n * UNIT for n in range(8)]
        block = ctx.enter_context(nc.Block())

        @block.sync
        def _(sp):
            sp.dma_start(dt[:], g.dt_bias[0].partition_broadcast(P)).then_inc(load, 16)
            sp.dma_start(al[:], g.a_log[0].partition_broadcast(P)).then_inc(load, 16)
            sp.dma_start(conv_rows[:], g.conv_w[0].rearrange("j (b p) -> (j b) p", p=P)).then_inc(load, 16)
            for u, c0 in list(enumerate(columns))[2:]:
                sp.wait_ge(w_ready, u - 1)
                sp.dma_start(w32[:, u % 2], win[:, :, c0:c0 + UNIT]).then_inc(w_in[u % 2], 16)
            sp.wait_ge(masked, NT)
            sp.dma_start(g.mask_dram, g.mask[:]).then_inc(mask_out, 16)
            sp.wait_ge(mask_out, 16)
            for n in range(8):
                sp.wait_ge(stored[n], 16 * 10 + 1)

        @block.gpsimd
        def _(pool):
            def split(s, arrived, free, n):
                pool.wait_ge(w_in[s], arrived).then_inc(pool_alone, 1)
                pool.wait_ge(proj, free).then_inc(pool_alone, 1)
                nc.gpsimd.tensor_copy(w_hi[:, s], w32[:, s]).then_inc(w_cast, 1)
                pool.wait_ge(w_cast, n + 1)
                nc.gpsimd.tensor_tensor(w_lo[:, s], w32[:, s], w_hi[:, s], ALU.subtract).then_inc(w_ready, 1)

            pool.nop().then_inc(w_cast, 2)
            pool.nop().then_inc(w_ready, 2)
            for s in range(2):
                split(s, 16, 16 + 8 * s, 2 + s)
            with pool.Fori(0, 6) as t:
                for s in range(2):
                    split(s, t * 16 + 32, t * 8 + 36 + 4 * s, t * 2 + 4 + s)

        @block.tensor
        def _(pe):
            pe.nop().then_inc(proj, 8)
            with pe.Fori(0, 2) as t:
                for s in range(2):
                    pe.wait_ge(w_ready, t * 2 + s + 1)
                    for i in range(NT):
                        pe.wait_ge(gated, t * 16 + s * 8 + i + 1)
                        for k in range(KD):
                            last = three(nc.tensor, g.ps[:, i * BANK:i * BANK + UNIT],
                                         g.h_hi[:, k, i * P:(i + 1) * P], g.h_lo[:, k, i * P:(i + 1) * P],
                                         w_hi[:, s, k], w_lo[:, s, k], k == 0, k == KD - 1)
                        last.then_inc(proj, 1)
            pe.wait_ge(gated, 40)
            pe.wait_ge(step_v, 4)
            for n, mask in enumerate((K_UPTO, K_AFTER, K_CH0, K_CH1)):
                last = nc.tensor.matmul(g.ps[:, n * NT * H:(n + 1) * NT * H], g.const[:, mask:mask + P],
                                        g.g[:].rearrange("p i h -> p (i h)"), start=True, stop=True)
            last.then_inc(sums_mm, 1)
            pe.wait_ge(load, 48)
            nc.tensor.transpose(g.ps[:, BANK:BANK + 96], conv_rows[:], g.const[0:96, K_ID:K_ID + 96]).then_inc(sums_mm, 1)
            pe.wait_ge(sums_ok, 1)
            with pe.Fori(0, 6) as t:
                for s in range(2):
                    pe.wait_ge(w_ready, t * 2 + 4 + s + 1)
                    for b in range(2):
                        for half in range(HALVES):
                            n = 4 * s + 2 * b + half
                            pe.wait_ge(gated, t * 8 + 33 + n)
                            cols = slice(half * BANK, (half + 1) * BANK)
                            for k in range(KD):
                                last = three(nc.tensor, bank(n), w_hi[:, s, k, b * P:(b + 1) * P], w_lo[:, s, k, b * P:(b + 1) * P],
                                             g.h_hi[:, k, cols], g.h_lo[:, k, cols], k == 0, k == KD - 1)
                            last.then_inc(proj, 1)

        @block.scalar
        def _(act):
            act.nop().then_inc(gated, 8)
            for i in range(8):
                act.nop().then_inc(stored[i], 1)
            act.wait_ge(load, 48)
            act.wait_ge(step_v, 1)
            nc.scalar.activation(big[:], y[:], ACT.Abs).then_inc(step_a, 1)
            act.wait_ge(step_a, 1)
            nc.scalar.activation(soft[:], big[:], ACT.Exp, scale=-1.0).then_inc(step_a, 1)
            nc.scalar.activation(al[:], al[:], ACT.Exp)
            act.wait_ge(step_a, 2)
            nc.scalar.activation(soft[:], soft[:], ACT.Ln, bias=1.0).then_inc(step_a, 1)
            nc.scalar.activation(g.beta[:], g.small[:, :, 16:24], ACT.Sigmoid).then_inc(step_a, 2)
            with act.Fori(0, 4) as u:
                for i in range(NT):
                    act.wait_ge(proj, u * 8 + 8 + i + 1)
                    act.wait_ge(stored[i], u * 16 + 1)
                    nc.scalar.activation(stage[:, i, 0:UNIT], g.ps[:, i * BANK:i * BANK + UNIT], ACT.Silu).then_inc(gated, 1)
                    act.wait_ge(gated, u * 8 + 8 + i + 1)
                    act.dma_start(g.z_dram[i * P:(i + 1) * P, bass.ds(u * UNIT, UNIT)], stage[:, i, 0:UNIT]).then_inc(stored[i], 16)
            act.wait_ge(sums_mm, 1)
            sums = g.ps[:, 0:4 * NT * H].rearrange("p (n i h) -> p n i h", n=4, h=H)
            nc.scalar.activation(g.decays[:], sums, ACT.Exp)
            act.wait_ge(sums_mm, 2)
            nc.scalar.copy(g.taps[:], g.ps[:, BANK:BANK + 96]).then_inc(sums_ok, 1)

            def gates(turns, function, before):
                with act.Fori(0, turns) as t:
                    for n in range(8):
                        channels, half = divmod(n, 2)
                        act.wait_ge(proj, t * 8 + 8 * before + 40 + n + 1)
                        act.wait_ge(stored[n], t * 16 + 16 * before + 64 + 1)
                        nc.scalar.activation(stage[:, n, :], bank(n), function).then_inc(gated, 1)
                        act.wait_ge(gated, t * 8 + 8 * before + 40 + n + 1)
                        act.dma_start(g.sig_dram[bass.ds(t * 4 * P + (before * 4 + channels) * P, P), half * BANK:(half + 1) * BANK],
                                      stage[:, n, :]).then_inc(stored[n], 16)

            gates(2, ACT.Silu, 0)
            gates(4, ACT.Sigmoid, 2)

        @block.vector
        def _(dve):
            dve.wait_ge(load, 48)
            nc.vector.tensor_tensor(y[:], g.small[:, :, 8:16], dt[:].unsqueeze(1).broadcast_to(everywhere), ALU.add).then_inc(step_v, 1)
            dve.wait_ge(step_v, 1)
            nc.vector.tensor_scalar(neg[:], y[:], 0.0, None, ALU.max).then_inc(step_v, 1)
            dve.wait_ge(step_a, 3)
            dve.wait_ge(step_v, 2)
            nc.vector.tensor_tensor(y[:], neg[:], soft[:], ALU.add).then_inc(step_v, 1)
            dve.wait_ge(step_v, 3)
            nc.vector.scalar_tensor_tensor(out=g.g[:], in0=y[:], scalar=-1.0, in1=al[:].unsqueeze(1).broadcast_to(everywhere),
                                           op0=ALU.mult, op1=ALU.mult).then_inc(step_v, 1)
            dve.wait_ge(step_a, 5)
            nc.vector.tensor_scalar(g.nbeta[:], g.beta[:], -1.0, None, ALU.mult)
            nc.vector.memset(g.eps[:], EPS)
            dve.nop().then_inc(rep_ok, 2)
            for n, pair in enumerate(((7, 2), (6, 3), (5, 4))):
                tiles = [g.score[:, g.first[i]:g.first[i + 1]] for i in pair]
                with dve.Fori(0, TOPK // 8) as r:
                    for e, s in enumerate(tiles):
                        dve.wait_ge(rep_ok, r * 2 + 64 * n + e + 1).then_inc(alone, 1)
                        nc.vector.max(best[:, e], s).then_inc(top_ok, 1)
                    for e, s in enumerate(tiles):
                        dve.wait_ge(top_ok, r * 2 + 64 * n + 1 + e).then_inc(alone, 1)
                        nc.vector.match_replace(s, best[:, e], s, TAKEN).then_inc(rep_ok, 1)
                dve.wait_ge(rep_ok, 64 * (n + 1) + 2)
            for i in range(NT):
                s = g.score[:, g.first[i]:g.first[i + 1]]
                m = g.mask[:, g.first[i]:g.first[i + 1]]
                if (i + 1) * P <= TOPK:
                    nc.vector.tensor_scalar(m, s, BELOW * 0.9, CLOSED, ALU.is_le, ALU.mult).then_inc(masked, 1)
                else:
                    nc.vector.tensor_scalar(m, s, TAKEN, CLOSED, ALU.not_equal, ALU.mult).then_inc(masked, 1)


GROUP = 4
LEVELS = 6


def phase_delta(nc, g):
    with ExitStack() as ctx:
        sb = lambda n, s, d=F32: ctx.enter_context(nc.sbuf_tensor("e_" + n, s, d))
        sem = lambda n: nc.alloc_semaphore("e_" + n)
        PAD = 4
        w32, w_hi, w_lo = sb("w32", [P, 3, KD, P]), sb("w_hi", [P, 3, KD, P], F16), sb("w_lo", [P, 3, KD, P], BF16)
        raw = sb("raw", [P, 2, PAD + T])
        y = sb("y", [P, 3, T])
        v_tok = sb("v_tok", [P, NT, P])
        k_dec = sb("k_dec", [P, NT, P])
        b1, b2 = sb("b1", [P, NT, P]), sb("b2", [P, NT, P])
        x = sb("x", [P, NT, P])
        gam = sb("gam", [P, NT, P])
        a_t = sb("a_t", [P, NT, P])
        m_t = sb("m_t", [P, 2, NT, P])
        g_col = sb("g_col", [P, NT])
        ones = sb("ones", [P, P])
        u_st, w_st, qg_st = sb("u_st", [P, GROUP, NT, P]), sb("w_st", [P, GROUP, T]), sb("qg_st", [P, GROUP, T])
        kd_st, at_st = sb("kd_st", [P, GROUP, NT, P]), sb("at_st", [P, GROUP, NT, P])
        s_st, v_new = sb("s_st", [P, GROUP, P]), sb("v_new", [P, GROUP, P])
        o_st = sb("o_st", [P, GROUP * P])
        each = dict(w_cast=3, w_ready=3, proj=6, raw_ok=6, conv=12, silu=3, sq=2, ssq=2, ln_ok=2, root=2, norm=2, gcol=1, glhs=1,
                    glhs_mm=1, gexp=1, gmask=1, beta_ok=1, decb=1, dexp=1, qg_ok=1, kk=1, qk=1, at=1, attn_ok=1, ktok=1, vtok=1,
                    ktok_r=1, vtok_r=1, mt=LEVELS, u0=1, m1=1, t_ok=10, u_ok=10, xm=10, x_ok=10, tx=10, uw=1, us_ok=1, ws_ok=1)
        s = {n: sem(n) for n in [*each, "alone", "pad", "wS", "qS", "o_mm", "kdv", "vn", "s_ok", "o_ok", "oss", "zero"]}

        def at(name, h, k):
            return s[name], h * each[name] + k + 1

        def start(engine, names):
            for n in names.split():
                engine.nop().then_inc(s[n], 1)

        w_in = [sem(f"w_in{n}") for n in range(3)]
        o_out = sem("o_out")
        bank = lambda k: g.ps[:, k * BANK:(k + 1) * BANK]
        pair = lambda k: g.ps[:, k * BANK:(k + 2) * BANK].rearrange("p (i n) -> p i n", n=P)
        tile_of = lambda k, i: g.ps[:, k * BANK + i * P:k * BANK + (i + 1) * P]
        win = g.w_in[0].rearrange("(k p) n -> p k n", p=P)
        upto = g.const[:, K_UPTO:K_UPTO + P]
        after = g.const[:, K_AFTER:K_AFTER + P]
        ident = g.const[:, K_ID:K_ID + P]
        full = [P, NT, P]
        over = lambda m: m.unsqueeze(1).broadcast_to(full)
        level = lambda l: over(g.const[:, K_LEVEL + l * P:K_LEVEL + (l + 1) * P])
        per = lambda t, h: t[:, :, bass.ds(h, 1)].broadcast_to(full)
        CHUNKS = T // CHUNK
        block = ctx.enter_context(nc.Block())

        @block.sync
        def _(sp):
            for h in range(H):
                for n in range(3):
                    if h:
                        sp.wait_ge(*at("w_ready", h - 1, n + 1))
                    c0 = (C_Q, C_K, C_V)[n] + h * P
                    sp.dma_start(w32[:, n], win[:, :, c0:c0 + P]).then_inc(w_in[n], 16)
            sp.wait_ge(o_out, 16 * NT * (H // GROUP))

        @block.gpsimd
        def _(pool):
            start(pool, "w_cast w_ready gcol glhs gmask beta_ok mt")

            def split(h, n):
                pool.wait_ge(w_in[n], h * 16 + 16).then_inc(s["alone"], 1)
                pool.wait_ge(*at("proj", h, 2 * n + 2 - each["proj"])).then_inc(s["alone"], 1)
                nc.gpsimd.tensor_copy(w_hi[:, n], w32[:, n]).then_inc(s["w_cast"], 1)
                pool.wait_ge(*at("w_cast", h, n + 1))
                nc.gpsimd.tensor_tensor(w_lo[:, n], w32[:, n], w_hi[:, n], ALU.subtract).then_inc(s["w_ready"], 1)

            def decays(h):
                pool.wait_ge(*at("decb", h, 0)).then_inc(s["alone"], 1)
                nc.gpsimd.tensor_copy(g_col[:], g.g[:, :, bass.ds(h, 1)].rearrange("p i o -> p (i o)")).then_inc(s["gcol"], 1)
                pool.wait_ge(*at("gcol", h, 1))
                pool.wait_ge(*at("xm", h, 8 - each["xm"]))
                nc.gpsimd.tensor_tensor(m_t[:, 0], over(after), g_col[:].unsqueeze(2).broadcast_to(full), ALU.mult).then_inc(s["glhs"], 1)
                pool.wait_ge(*at("gexp", h, 1))
                nc.gpsimd.tensor_tensor(gam[:], gam[:], over(upto), ALU.mult).then_inc(s["gmask"], 1)
                pool.wait_ge(*at("gmask", h, 1))
                pool.wait_ge(*at("mt", h, 0))
                nc.gpsimd.tensor_tensor(a_t[:], gam[:], per(g.beta, h), ALU.mult).then_inc(s["beta_ok"], 1)

            def head(h, front, more):
                for l in range(LEVELS):
                    if l == 0:
                        pool.wait_ge(*at("at", h, 1))
                        pool.wait_ge(*at("glhs_mm", h, 1))
                    elif l == 1:
                        pool.wait_ge(*at("qg_ok", h, 1))
                    elif l == 2:
                        pool.wait_ge(*at("u0", h, 1))
                        pool.wait_ge(*at("m1", h, 1))
                    else:
                        pool.wait_ge(*at("xm", h, 2 * (l - 2)))
                    nc.gpsimd.tensor_tensor(m_t[:, l % 2], a_t[:], level(l), ALU.mult).then_inc(s["mt"], 1)
                    if more and l >= 3:
                        split(h + 2, l - 3)
                if front:
                    decays(h + 1)

            for n in range(3):
                pool.wait_ge(w_in[n], 16)
                nc.gpsimd.tensor_copy(w_hi[:, n], w32[:, n]).then_inc(s["w_cast"], 1)
                pool.wait_ge(*at("w_cast", 0, n + 1))
                nc.gpsimd.tensor_tensor(w_lo[:, n], w32[:, n], w_hi[:, n], ALU.subtract).then_inc(s["w_ready"], 1)
            nc.gpsimd.tensor_copy(g_col[:], g.g[:, :, 0]).then_inc(s["gcol"], 1)
            pool.wait_ge(*at("gcol", 0, 1))
            nc.gpsimd.tensor_tensor(m_t[:, 0], over(after), g_col[:].unsqueeze(2).broadcast_to(full), ALU.mult).then_inc(s["glhs"], 1)
            for n in range(3):
                split(1, n)
            pool.wait_ge(*at("gexp", 0, 1))
            nc.gpsimd.tensor_tensor(gam[:], gam[:], over(upto), ALU.mult).then_inc(s["gmask"], 1)
            pool.wait_ge(*at("gmask", 0, 1))
            nc.gpsimd.tensor_tensor(a_t[:], gam[:], g.beta[:, :, 0:1].broadcast_to(full), ALU.mult).then_inc(s["beta_ok"], 1)
            with pool.Fori(0, H - 2) as h:
                head(h, True, True)
            head(H - 2, True, False)
            head(H - 1, False, False)

        @block.scalar
        def _(act):
            start(act, "raw_ok silu sq ln_ok root gexp dexp vtok_r x_ok ws_ok")
            squares = lambda n: (gam[:].rearrange("p i n -> p (i n)"), raw[:, 1, PAD:])[n]

            def project(h, n):
                for half in range(HALVES):
                    act.wait_ge(*at("proj", h, 2 * n + half + 1))
                    if half == 0:
                        act.wait_ge(*(at("conv", h, 0), at("norm", h, 0), at("conv", h, 4))[n])
                        act.wait_ge(s["pad"], 1)
                    nc.scalar.copy(raw[:, n % 2, PAD + half * BANK:PAD + (half + 1) * BANK], bank(half)).then_inc(s["raw_ok"], 1)

            def silu(h, n):
                act.wait_ge(*at("conv", h, 4 * n + 4))
                nc.scalar.activation(y[:, n], y[:, n], ACT.Silu).then_inc(s["silu"], 1)
                if n < 2:
                    act.wait_ge(*at("silu", h, n + 1))
                    act.wait_ge(*(at("attn_ok", h, 0), at("conv", h, 8))[n])
                    nc.scalar.activation(squares(n), y[:, n], ACT.Square).then_inc(s["sq"], 1)

            def roots(h):
                for n in range(2):
                    act.wait_ge(*at("ssq", h, n + 1))
                    nc.scalar.activation(squares(n), pair(0).rearrange("p i n -> p (i n)"), ACT.Ln, bias=g.eps[:]).then_inc(s["ln_ok"], 1)
                for n in range(2):
                    act.wait_ge(*at("ln_ok", h, n + 1))
                    nc.scalar.activation(squares(n), squares(n), ACT.Exp, scale=-0.5).then_inc(s["root"], 1)

            def gamma(h):
                act.wait_ge(*at("glhs_mm", h, 1))
                act.wait_ge(*at("norm", h, 1))
                nc.scalar.activation(gam[:], pair(4), ACT.Exp).then_inc(s["gexp"], 1)

            def head(h, hh, front):
                act.wait_ge(*at("decb", h, 1))
                act.wait_ge(*at("xm", h, 0))
                nc.scalar.activation(m_t[:, 1], pair(6), ACT.Exp).then_inc(s["dexp"], 1)
                act.wait_ge(*at("vtok", h, 1))
                act.wait_ge(*at("uw", h, 0))
                nc.scalar.copy(v_tok[:], pair(0)).then_inc(s["vtok_r"], 1)
                for l in range(1, LEVELS):
                    for half in range(2):
                        act.wait_ge(*at("xm", h, 2 * l - 1 + half))
                        if l > 1:
                            act.wait_ge(*at("tx", h, 2 * (l - 1) - 1 + half))
                        else:
                            act.wait_ge(*at("uw", h, 0))
                        nc.scalar.copy(x[:, 4 * half:4 * half + 4], bank(2 + half).rearrange("p (i n) -> p i n", n=P)).then_inc(s["x_ok"], 1)
                    if front:
                        if 2 <= l < 4:
                            silu(h + 1, l - 2)
                        if l < 4:
                            project(h + 1, l - 1)
                        elif l == 4:
                            roots(h + 1)
                        else:
                            gamma(h + 1)
                            silu(h + 1, 2)
                act.wait_ge(*at("uw", h, 1))
                nc.scalar.copy(w_st[:, bass.ds(hh, 1), :], pair(2).rearrange("p i n -> p (i n)").unsqueeze(1)).then_inc(s["ws_ok"], 1)

            def first():
                for n in range(3):
                    project(0, n)
                    if n:
                        silu(0, n - 1)
                silu(0, 2)
                roots(0)
                gamma(0)

            def outputs(group):
                for n in range(CHUNKS):
                    rows = slice((n % 2) * CHUNK, (n % 2 + 1) * CHUNK)
                    act.wait_ge(s["o_mm"], group * CHUNKS + n + 1)
                    i = n // 2
                    if n % 2 == 0 and (group or i):
                        act.wait_ge(o_out, 16 * (group * NT + i))
                    nc.scalar.copy(o_st[rows], g.ps[rows, 2 * BANK:3 * BANK]).then_inc(s["o_ok"], 1)
                    act.wait_ge(s["o_ok"], group * CHUNKS + n + 1)
                    for hh in range(GROUP):
                        done = (group * CHUNKS + n) * GROUP + hh
                        if done:
                            act.wait_ge(s["oss"], done)
                        h = group * GROUP + hh
                        nc.scalar.activation(x[rows, 0], o_st[rows, hh * P:(hh + 1) * P], ACT.Square,
                                             accum_out=g.oss[rows, i, h:h + 1]).then_inc(s["oss"], 1)
                    if n % 2:
                        act.wait_ge(s["o_ok"], group * CHUNKS + n + 1)
                        act.dma_start(g.o_dram[i * P:(i + 1) * P, group * GROUP * P:(group + 1) * GROUP * P], o_st[:]).then_inc(o_out, 16)
                act.wait_ge(s["oss"], (group + 1) * CHUNKS * GROUP)

            first()
            with act.Fori(0, GROUP) as h:
                head(h, h, True)
            outputs(0)
            with act.Fori(0, GROUP - 1) as hh:
                head(hh + GROUP, hh, True)
            head(H - 1, GROUP - 1, False)
            outputs(1)

        @block.vector
        def _(dve):
            nc.vector.memset(raw[:, :, 0:PAD], 0.0).then_inc(s["pad"], 1)
            nc.vector.memset(ones[:], 1.0).then_inc(s["pad"], 1)

            start(dve, "conv norm at qg_ok ktok_r u0 attn_ok t_ok u_ok us_ok")

            def convolve(h, n):
                for j in range(4):
                    tap = g.taps[:, bass.ds(h + 24 * j + 8 * n, 1)]
                    shifted = raw[:, n % 2, PAD - 3 + j:PAD - 3 + j + T]
                    if j == 0:
                        dve.wait_ge(*at("raw_ok", h, 2 * n + 2))
                        dve.wait_ge(*(at("qk", h, 0), at("qk", h, 0), at("vtok", h, 0))[n])
                        dve.wait_ge(*at("qg_ok", h, 0))
                        nc.vector.tensor_scalar(y[:, n], shifted, tap, None, ALU.mult).then_inc(s["conv"], 1)
                    else:
                        dve.wait_ge(*at("conv", h, 4 * n + j))
                        nc.vector.scalar_tensor_tensor(out=y[:, n], in0=shifted, scalar=tap, in1=y[:, n],
                                                       op0=ALU.mult, op1=ALU.add).then_inc(s["conv"], 1)

            def normalize(h, n):
                dve.wait_ge(*at("root", h, n + 1))
                nc.vector.scalar_tensor_tensor(out=y[:, n], in0=y[:, n], scalar=P ** -0.5 if n == 0 else 1.0,
                                               in1=(gam[:].rearrange("p i n -> p (i n)"), raw[:, 1, PAD:])[n],
                                               op0=ALU.mult, op1=ALU.mult).then_inc(s["norm"], 1)

            def head(h, hh, front):
                dve.wait_ge(*at("kk", h, 1))
                dve.wait_ge(*at("beta_ok", h, 1))
                nc.vector.tensor_tensor(a_t[:], pair(4), a_t[:], ALU.mult).then_inc(s["at"], 1)
                dve.wait_ge(*at("dexp", h, 1))
                nc.vector.tensor_tensor(qg_st[:, bass.ds(hh, 1)].rearrange("p o n -> p (o n)"), y[:, 0], m_t[:, 1].rearrange("p i n -> p (i n)"), ALU.mult).then_inc(s["qg_ok"], 1)
                dve.wait_ge(*at("ktok", h, 1))
                dve.wait_ge(*at("uw", h, 0))
                nc.vector.tensor_tensor(k_dec[:], pair(2), per(g.decays[:, 0], h), ALU.mult)
                nc.vector.tensor_tensor(kd_st[:, bass.ds(hh, 1)].rearrange("p o i n -> p (o i) n"), pair(2), per(g.decays[:, 1], h), ALU.mult).then_inc(s["ktok_r"], 1)
                dve.wait_ge(*at("mt", h, 1))
                nc.vector.tensor_tensor(b2[:], over(ident), m_t[:, 0], ALU.subtract).then_inc(s["u0"], 1)
                dve.wait_ge(*at("m1", h, 1))
                nc.vector.tensor_tensor(b1[:], over(ident), pair(0), ALU.subtract).then_inc(s["t_ok"], 2)
                dve.wait_ge(*at("qk", h, 1))
                nc.vector.tensor_tensor(at_st[:, bass.ds(hh, 1)].rearrange("p o i n -> p (o i) n"), pair(4), gam[:], ALU.mult).then_inc(s["attn_ok"], 1)
                for l in range(1, LEVELS):
                    for half in range(2):
                        t4 = slice(4 * half, 4 * half + 4)
                        part = lambda b, second: b[:, t4].rearrange("p i (c two w) -> p (i c) two w", two=2, w=1 << l)[:, :, second]
                        delta = lambda k: g.ps[:, k * BANK:k * BANK + BANK // 2].rearrange("p (c w) -> p c w", w=1 << l)
                        dve.wait_ge(*at("tx", h, 2 * l - 1 + half))
                        if l < LEVELS - 1:
                            dve.wait_ge(*at("t_ok", h, 2 * l if l == 1 else 2 * l - 1 + half))
                            nc.vector.tensor_tensor(part(b1, 0), part(b1, 0), delta(4 + half), ALU.subtract).then_inc(s["t_ok"], 1)
                        if l == 1:
                            dve.wait_ge(*at("u0", h, 1))
                        else:
                            dve.wait_ge(*at("u_ok", h, 2 * (l - 1) - 1 + half))
                        nc.vector.tensor_tensor(part(b2, 1), part(b2, 1), delta(6 + half), ALU.subtract).then_inc(s["u_ok"], 1)
                    if front:
                        if l < 4:
                            convolve(h + 1, l - 1)
                        elif l == 4:
                            normalize(h + 1, 0)
                            normalize(h + 1, 1)
                dve.wait_ge(*at("uw", h, 1))
                nc.vector.tensor_tensor(u_st[:, bass.ds(hh, 1)].rearrange("p o i n -> p (o i) n"), pair(0), per(g.beta, h), ALU.mult).then_inc(s["us_ok"], 1)

            def chunks(group):
                nc.vector.memset(s_st[:], 0.0).then_inc(s["zero"], 1)
                for n in range(CHUNKS):
                    i, c = divmod(n, 2)
                    rows = slice(c * CHUNK, (c + 1) * CHUNK)
                    done = (group * CHUNKS + n) * GROUP
                    for two in range(GROUP // 2):
                        dve.wait_ge(s["wS"], done // 2 + two + 1)
                        if done:
                            dve.wait_ge(s["kdv"], done // 2 - 1 + two)
                        for hh in (2 * two, 2 * two + 1):
                            h = group * GROUP + hh
                            nc.vector.scalar_tensor_tensor(
                                out=v_new[rows, hh], in0=g.ps[rows, two * BANK + hh * P:two * BANK + (hh + 1) * P],
                                scalar=g.nbeta[rows, i, h:h + 1], in1=u_st[rows, hh, i], op0=ALU.mult, op1=ALU.add).then_inc(s["vn"], 1)
                    for two in range(GROUP // 2):
                        dve.wait_ge(s["kdv"], done // 2 + two + 1)
                        if n:
                            dve.wait_ge(s["s_ok"], done - GROUP + 2 * two + 2)
                        else:
                            dve.wait_ge(s["zero"], group + 1)
                        for hh in (2 * two, 2 * two + 1):
                            h = group * GROUP + hh
                            nc.vector.scalar_tensor_tensor(
                                out=s_st[:, hh], in0=s_st[:, hh], scalar=g.decays[:, 2 + c, i, h:h + 1],
                                in1=tile_of(4 + two, hh), op0=ALU.mult, op1=ALU.add).then_inc(s["s_ok"], 1)

            for n in range(3):
                convolve(0, n)
            normalize(0, 0)
            normalize(0, 1)
            with dve.Fori(0, GROUP) as h:
                head(h, h, True)
            chunks(0)
            with dve.Fori(0, GROUP - 1) as hh:
                head(hh + GROUP, hh, True)
            head(H - 1, GROUP - 1, False)
            chunks(1)

        @block.tensor
        def _(pe):
            start(pe, "proj ssq glhs_mm decb kk qk ktok vtok m1 xm tx uw")
            mm = nc.tensor.matmul

            def project(h, n, half):
                if half == 0:
                    pe.wait_ge(*at("w_ready", h, n + 1))
                    if n == 0 and not (isinstance(h, int) and h == 0):
                        pe.wait_ge(*at("t_ok", h, 2 - each["t_ok"]))
                if n:
                    pe.wait_ge(*at("raw_ok", h, 2 * n + half - 1))
                cols = slice(half * BANK, (half + 1) * BANK)
                for k in range(KD):
                    last = three(nc.tensor, bank(half), w_hi[:, n, k], w_lo[:, n, k],
                                 g.h_hi[:, k, cols], g.h_lo[:, k, cols], k == 0, k == KD - 1)
                last.then_inc(s["proj"], 1)

            def sums(h, n):
                pe.wait_ge(*at("sq", h, n + 1))
                pe.wait_ge(*(at("raw_ok", h, 6), at("ln_ok", h, 1))[n])
                pe.wait_ge(s["pad"], 2)
                for half in range(HALVES):
                    src = (gam[:, 4 * half:4 * half + 4], raw[:, 1, PAD + half * BANK:PAD + (half + 1) * BANK])[n]
                    last = mm(bank(half), ones[:], src, start=True, stop=True)
                last.then_inc(s["ssq"], 1)

            def decays(h):
                pe.wait_ge(*at("glhs", h, 1))
                for i in range(NT):
                    last = mm(tile_of(4, i), m_t[:, 0, i], upto, start=True, stop=True)
                last.then_inc(s["glhs_mm"], 1)

            def between(h, slot):
                if slot < 6:
                    project(h, slot // 2, slot % 2)
                elif slot < 8:
                    sums(h, slot - 6)
                elif slot == 8:
                    pe.wait_ge(*at("t_ok", h, 0))
                    decays(h)

            def head(h, front):
                pe.wait_ge(*at("gcol", h, 1))
                pe.wait_ge(*at("u_ok", h, 0))
                for i in range(NT):
                    last = mm(tile_of(6, i), g_col[:, i:i + 1].broadcast_to([P, P]), upto, start=True, stop=True)
                last.then_inc(s["decb"], 1)
                pe.wait_ge(*at("norm", h, 2))
                pe.wait_ge(*at("gexp", h, 1))
                for i in range(NT):
                    tok = slice(i * P, (i + 1) * P)
                    last = mm(tile_of(4, i), y[:, 1, tok], y[:, 1, tok], start=True, stop=True)
                last.then_inc(s["kk"], 1)
                pe.wait_ge(*at("ws_ok", h, 0))
                for i in range(NT):
                    last = nc.tensor.transpose(tile_of(2, i), y[:, 1, i * P:(i + 1) * P], ident)
                last.then_inc(s["ktok"], 1)
                pe.wait_ge(*at("silu", h, 3))
                pe.wait_ge(*at("ln_ok", h, 2))
                pe.wait_ge(*at("us_ok", h, 0))
                for i in range(NT):
                    last = nc.tensor.transpose(tile_of(0, i), y[:, 2, i * P:(i + 1) * P], ident)
                last.then_inc(s["vtok"], 1)
                pe.wait_ge(*at("at", h, 1))
                for i in range(NT):
                    tok = slice(i * P, (i + 1) * P)
                    last = mm(tile_of(4, i), y[:, 1, tok], y[:, 0, tok], start=True, stop=True)
                last.then_inc(s["qk"], 1)
                pe.wait_ge(*at("mt", h, 1))
                pe.wait_ge(*at("vtok_r", h, 1))
                for i in range(NT):
                    last = nc.tensor.transpose(tile_of(0, i), m_t[:, 0, i], ident)
                last.then_inc(s["m1"], 1)
                for l in range(1, LEVELS):
                    pe.wait_ge(*at("mt", h, l + 1))
                    part = lambda b, i, second: b[:, i].rearrange("p (c two w) -> p c two w", two=2, w=1 << l)[:, :, second]
                    short = lambda k, i: g.ps[:, (k + i // 4) * BANK + i % 4 * CHUNK:(k + i // 4) * BANK + (i % 4 + 1) * CHUNK]
                    for half in range(2):
                        if l == 1:
                            pe.wait_ge(*at("t_ok", h, 2))
                            pe.wait_ge(*at("ktok_r", h, 1))
                        else:
                            pe.wait_ge(*at("t_ok", h, 2 * l - 1 + half))
                            pe.wait_ge(*at("x_ok", h, 2 * (l - 1) - 1 + half))
                        for i in range(4 * half, 4 * half + 4):
                            last = mm(tile_of(2, i), m_t[:, l % 2, i], b1[:, i], start=True, stop=True)
                        last.then_inc(s["xm"], 1)
                    if front:
                        between(h + 1, 2 * l - 2)
                    for half in range(2):
                        tiles = range(4 * half, 4 * half + 4)
                        pe.wait_ge(*at("x_ok", h, 2 * l - 1 + half))
                        if l == 1:
                            pe.wait_ge(*at("u0", h, 1))
                            pe.wait_ge(*at("attn_ok", h, 1))
                            pe.wait_ge(*at("dexp", h, 1))
                        else:
                            pe.wait_ge(*at("u_ok", h, 2 * (l - 1) - 1 + half))
                        if l < LEVELS - 1:
                            for i in tiles:
                                mm(short(4, i), b2[:, i], part(x, i, 0), start=True, stop=True)
                        for i in tiles:
                            last = mm(short(6, i), x[:, i], part(b2, i, 1), start=True, stop=True)
                        last.then_inc(s["tx"], 1)
                    if front:
                        between(h + 1, 2 * l - 1)
                pe.wait_ge(*at("u_ok", h, 10))
                if front:
                    pe.wait_ge(*at("ln_ok", h + 1, 2))
                for i in range(NT):
                    mm(tile_of(0, i), b2[:, i], v_tok[:, i], start=True, stop=True)
                for i in range(NT):
                    last = mm(tile_of(2, i), k_dec[:, i], b2[:, i], start=True, stop=True)
                last.then_inc(s["uw"], 1)

            def chunks(group):
                pe.wait_ge(*at("us_ok", GROUP * (group + 1), 0))
                pe.wait_ge(*at("ws_ok", GROUP * (group + 1), 0))
                if group + 1 < H // GROUP:
                    pe.wait_ge(*at("gexp", GROUP * (group + 1), 1))
                pe.wait_ge(s["zero"], group + 1)
                for n in range(CHUNKS):
                    i, c = divmod(n, 2)
                    rows = slice(c * CHUNK, (c + 1) * CHUNK)
                    tok = slice(n * CHUNK, (n + 1) * CHUNK)
                    done = (group * CHUNKS + n) * GROUP
                    if n >= 2 or group:
                        pe.wait_ge(s["o_ok"], group * CHUNKS + n - 1)
                    outs = g.ps[rows, 2 * BANK:3 * BANK]
                    for two in range(GROUP // 2):
                        both = (2 * two, 2 * two + 1)
                        for hh in both:
                            if n:
                                pe.wait_ge(s["s_ok"], done - GROUP + hh + 1)
                            last = mm(g.ps[rows, two * BANK + hh * P:two * BANK + (hh + 1) * P], w_st[:, hh, tok], s_st[:, hh],
                                      start=True, stop=True)
                        last.then_inc(s["wS"], 1)
                        for hh in both:
                            mm(outs[:, hh * P:(hh + 1) * P], qg_st[:, hh, tok], s_st[:, hh],
                               start=(hh == 0), stop=False, skip_group_check=True)
                    for two in range(GROUP // 2):
                        for hh in (2 * two, 2 * two + 1):
                            pe.wait_ge(s["vn"], done + hh + 1)
                            last = mm(outs[:, hh * P:(hh + 1) * P], at_st[rows, hh, i, rows], v_new[rows, hh],
                                      start=False, stop=True, skip_group_check=True)
                            if hh == GROUP - 1:
                                last.then_inc(s["o_mm"], 1)
                            last = mm(tile_of(4 + two, hh), kd_st[rows, hh, i], v_new[rows, hh], start=True, stop=True)
                        last.then_inc(s["kdv"], 1)
                pe.wait_ge(s["o_ok"], CHUNKS * (group + 1))
                pe.wait_ge(s["s_ok"], CHUNKS * GROUP * (group + 1))

            for slot in range(8):
                between(0, slot)
            decays(0)
            with pe.Fori(0, GROUP) as h:
                head(h, True)
            chunks(0)
            with pe.Fori(0, GROUP - 1) as hh:
                head(hh + GROUP, True)
            head(H - 1, False)
            chunks(1)


SHRINK = 1.0 / 16


def project_blocks(nc, pe, g, w_hi, w_lo, x_hi, x_lo, w_ready, proj, free, x_in=()):
    with pe.Fori(0, 2) as t:
        for s in range(2):
            pe.wait_ge(w_ready, t * 2 + s + 1)
            for b in range(2):
                for half in range(HALVES):
                    n = 4 * s + 2 * b + half
                    if x_in:
                        pe.wait_ge(x_in[half], 32)
                    pe.wait_ge(free, t * 8 + n + 1)
                    cols = slice(half * BANK, (half + 1) * BANK)
                    for k in range(KD):
                        last = three(nc.tensor, g.ps[:, n * BANK:(n + 1) * BANK],
                                     w_hi[:, s, k, b * P:(b + 1) * P], w_lo[:, s, k, b * P:(b + 1) * P],
                                     x_hi[:, k, cols], x_lo[:, k, cols], k == 0, k == KD - 1)
                    last.then_inc(proj, 1)


def split_block(nc, pool, w32, w_hi, w_lo, s, cast, n):
    nc.gpsimd.tensor_copy(w_hi[:, s], w32[:, s]).then_inc(cast, 1)
    pool.wait_ge(cast, n + 1)
    return nc.gpsimd.tensor_tensor(w_lo[:, s], w32[:, s], w_hi[:, s], ALU.subtract)


def phase_delta_out(nc, g):
    with ExitStack() as ctx:
        sb = lambda n, s, d=F32: ctx.enter_context(nc.sbuf_tensor("f_" + n, s, d))
        sem = lambda n: nc.alloc_semaphore("f_" + n)
        w32, w_hi, w_lo = g.w32, g.w_hi, g.w_lo
        o, z = sb("o", [P, NT, D]), sb("z", [P, 2, D])
        w_gate, b_gate = sb("w_gate", [P, KD, D]), sb("b_gate", [1, D])
        wg_in, bg_in, gate_mm, gate_sum, gate_out = sem("wg_in"), sem("bg_in"), sem("gate_mm"), sem("gate_sum"), sem("gate_out")
        gn, gn_s = sb("gn", [P, 1]), sb("gn_s", [P, 1])
        mean_sq, rstd = sb("mean_sq", [P, NT, H]), sb("rstd", [P, NT, H])
        a_hi, a_lo = sb("a_hi", [P, H, T], F16), sb("a_lo", [P, H, T], F16)
        ga, m1 = sb("ga", [P, 4, BANK]), sb("m1", [P, 4, BANK])
        w_in, w_cast, w_ready = [sem("w_in0"), sem("w_in1")], sem("w_cast"), sem("w_ready")
        o_in, z_in, gn_in = [sem(f"o_in{i}") for i in range(NT)], [sem(f"z_in{i}") for i in range(2)], sem("gn_in")
        mean, root, inv, scaled = sem("mean"), sem("root"), sem("inv"), sem("scaled")
        gated, turned, hi_ok, lo_ok = sem("gated"), sem("turned"), sem("hi_ok"), sem("lo_ok")
        proj, free = sem("proj"), sem("free")
        ga_in, m_out = [sem(f"ga_in{i}") for i in range(4)], [sem(f"m_out{i}") for i in range(4)]
        wo = g.w_o_gdn[0].rearrange("(k p) n -> p k n", p=P)
        win = g.w_in[0].rearrange("(k p) n -> p k n", p=P)
        block = ctx.enter_context(nc.Block())

        def low(dve, i):
            dve.wait_ge(hi_ok, i + 1)
            cols = slice(i * P, (i + 1) * P)
            nc.vector.scalar_tensor_tensor(out=a_lo[:, :, cols], in0=g.ps[:, (i % 2) * T:(i % 2 + 1) * T].rearrange("p (h t) -> p h t", t=P),
                                           scalar=gn_s[:], in1=a_hi[:, :, cols], op0=ALU.mult, op1=ALU.subtract).then_inc(lo_ok, 1)

        def product(n):
            return g.m_dram[(n // 2) * P:(n // 2 + 1) * P, (n % 2) * BANK:(n % 2 + 1) * BANK]

        @block.sync
        def _(sp):
            sp.dma_start(gn[:], g.gdn_norm_g[0].rearrange("(p o) -> p o", o=1)).then_inc(gn_in, 16)
            sp.dma_start(w32[:, 0], wo[:, :, 0:UNIT]).then_inc(w_in[0], 16)
            sp.dma_start(b_gate[:], g.b_ada[0:1, 2 * D:3 * D]).then_inc(bg_in, 16)
            for i in range(NT):
                sp.dma_start(o[:, i], g.o_dram[i * P:(i + 1) * P, :]).then_inc(o_in[i], 16)
                if i == 2:
                    sp.dma_start(w32[:, 1], wo[:, :, UNIT:2 * UNIT]).then_inc(w_in[1], 16)
                if i >= 2:
                    sp.wait_ge(gated, H * (i - 1))
                sp.dma_start(z[:, i % 2], g.z_dram[i * P:(i + 1) * P, :]).then_inc(z_in[i % 2], 16)
            sp.dma_start(w_gate[:], g.w_ada[0, :, 2 * D:3 * D].rearrange("(k p) n -> p k n", p=P)).then_inc(wg_in, 16)
            for n in range(16):
                if n in (0, 1, 8, 12):
                    u = (0, 1, 8, 12).index(n) + 2
                    sp.wait_ge(w_ready, u - 1)
                    src = wo[:, :, u * UNIT:(u + 1) * UNIT] if u < 4 else win[:, :, (C_CKV, C_QB)[u - 4]:(C_CKV, C_QB)[u - 4] + UNIT]
                    sp.dma_start(w32[:, u % 2], src).then_inc(w_in[u % 2], 16)
                if n >= 4:
                    sp.wait_ge(free, 8 + n - 3)
                    sp.dma_start(product(n - 4), m1[:, n % 4]).then_inc(m_out[n % 4], 16)
                sp.dma_start(ga[:, n % 4], g.sig_dram[D + (n // 2) * P:D + (n // 2 + 1) * P, (n % 2) * BANK:(n % 2 + 1) * BANK]).then_inc(ga_in[n % 4], 16)
            for n in range(12, 16):
                sp.wait_ge(free, 8 + n + 1)
                sp.dma_start(product(n), m1[:, n % 4]).then_inc(m_out[n % 4], 16)
            sp.wait_ge(w_in[1], 48)
            sp.wait_ge(gate_sum, HALVES)
            sp.dma_start(g.gate_dram, b_gate[:]).then_inc(gate_out, 16)
            sp.wait_ge(gate_out, 16)
            for n in range(4):
                sp.wait_ge(m_out[n], 16 * 4 + 1)

        @block.gpsimd
        def _(pool):
            for u in range(5):
                pool.wait_ge(w_in[u % 2], 16 * (u // 2 + 1))
                if u >= 2:
                    pool.wait_ge(proj, 4 * (u - 1))
                split_block(nc, pool, w32, w_hi, w_lo, u % 2, w_cast, u).then_inc(w_ready, 1)

        @block.scalar
        def _(act):
            act.wait_ge(mean, 1)
            nc.scalar.activation(rstd[:], mean_sq[:], ACT.Sqrt).then_inc(root, 1)
            act.wait_ge(scaled, 1)
            for i in range(NT):
                act.wait_ge(turned, i + 1)
                nc.scalar.activation(a_hi[:, :, i * P:(i + 1) * P], g.ps[:, (i % 2) * T:(i % 2 + 1) * T].rearrange("p (h t) -> p h t", t=P),
                                     ACT.Copy, scale=gn_s[:]).then_inc(hi_ok, 1)

        @block.vector
        def _(dve):
            nc.vector.tensor_scalar(mean_sq[:], g.oss[:], 1.0 / P, EPS, ALU.mult, ALU.add).then_inc(mean, 1)
            dve.wait_ge(gn_in, 16)
            nc.vector.tensor_scalar(gn_s[:], gn[:], SHRINK, None, ALU.mult).then_inc(scaled, 1)
            dve.wait_ge(root, 1)
            nc.vector.reciprocal(rstd[:], rstd[:]).then_inc(inv, 1)
            dve.wait_ge(inv, 1)
            dve.wait_ge(scaled, 1)
            for i in range(NT):
                dve.wait_ge(o_in[i], 16)
                dve.wait_ge(z_in[i % 2], 16 * (i // 2 + 1))
                for h in range(H):
                    head = slice(h * P, (h + 1) * P)
                    nc.vector.scalar_tensor_tensor(out=o[:, i, head], in0=o[:, i, head], scalar=rstd[:, i, h:h + 1],
                                                   in1=z[:, i % 2, head], op0=ALU.mult, op1=ALU.mult).then_inc(gated, 1)
                if i:
                    low(dve, i - 1)
            low(dve, NT - 1)
            dve.nop().then_inc(free, 8)
            for n in range(4):
                dve.nop().then_inc(m_out[n], 1)
            with dve.Fori(0, 2) as t:
                for n in range(8):
                    dve.wait_ge(proj, t * 8 + n + 1)
                    dve.wait_ge(ga_in[n % 4], t * 32 + 16 * (n // 4 + 1))
                    dve.wait_ge(m_out[n % 4], t * 32 + 16 * (n // 4) + 1)
                    nc.vector.scalar_tensor_tensor(out=m1[:, n % 4], in0=g.ps[:, n * BANK:(n + 1) * BANK], scalar=1.0 / SHRINK,
                                                   in1=ga[:, n % 4], op0=ALU.mult, op1=ALU.mult).then_inc(free, 1)
            dve.wait_ge(gate_mm, 1)
            dve.wait_ge(bg_in, 16)
            for half in range(HALVES):
                cols = slice(half * BANK, (half + 1) * BANK)
                nc.vector.tensor_tensor(b_gate[:, cols], g.ps[0:1, cols], b_gate[:, cols], ALU.add).then_inc(gate_sum, 1)

        @block.tensor
        def _(pe):
            for i in range(NT):
                pe.wait_ge(gated, H * (i + 1))
                if i >= 2:
                    pe.wait_ge(lo_ok, i - 1)
                for h in range(H):
                    last = nc.tensor.transpose(g.ps[:, (i % 2) * T + h * P:(i % 2) * T + (h + 1) * P], o[:, i, h * P:(h + 1) * P],
                                               g.const[:, K_ID:K_ID + P])
                last.then_inc(turned, 1)
            pe.wait_ge(lo_ok, NT)
            project_blocks(nc, pe, g, w_hi, w_lo, a_hi, a_lo, w_ready, proj, free)
            pe.wait_ge(wg_in, 16)
            pe.wait_ge(free, 8 + 16 - 6)
            for half in range(HALVES):
                for k in range(KD):
                    last = nc.tensor.matmul(g.ps[0:1, half * BANK:(half + 1) * BANK], g.sc_col[:, k:k + 1],
                                            w_gate[:, k, half * BANK:(half + 1) * BANK], start=(k == 0), stop=(k == KD - 1))
            last.then_inc(gate_mm, 1)


def phase_merge(nc, g):
    with ExitStack() as ctx:
        sb = lambda n, s, d=F32: ctx.enter_context(nc.sbuf_tensor("i_" + n, s, d))
        sem = lambda n: nc.alloc_semaphore("i_" + n)
        w32, w_hi, w_lo = g.w32, g.w_hi, g.w_lo
        v_hi, v_lo = sb("v_hi", [P, KD, D], F16), sb("v_lo", [P, KD, D], BF16)
        b_hi, b_lo = sb("b_hi", [P, H, T], F16), sb("b_lo", [P, H, T], F16)
        m_hi, m_lo = sb("m_hi", [P, KD, T], F16), sb("m_lo", [P, KD, T], F16)
        gb, m1 = sb("gb", [P, 4, BANK]), sb("m1", [P, 4, BANK])
        x, y = sb("x", [P, 2, D]), sb("y", [P, 2, D])
        fg, gate = sb("fg", [P, D]), sb("gate", [P, D])
        ss = sb("ss", [P, 4])
        w_in, w_cast, w_ready = [sem("w_in0"), sem("w_in1")], sem("w_cast"), sem("w_ready")
        b_in, fg_in, proj, free = [sem("b_in0"), sem("b_in1")], sem("fg_in"), sem("proj"), sem("free")
        gb_in, m_in = [sem(f"gb_in{i}") for i in range(4)], [sem(f"m_in{i}") for i in range(4)]
        split_ok = sem("split_ok")
        summed, hi_ok, lo_ok = sem("summed"), sem("hi_ok"), sem("lo_ok")
        out_mm, gate_ok, res, sq_ok, mean, root, inv, done = (sem(n) for n in "out_mm gate_ok res sq_ok mean root inv done".split())
        x_in, y_out = [sem("x_in0"), sem("x_in1")], [sem("y_out0"), sem("y_out1")]
        wo, wv = g.w_o_dsa[0].rearrange("(k p) n -> p k n", p=P), g.w_out[0].rearrange("(k p) n -> p k n", p=P)
        order = [("v", 0), ("v", 1), ("o", 2), ("v", 2), ("o", 3), ("v", 3)]
        block = ctx.enter_context(nc.Block())

        @block.sync
        def _(sp):
            def load(j):
                which, u = order[j]
                sp.dma_start(w32[:, j % 2], (wo if which == "o" else wv)[:, :, u * UNIT:(u + 1) * UNIT]).then_inc(w_in[j % 2], 16)

            for half in range(HALVES):
                cols = slice(half * BANK, (half + 1) * BANK)
                for part, of in ((b_hi, g.bhi_dram), (b_lo, g.blo_dram)):
                    sp.dma_start(part[:, :, cols], of.rearrange("(h p) t -> p h t", p=P)[:, :, cols]).then_inc(b_in[half], 16)
            load(0)
            load(1)
            for i in range(2):
                sp.dma_start(x[:, i], g.x[0, i * P:(i + 1) * P, :]).then_inc(x_in[i], 16)
            sp.dma_start(fg[:], g.final_g.partition_broadcast(P)).then_inc(fg_in, 16)
            sp.dma_start(gate[:], g.gate_dram[0].partition_broadcast(P)).then_inc(fg_in, 16)
            for n in range(16):
                if n >= 4:
                    sp.wait_ge(summed, n - 3)
                at = (slice((n // 2) * P, (n // 2 + 1) * P), slice((n % 2) * BANK, (n % 2 + 1) * BANK))
                sp.dma_start(gb[:, n % 4], g.sig_dram[2 * D + (n // 2) * P:2 * D + (n // 2 + 1) * P, at[1]]).then_inc(gb_in[n % 4], 16)
                if n >= 4:
                    sp.wait_ge(hi_ok, n - 3)
                    sp.wait_ge(lo_ok, n - 3)
                sp.dma_start(m1[:, n % 4], g.m_dram[at[0], at[1]]).then_inc(m_in[n % 4], 16)
                if n in (1, 3, 5, 7):
                    j = 2 + n // 2
                    sp.wait_ge(split_ok, j - 1)
                    load(j)
            for i in range(NT):
                sp.wait_ge(done, i + 1)
                sp.dma_start(g.out[0, i * P:(i + 1) * P, :], y[:, i % 2]).then_inc(y_out[i % 2], 16)
                if i + 2 < NT:
                    sp.dma_start(x[:, i % 2], g.x[0, (i + 2) * P:(i + 3) * P, :]).then_inc(x_in[i % 2], 16)
            for n in range(2):
                sp.wait_ge(y_out[n], 16 * NT // 2)

        @block.gpsimd
        def _(pool):
            pool.nop().then_inc(w_ready, 2)
            for j, (which, u) in enumerate(order):
                pool.wait_ge(w_in[j % 2], 16 * (j // 2 + 1))
                if which == "o":
                    pool.wait_ge(proj, 4 * (u - 1))
                    hi, lo = w_hi[:, u % 2], w_lo[:, u % 2]
                else:
                    hi, lo = v_hi[:, :, u * UNIT:(u + 1) * UNIT], v_lo[:, :, u * UNIT:(u + 1) * UNIT]
                nc.gpsimd.tensor_copy(hi, w32[:, j % 2]).then_inc(w_cast, 1)
                pool.wait_ge(w_cast, j + 1)
                nc.gpsimd.tensor_tensor(lo, w32[:, j % 2], hi, ALU.subtract).then_inc(split_ok, 1)
                pool.wait_ge(split_ok, j + 1)
                if which == "o":
                    pool.nop().then_inc(w_ready, 1)

        @block.tensor
        def _(pe):
            project_blocks(nc, pe, g, w_hi, w_lo, b_hi, b_lo, w_ready, proj, free, b_in)
            pe.wait_ge(split_ok, 6)
            pe.wait_ge(lo_ok, 16)
            with pe.Fori(0, NT // 2) as t:
                for e in range(2):
                    pe.wait_ge(gate_ok, t * 4 + 2 * e + 2)
                    for half in range(HALVES):
                        for k in range(KD):
                            tok = bass.ds((t * 2 + e) * P, P)
                            last = three(nc.tensor, g.ps[:, (2 * e + half) * BANK:(2 * e + half + 1) * BANK], m_hi[:, k, tok], m_lo[:, k, tok],
                                         v_hi[:, k, half * BANK:(half + 1) * BANK], v_lo[:, k, half * BANK:(half + 1) * BANK], k == 0, k == KD - 1)
                    last.then_inc(out_mm, 1)

        @block.scalar
        def _(act):
            with act.Fori(0, 2) as t:
                for n in range(8):
                    b, half = divmod(n, 2)
                    act.wait_ge(summed, t * 8 + n + 1)
                    nc.scalar.mul(m_hi[:, bass.ds(t * 4 + b, 1), half * BANK:(half + 1) * BANK], m1[:, n % 4].unsqueeze(1), SHRINK).then_inc(hi_ok, 1)
            for i in range(NT):
                act.wait_ge(res, i + 1)
                if i >= 2:
                    act.wait_ge(y_out[i % 2], 16 * (i // 2))
                nc.scalar.activation(y[:, i % 2], x[:, i % 2], ACT.Square, accum_out=ss[:, 2 * (i % 2):2 * (i % 2) + 1]).then_inc(sq_ok, 1)
                act.wait_ge(mean, i + 1)
                nc.scalar.activation(ss[:, 2 * (i % 2) + 1:2 * (i % 2) + 2], ss[:, 2 * (i % 2) + 1:2 * (i % 2) + 2], ACT.Sqrt).then_inc(root, 1)

        @block.vector
        def _(dve):
            dve.nop().then_inc(free, 8)
            with dve.Fori(0, 2) as t:
                for n in range(8):
                    b, half = divmod(n, 2)
                    dve.wait_ge(proj, t * 8 + n + 1)
                    dve.wait_ge(gb_in[n % 4], t * 32 + 16 * (n // 4 + 1))
                    nc.vector.tensor_tensor(gb[:, n % 4], g.ps[:, n * BANK:(n + 1) * BANK], gb[:, n % 4], ALU.mult).then_inc(free, 1)
                    dve.wait_ge(m_in[n % 4], t * 32 + 16 * (n // 4 + 1))
                    dve.wait_ge(free, t * 8 + 8 + n + 1)
                    nc.vector.tensor_tensor(m1[:, n % 4], m1[:, n % 4], gb[:, n % 4], ALU.add).then_inc(summed, 1)
                    dve.wait_ge(hi_ok, t * 8 + n + 1)
                    at = (slice(None), bass.ds(t * 4 + b, 1), slice(half * BANK, (half + 1) * BANK))
                    nc.vector.scalar_tensor_tensor(out=m_lo[at], in0=m1[:, n % 4].unsqueeze(1), scalar=SHRINK,
                                                   in1=m_hi[at], op0=ALU.mult, op1=ALU.subtract).then_inc(lo_ok, 1)
            dve.nop().then_inc(gate_ok, 4)
            dve.wait_ge(fg_in, 32)
            dve.wait_ge(lo_ok, 16)
            for i in range(NT):
                e = i % 2
                dve.wait_ge(out_mm, i + 1)
                if i >= 2:
                    dve.wait_ge(y_out[e], 16 * (i // 2))
                nc.vector.scalar_tensor_tensor(out=y[:, e], in0=g.ps[:, e * T:(e + 1) * T], scalar=1.0 / SHRINK, in1=gate[:],
                                               op0=ALU.mult, op1=ALU.mult).then_inc(gate_ok, 2)
                dve.wait_ge(x_in[e], 16 * (i // 2 + 1))
                dve.wait_ge(gate_ok, 4 + 2 * (i + 1))
                nc.vector.tensor_tensor(x[:, e], x[:, e], y[:, e], ALU.add).then_inc(res, 1)
                dve.wait_ge(sq_ok, i + 1)
                nc.vector.tensor_scalar(ss[:, 2 * e + 1:2 * e + 2], ss[:, 2 * e:2 * e + 1], 1.0 / D, EPS, ALU.mult, ALU.add).then_inc(mean, 1)
                dve.wait_ge(root, i + 1)
                nc.vector.reciprocal(ss[:, 2 * e:2 * e + 1], ss[:, 2 * e + 1:2 * e + 2]).then_inc(inv, 1)
                dve.wait_ge(inv, i + 1)
                nc.vector.scalar_tensor_tensor(out=y[:, e], in0=x[:, e], scalar=ss[:, 2 * e:2 * e + 1], in1=fg[:],
                                               op0=ALU.mult, op1=ALU.mult).then_inc(done, 1)


NEAR = 2 * P


def phase_attention(nc, g):
    with ExitStack() as ctx:
        sb = lambda n, s, d: ctx.enter_context(nc.sbuf_tensor("j_" + n, s, d))
        a = {}
        a["q_hi"], a["q_lo"] = sb("q_hi", [P, H, T], F16), sb("q_lo", [P, H, T], F16)
        a["c_hi"], a["c_lo"] = sb("c_hi", [P, NT, RANK], F16), sb("c_lo", [P, NT, RANK], F16)
        a["ct_hi"], a["ct_lo"] = sb("ct_hi", [P, 2, T], F16), sb("ct_lo", [P, 2, T], F16)
        a["uk_hi"], a["uk_lo"] = sb("uk_hi", [P, H, RANK], F16), sb("uk_lo", [P, H, RANK], BF16)
        a["uv_hi"], a["uv_lo"] = sb("uv_hi", [P, 2, D], F16), sb("uv_lo", [P, 2, D], BF16)
        a["bias_hi"], a["bias_lo"] = sb("bias_hi", [P, H, NEAR], F16), sb("bias_lo", [P, H, NEAR], F16)
        a["mask"] = sb("mask", [P, g.first[NT]], BF16)
        a["ident_b"], a["flip_h"] = sb("ident_b", [P, P], BF16), sb("flip_h", [P, P], F16)
        latents(nc, g, a)
        attend(nc, g, a)


def latents(nc, g, a):
    q_hi, q_lo, c_hi, c_lo, ct_hi, ct_lo = (a[n] for n in ("q_hi", "q_lo", "c_hi", "c_lo", "ct_hi", "ct_lo"))
    uk_hi, uk_lo, uv_hi, uv_lo, bias_hi, bias_lo = (a[n] for n in ("uk_hi", "uk_lo", "uv_hi", "uv_lo", "bias_hi", "bias_lo"))
    with ExitStack() as ctx:
        sb = lambda n, s, d=F32: ctx.enter_context(nc.sbuf_tensor("k_" + n, s, d))
        sem = lambda n: nc.alloc_semaphore("k_" + n)
        w32, w_hi, w_lo = g.w32, g.w_hi, g.w_lo
        uk32, uv32 = sb("uk32", [P, 2, D]), sb("uv32", [P, 2, D])
        kvg = sb("kvg", [P, RANK])
        onehot, rel, rows = sb("onehot", [NBUCKETS, K_BUCKETS]), sb("rel", [NBUCKETS, H]), sb("rows", [H, K_BUCKETS])
        rows2 = sb("rows2", [H, K_BUCKETS])
        bias32 = sb("bias32", [P, H, NEAR])
        c32, sq = sb("c32", [P, NT, RANK]), sb("sq", [P, NT, RANK])
        ss, r = sb("ss", [P, NT]), sb("r", [P, NT])
        w_in, w_cast, w_ready = [sem("w_in0"), sem("w_in1")], sem("w_cast"), sem("w_ready")
        (uk_in, uv_in, kv_in, mask_in, rel_in, rows_out, bias_in, raw, ss_ok, mean, root, inv, normed, proj, q_h, q_l,
         rows_mm, rows_ok, b_h, uk_mm, uk_h, uk_l, uv_h, ch, turned, ct_h, ct_l) = (sem(n) for n in (
             "uk_in uv_in kv_in mask_in rel_in rows_out bias_in raw ss_ok mean root inv normed proj q_h q_l rows_mm rows_ok "
             "b_h uk_mm uk_h uk_l uv_h ch turned ct_h ct_l").split())
        bank = lambda k: g.ps[:, k * BANK:(k + 1) * BANK]
        win = g.w_in[0].rearrange("(k p) n -> p k n", p=P)
        order = [C_CKV] + [C_QB + u * UNIT for u in range(4)]
        block = ctx.enter_context(nc.Block())

        @block.sync
        def _(sp):
            sp.dma_start(w32[:, 0], win[:, :, order[2]:order[2] + UNIT]).then_inc(w_in[0], 16)
            sp.dma_start(kvg[:], g.kv_norm_g[0].partition_broadcast(P)).then_inc(kv_in, 16)
            sp.dma_start(onehot[:], g.buckets_dram).then_inc(rel_in, 16)
            sp.dma_start(rel[:], g.rel_bias).then_inc(rel_in, 16)
            sp.dma_start(uk32[:], g.w_uk[0].rearrange("(q p) h d -> p q (h d)", p=P)).then_inc(uk_in, 16)
            sp.dma_start(uv32[:], g.w_uv[0].rearrange("(q p) h d -> p q (h d)", p=P)).then_inc(uv_in, 16)
            sp.dma_start(a["mask"][:], g.mask_dram).then_inc(mask_in, 16)
            sp.wait_ge(rows_ok, 2)
            sp.dma_start(g.rows_dram, rows2[:]).then_inc(rows_out, 16)
            sp.wait_ge(rows_out, 16)
            sp.dma_start(bias32[:], bass.AP(g.rows_dram.tensor, 0, [[1, P], [K_BUCKETS, H], [1, NEAR]])).then_inc(bias_in, 16)
            for u in range(3, 5):
                sp.wait_ge(w_ready, u - 1)
                sp.dma_start(w32[:, u % 2], win[:, :, order[u]:order[u] + UNIT]).then_inc(w_in[u % 2], 16)
            sp.wait_ge(mask_in, 16)

        @block.gpsimd
        def _(pool):
            pool.nop().then_inc(w_cast, 1)
            pool.nop().then_inc(w_ready, 1)
            for u in range(1, 5):
                if u >= 2:
                    pool.wait_ge(w_in[u % 2], 16 * (u // 2))
                if u == 2:
                    pool.wait_ge(raw, NT)
                elif u > 2:
                    pool.wait_ge(proj, 4 * (u - 2))
                split_block(nc, pool, w32, w_hi, w_lo, u % 2, w_cast, u).then_inc(w_ready, 1)
                if u == 1:
                    pool.wait_ge(uv_in, 16)
                    nc.gpsimd.tensor_copy(uv_hi[:], uv32[:]).then_inc(uv_h, 1)
                    pool.wait_ge(uv_h, 1)
                    nc.gpsimd.tensor_tensor(uv_lo[:], uv32[:], uv_hi[:], ALU.subtract)
                    pool.wait_ge(b_h, 1)
                    nc.gpsimd.tensor_tensor(bias_lo[:], bias32[:], bias_hi[:], ALU.subtract)
            pool.wait_ge(ch, 1)
            nc.gpsimd.tensor_tensor(c_lo[:], c32[:], c_hi[:], ALU.subtract)

        @block.tensor
        def _(pe):
            pe.wait_ge(w_ready, 1)
            for i in range(NT):
                for k in range(KD):
                    last = three(nc.tensor, g.ps[:, i * BANK:i * BANK + RANK], g.h_hi[:, k, i * P:(i + 1) * P], g.h_lo[:, k, i * P:(i + 1) * P],
                                 w_hi[:, 0, k], w_lo[:, 0, k], k == 0, k == KD - 1)
                last.then_inc(raw, 1)
            pe.wait_ge(rel_in, 32)
            pe.wait_ge(normed, 1)
            nc.tensor.matmul(g.ps[0:H, 0:K_BUCKETS], rel[:], onehot[:], start=True, stop=True).then_inc(rows_mm, 1)
            pe.wait_ge(uk_in, 16)
            for n in range(4):
                pe.wait_ge(normed, 2 * n + 3 if n < 3 else NT)
                for j in range(4):
                    h, q = 2 * n + j // 2, j % 2
                    last = nc.tensor.transpose(g.ps[:, (1 + n) * BANK + j * P:(1 + n) * BANK + (j + 1) * P], uk32[:, q, h * P:(h + 1) * P],
                                               g.const[:, K_ID:K_ID + P])
                last.then_inc(uk_mm, 1)
            pe.wait_ge(normed, NT)
            pe.wait_ge(rows_ok, 1)
            for u in range(4):
                pe.wait_ge(w_ready, u + 2)
                for b in range(2):
                    for half in range(HALVES):
                        n = 4 * u + 2 * b + half
                        if n >= 3:
                            pe.wait_ge(q_l, n - 2)
                        at = (0, 5, 6)[n % 3]
                        cols = slice(half * BANK, (half + 1) * BANK)
                        s = (u + 1) % 2
                        for k in range(KD):
                            last = three(nc.tensor, bank(at), w_hi[:, s, k, b * P:(b + 1) * P], w_lo[:, s, k, b * P:(b + 1) * P],
                                         g.h_hi[:, k, cols], g.h_lo[:, k, cols], k == 0, k == KD - 1)
                        last.then_inc(proj, 1)
            pe.wait_ge(normed, NT)
            pe.wait_ge(uk_l, 4)
            for n in range(4):
                q, half = divmod(n, HALVES)
                for j in range(4):
                    last = nc.tensor.transpose(g.ps[:, (1 + n) * BANK + j * P:(1 + n) * BANK + (j + 1) * P],
                                               c32[:, 4 * half + j, q * P:(q + 1) * P], g.const[:, K_ID:K_ID + P])
                last.then_inc(turned, 1)

        @block.scalar
        def _(act):
            for i in range(NT):
                act.wait_ge(raw, i + 1)
                nc.scalar.activation(sq[:, i], g.ps[:, i * BANK:i * BANK + RANK], ACT.Square, accum_out=ss[:, i:i + 1]).then_inc(ss_ok, 1)
            act.wait_ge(mean, 1)
            nc.scalar.activation(r[:], r[:], ACT.Sqrt).then_inc(root, 1)
            for n in range(4):
                act.wait_ge(uk_mm, n + 1)
                nc.scalar.copy(uk_hi[:, 2 * n:2 * n + 2], bank(1 + n).rearrange("p (h c) -> p h c", c=RANK)).then_inc(uk_h, 1)
            act.wait_ge(bias_in, 16)
            nc.scalar.copy(bias_hi[:], bias32[:]).then_inc(b_h, 1)
            for n in range(16):
                act.wait_ge(proj, n + 1)
                nc.scalar.copy(q_hi[:, n // 2, (n % 2) * BANK:(n % 2 + 1) * BANK], bank((0, 5, 6)[n % 3])).then_inc(q_h, 1)
                if n == 3:
                    act.wait_ge(normed, NT)
                    nc.scalar.copy(c_hi[:], c32[:]).then_inc(ch, 1)
            for n in range(4):
                act.wait_ge(turned, n + 1)
                nc.scalar.copy(ct_hi[:, n // 2, (n % 2) * BANK:(n % 2 + 1) * BANK], bank(1 + n)).then_inc(ct_h, 1)

        @block.vector
        def _(dve):
            nc.vector.tensor_copy(a["ident_b"][:], g.const[:, K_ID:K_ID + P])
            nc.vector.tensor_copy(a["flip_h"][:], g.const[:, K_FLIP:K_FLIP + P])
            dve.wait_ge(ss_ok, NT)
            nc.vector.tensor_scalar(r[:], ss[:], 1.0 / RANK, EPS, ALU.mult, ALU.add).then_inc(mean, 1)
            dve.wait_ge(root, 1)
            nc.vector.reciprocal(ss[:], r[:]).then_inc(inv, 1)
            dve.wait_ge(inv, 1)
            dve.wait_ge(kv_in, 16)
            for i in range(NT):
                nc.vector.scalar_tensor_tensor(out=c32[:, i], in0=g.ps[:, i * BANK:i * BANK + RANK], scalar=ss[:, i:i + 1],
                                               in1=kvg[:], op0=ALU.mult, op1=ALU.mult).then_inc(normed, 1)
            dve.wait_ge(rows_mm, 1)
            nc.vector.tensor_copy(rows[:], g.ps[0:H, 0:K_BUCKETS]).then_inc(rows_ok, 1)
            dve.wait_ge(rows_ok, 1)
            nc.vector.tensor_scalar(rows2[:], rows[:], rows[:, 0:1], None, ALU.subtract).then_inc(rows_ok, 1)
            for n in range(4):
                dve.wait_ge(uk_h, n + 1)
                nc.vector.tensor_tensor(uk_lo[:, 2 * n:2 * n + 2], bank(1 + n).rearrange("p (h c) -> p h c", c=RANK),
                                        uk_hi[:, 2 * n:2 * n + 2], ALU.subtract).then_inc(uk_l, 1)
            for n in range(16):
                dve.wait_ge(q_h, n + 1)
                at = (slice(None), n // 2, slice((n % 2) * BANK, (n % 2 + 1) * BANK))
                nc.vector.tensor_tensor(q_lo[at], bank((0, 5, 6)[n % 3]), q_hi[at], ALU.subtract).then_inc(q_l, 1)
            for n in range(4):
                dve.wait_ge(ct_h, n + 1)
                at = (slice(None), n // 2, slice((n % 2) * BANK, (n % 2 + 1) * BANK))
                nc.vector.tensor_tensor(ct_lo[at], bank(1 + n), ct_hi[at], ALU.subtract).then_inc(ct_l, 1)


def attend(nc, g, a):
    q_hi, q_lo, c_hi, c_lo, ct_hi, ct_lo = (a[n] for n in ("q_hi", "q_lo", "c_hi", "c_lo", "ct_hi", "ct_lo"))
    uk_hi, uk_lo, uv_hi, uv_lo, bias_hi, bias_lo = (a[n] for n in ("uk_hi", "uk_lo", "uv_hi", "uv_lo", "bias_hi", "bias_lo"))
    mask, ident_b, flip_h = a["mask"], a["ident_b"], a["flip_h"]
    with ExitStack() as ctx:
        sb = lambda n, s, d=F32: ctx.enter_context(nc.sbuf_tensor("l_" + n, s, d))
        sem = lambda n: nc.alloc_semaphore("l_" + n)
        lat_hi, lat_lo = sb("lat_hi", [P, 2, T], F16), sb("lat_lo", [P, 2, T], F16)
        p = sb("p", [P, 2, T])
        pt_hi, pt_lo = sb("pt_hi", [P, 2, NT, P], F16), sb("pt_lo", [P, 2, NT, P], F16)
        ol_hi, ol_lo = sb("ol_hi", [P, 2, 2, P], F16), sb("ol_lo", [P, 2, 2, P], F16)
        top, total, share = sb("top", [P, 2]), sb("total", [P, 2]), sb("share", [P, 2])
        z = sb("z", [P, 2, T])
        b32 = sb("b32", [P, 2, P])
        b_hi, b_lo = sb("b_hi", [P, 2, T], F16), sb("b_lo", [P, 2, T], F16)
        (lat, lat_h, lat_l, logit, top_ok, exp_ok, inv, shared, turned, pt_h, pt_l, pv, ol_h, ol_l, up, got, b_h, b_l) = (
            sem(n) for n in "lat lat_h lat_l logit top_ok exp_ok inv shared turned pt_h pt_l pv ol_h ol_l up got b_h b_l".split())
        z_in, b_out = [sem("z_in0"), sem("z_in1")], [sem("b_out0"), sem("b_out1")]
        w_in, w_cast, w_ready = [sem("w_in0"), sem("w_in1")], sem("w_cast"), sem("w_ready")
        wo = g.w_o_dsa[0].rearrange("(k p) n -> p k n", p=P)
        block = ctx.enter_context(nc.Block())
        TURNS = H // 2
        steps = [(e, i) for e in range(2) for i in reversed(range(NT))]
        N = len(steps)
        wide = [(i + 1) * P for _, i in steps]
        bank = lambda k: g.ps[:, k * BANK:(k + 1) * BANK]

        def start(engine, *sems):
            for n in sems:
                engine.nop().then_inc(n, 1)

        @block.sync
        def _(sp):
            for u in range(2):
                sp.dma_start(g.w32[:, u], wo[:, :, u * UNIT:(u + 1) * UNIT]).then_inc(w_in[u], 16)
            for t in range(TURNS):
                for e in range(2):
                    h = 2 * t + e
                    if t:
                        sp.wait_ge(got, N * (t - 1) + NT * (e + 1) + 1)
                    sp.dma_start(z[:, e], g.sig_dram[h * P:(h + 1) * P, :]).then_inc(z_in[e], 16)
            for e in range(2):
                sp.wait_ge(b_out[e], 32 * TURNS + 1)

        @block.tensor
        def _(pe):
            mm = nc.tensor.matmul

            def queries(t, e):
                for half in range(HALVES):
                    for q in range(2):
                        n = 2 * half + q
                        pe.wait_ge(exp_ok, t * N + e * NT + 1)
                        cols = slice(half * BANK, (half + 1) * BANK)
                        head = bass.ds(t * 2 + e, 1)
                        last = three(nc.tensor, bank(n), uk_hi[:, head, q * P:(q + 1) * P], uk_lo[:, head, q * P:(q + 1) * P],
                                     q_hi[:, head, cols], q_lo[:, head, cols], True, True)
                        last.then_inc(lat, 1)
                pe.wait_ge(lat_l, t * 8 + 4 * e + 4 + 1)

            def logits(t, n):
                e, i = steps[n]
                head = bass.ds(t * 2 + e, 1)
                if n >= 2 and n != NT:
                    pe.wait_ge(exp_ok, t * N + n - 1 + 1)
                tok = slice(i * P, (i + 1) * P)
                at = (n % 2) * T
                for c0 in range(0, wide[n], BANK):
                    c1 = min(wide[n], c0 + BANK)
                    out = g.ps[:, at + c0:at + c1]
                    for q in range(2):
                        three(nc.tensor, out, lat_hi[:, q, tok], lat_lo[:, q, tok], ct_hi[:, q, c0:c1], ct_lo[:, q, c0:c1], q == 0, False)
                    n0, n1 = max(c0, (i - 1) * P, 0), min(c1, (i + 1) * P)
                    if n0 < n1:
                        b0 = n0 - (i - 1) * P
                        for part in (bias_hi, bias_lo):
                            mm(g.ps[:, at + n0:at + n1], flip_h[:], part[:, head, b0:b0 + n1 - n0], start=False, stop=False)
                    last = mm(out, ident_b[:], mask[:, g.first[i] + c0:g.first[i] + c1], start=False, stop=True)
                last.then_inc(logit, 1)

            def turn(t, n):
                e, i = steps[n]
                pe.wait_ge(shared, t * N + n + 2)
                pe.wait_ge(pt_l, t * N + n + 1)
                for j in range(i + 1):
                    last = nc.tensor.transpose(g.ps[:, 4 * BANK + j * P:4 * BANK + (j + 1) * P], p[:, n % 2, j * P:(j + 1) * P],
                                               g.const[:, K_ID:K_ID + P])
                last.then_inc(turned, 1)

            def values(t, n):
                e, i = steps[n]
                pe.wait_ge(pt_l, t * N + n + 2)
                pe.wait_ge(ol_l, t * N + n + 1)
                for q in range(2):
                    for j in range(i + 1):
                        cs = slice(q * P, (q + 1) * P)
                        last = three(nc.tensor, g.ps[:, 6 * BANK + q * P:6 * BANK + (q + 1) * P], c_hi[:, j, cs], c_lo[:, j, cs],
                                     pt_hi[:, n % 2, j], pt_lo[:, n % 2, j], j == 0, j == i)
                last.then_inc(pv, 1)

            def lift(t, n):
                e, i = steps[n]
                pe.wait_ge(ol_l, t * N + n + 2)
                pe.wait_ge(got, t * N + n + 1)
                for q in range(2):
                    cols = bass.ds((t * 2 + e) * P, P)
                    last = three(nc.tensor, g.ps[:, 7 * BANK:7 * BANK + P], uv_hi[:, q, cols], uv_lo[:, q, cols],
                                 ol_hi[:, n % 2, q], ol_lo[:, n % 2, q], q == 0, q == 1)
                last.then_inc(up, 1)

            start(pe, lat, logit, turned, pv, up)
            with pe.Fori(0, TURNS) as t:
                for n in range(N + 3):
                    if n in (0, NT):
                        queries(t, n // NT)
                    if n < N:
                        logits(t, n)
                    if 0 <= n - 1 < N:
                        turn(t, n - 1)
                    if 0 <= n - 2 < N:
                        values(t, n - 2)
                    if 0 <= n - 3 < N:
                        lift(t, n - 3)

        @block.scalar
        def _(act):
            def queries(t, e):
                for n in range(4):
                    half, q = divmod(n, 2)
                    cols = slice(half * BANK, (half + 1) * BANK)
                    act.wait_ge(lat, t * 8 + 4 * e + n + 2)
                    nc.scalar.mul(lat_hi[:, q, cols], bank(n), P ** -0.5).then_inc(lat_h, 1)

            def soften(t, n):
                act.wait_ge(top_ok, t * N + n + 2)
                act.wait_ge(turned, (t * N + n - 1 if n >= 2 else t * N) + 1)
                nc.scalar.activation(p[:, n % 2, 0:wide[n]], g.ps[:, (n % 2) * T:(n % 2) * T + wide[n]], ACT.Exp,
                                     bias=top[:, n % 2:n % 2 + 1], accum_out=total[:, n % 2:n % 2 + 1]).then_inc(exp_ok, 1)

            def split_p(t, n):
                i = steps[n][1]
                act.wait_ge(turned, t * N + n + 2)
                act.wait_ge(pv, (t * N + n - 1 if n >= 2 else t * N) + 1)
                nc.scalar.copy(pt_hi[:, n % 2, 0:i + 1], g.ps[:, 4 * BANK:4 * BANK + wide[n]].rearrange("p (j t) -> p j t", t=P)).then_inc(pt_h, 1)

            def split_o(t, n):
                act.wait_ge(pv, t * N + n + 2)
                act.wait_ge(up, (t * N + n - 1 if n >= 2 else t * N) + 1)
                nc.scalar.copy(ol_hi[:, n % 2], g.ps[:, 6 * BANK:6 * BANK + RANK].rearrange("p (q t) -> p q t", t=P)).then_inc(ol_h, 1)

            def split_b(t, n):
                e, i = steps[n]
                act.wait_ge(got, t * N + n + 2)
                if i == NT - 1:
                    act.wait_ge(b_out[e], t * 32 + 1)
                nc.scalar.copy(b_hi[:, e, i * P:(i + 1) * P], b32[:, n % 2]).then_inc(b_h, 1)
                if i == 0:
                    act.wait_ge(b_l, t * N + n + 2)
                    act.wait_ge(b_h, t * N + n + 2)
                    rows = bass.ds((t * 2 + e) * P, P)
                    act.dma_start(g.bhi_dram[rows, :], b_hi[:, e]).then_inc(b_out[e], 16)
                    act.dma_start(g.blo_dram[rows, :], b_lo[:, e]).then_inc(b_out[e], 16)

            start(act, lat_h, exp_ok, pt_h, ol_h, b_h, *b_out)
            with act.Fori(0, TURNS) as t:
                for n in range(N + 4):
                    if n in (0, NT):
                        queries(t, n // NT)
                    if n < N:
                        soften(t, n)
                    if 0 <= n - 1 < N:
                        split_p(t, n - 1)
                    if 0 <= n - 2 < N:
                        split_o(t, n - 2)
                    if 0 <= n - 3 < N:
                        split_b(t, n - 3)

        @block.vector
        def _(dve):
            def queries(t, e):
                for n in range(4):
                    half, q = divmod(n, 2)
                    cols = slice(half * BANK, (half + 1) * BANK)
                    dve.wait_ge(lat_h, t * 8 + 4 * e + n + 2)
                    nc.vector.scalar_tensor_tensor(out=lat_lo[:, q, cols], in0=bank(n), scalar=P ** -0.5, in1=lat_hi[:, q, cols],
                                                   op0=ALU.mult, op1=ALU.subtract).then_inc(lat_l, 1)

            def peak(t, n):
                dve.wait_ge(logit, t * N + n + 2)
                dve.wait_ge(exp_ok, (t * N + n - 1 if n >= 2 else t * N) + 1)
                nc.vector.tensor_reduce(top[:, n % 2:n % 2 + 1], g.ps[:, (n % 2) * T:(n % 2) * T + wide[n]], AX.X, ALU.max,
                                        negate=True).then_inc(top_ok, 1)

            def norm(t, n):
                dve.wait_ge(exp_ok, t * N + n + 2)
                nc.vector.reciprocal(share[:, n % 2:n % 2 + 1], total[:, n % 2:n % 2 + 1]).then_inc(inv, 1)
                dve.wait_ge(inv, t * N + n + 2)
                nc.vector.tensor_scalar(p[:, n % 2, 0:wide[n]], p[:, n % 2, 0:wide[n]], share[:, n % 2:n % 2 + 1], None, ALU.mult).then_inc(shared, 1)

            def split_p(t, n):
                i = steps[n][1]
                dve.wait_ge(pt_h, t * N + n + 2)
                nc.vector.tensor_tensor(pt_lo[:, n % 2, 0:i + 1], g.ps[:, 4 * BANK:4 * BANK + wide[n]].rearrange("p (j t) -> p j t", t=P),
                                        pt_hi[:, n % 2, 0:i + 1], ALU.subtract).then_inc(pt_l, 1)

            def split_o(t, n):
                dve.wait_ge(ol_h, t * N + n + 2)
                nc.vector.tensor_tensor(ol_lo[:, n % 2], g.ps[:, 6 * BANK:6 * BANK + RANK].rearrange("p (q t) -> p q t", t=P),
                                        ol_hi[:, n % 2], ALU.subtract).then_inc(ol_l, 1)

            def gate(t, n):
                e, i = steps[n]
                dve.wait_ge(up, t * N + n + 2)
                dve.wait_ge(b_l, (t * N + n - 1 if n >= 2 else t * N) + 1)
                dve.wait_ge(z_in[e], t * 16 + 16)
                nc.vector.tensor_tensor(b32[:, n % 2], g.ps[:, 7 * BANK:7 * BANK + P], z[:, e, i * P:(i + 1) * P], ALU.mult).then_inc(got, 1)

            start(dve, lat_l, top_ok, inv, shared, pt_l, ol_l, got)
            with dve.Fori(0, TURNS) as t:
                for n in range(N + 4):
                    if n in (0, NT):
                        queries(t, n // NT)
                    if n < N:
                        peak(t, n)
                        norm(t, n)
                    if 0 <= n - 1 < N:
                        split_p(t, n - 1)
                    if 0 <= n - 2 < N:
                        split_o(t, n - 2)
                    if 0 <= n - 3 < N:
                        gate(t, n - 3)

        @block.gpsimd
        def _(pool):
            for u in range(2):
                pool.wait_ge(w_in[u], 16)
                split_block(nc, pool, g.w32, g.w_hi, g.w_lo, u, w_cast, u).then_inc(w_ready, 1)
            start(pool, b_l)
            with pool.Fori(0, TURNS) as t:
                for n, (e, i) in enumerate(steps):
                    pool.wait_ge(b_h, t * N + n + 2)
                    nc.gpsimd.tensor_tensor(b_lo[:, e, i * P:(i + 1) * P], b32[:, n % 2], b_hi[:, e, i * P:(i + 1) * P], ALU.subtract).then_inc(b_l, 1)


def program(nc, g):
    scratch = lambda n, s, d=F32: nc.dram_tensor(n, s, d, kind="Internal").ap()
    g.gate_dram = scratch("gate_row", [1, D])
    g.z_dram = scratch("delta_gate", [T, D])
    g.sig_dram = scratch("channel_gates", [3 * D, T])
    g.mask_dram = scratch("mask", [P, P * NT * (NT + 1) // 2], BF16)
    g.o_dram = scratch("delta_out", [T, D])
    g.m_dram = scratch("merge_half", [D, T])
    g.rows_dram = scratch("bias_rows", [H, K_BUCKETS])
    g.bhi_dram, g.blo_dram = scratch("attended_hi", [D, T], F16), scratch("attended_lo", [D, T], F16)
    g.first = [P * i * (i + 1) // 2 for i in range(NT + 1)]
    with ExitStack() as ctx:
        g.ps = ctx.enter_context(nc.psum_tensor("ps", [P, 8 * BANK], F32))
        sb = lambda n, s, d=F32: ctx.enter_context(nc.sbuf_tensor("g_" + n, s, d))
        g.const = sb("const", [P, K_ALL])
        g.eps = sb("eps", [P, 1])
        g.sc_col = sb("sc_col", [P, KD])
        g.oss = sb("oss", [P, NT, H])
        with ExitStack() as inner:
            sb = lambda n, s, d=F32: inner.enter_context(nc.sbuf_tensor("g_" + n, s, d))
            g.h_hi, g.h_lo = sb("h_hi", [P, KD, T], F16), sb("h_lo", [P, KD, T], F16)
            with ExitStack() as tables:
                sb = lambda n, s, d=F32: tables.enter_context(nc.sbuf_tensor("g_" + n, s, d))
                g.g, g.beta, g.nbeta = sb("g", [P, NT, H]), sb("beta", [P, NT, H]), sb("nbeta", [P, NT, H])
                g.decays = sb("decays", [P, 4, NT, H])
                g.taps = sb("taps", [P, 96])
                with nc.cleanup_on_exit(), ExitStack() as early:
                    sb = lambda n, s, d=F32: early.enter_context(nc.sbuf_tensor("g_" + n, s, d))
                    g.s32, g.s_hi, g.s_lo = sb("s32", [P, KD, NS]), sb("s_hi", [P, KD, NS], F16), sb("s_lo", [P, KD, NS], BF16)
                    g.w32 = sb("early_w32", [P, 2, KD, UNIT])
                    phase_hidden(nc, g)
                    with ExitStack() as scores:
                        sb = lambda n, s, d=F32: scores.enter_context(nc.sbuf_tensor("g_" + n, s, d))
                        g.w_hi, g.w_lo = sb("early_w_hi", [P, 2, KD, UNIT], F16), sb("early_w_lo", [P, 2, KD, UNIT], BF16)
                        g.small = sb("small", [P, NT, 24])
                        g.score = sb("score", [P, g.first[NT]])
                        g.mask = sb("mask", [P, g.first[NT]], BF16)
                        phase_index(nc, g)
                        phase_topk(nc, g)
                with nc.cleanup_on_exit():
                    phase_delta(nc, g)
            sb = lambda n, s, d=F32: inner.enter_context(nc.sbuf_tensor("g_" + n, s, d))
            g.w32, g.w_hi, g.w_lo = sb("w32", [P, 2, KD, UNIT]), sb("w_hi", [P, 2, KD, UNIT], F16), sb("w_lo", [P, 2, KD, UNIT], BF16)
            with nc.cleanup_on_exit():
                phase_delta_out(nc, g)
                phase_attention(nc, g)
            with nc.cleanup_on_exit():
                phase_merge(nc, g)


INPUTS = ["x", "c", "norm_g", "w_ada", "b_ada", "w_in", "conv_w", "a_log", "dt_bias", "gdn_norm_g", "w_o_gdn",
          "kv_norm_g", "w_uk", "w_uv", "w_o_dsa", "w_out", "rel_bias", "final_g"]


def kernel(**inputs):
    import concourse.bacc as bacc
    from concourse.bass_utils import run_bass_kernel_spmd

    nc = bacc.Bacc("TRN2", target_bir_lowering=False, num_devices=1)
    g = Tensors()
    arrays = {"in_" + n: np.ascontiguousarray(inputs[n]) for n in INPUTS}
    arrays["in_const_dram"], arrays["in_buckets_dram"] = constant_table(), bucket_table()
    for n, a in arrays.items():
        g.__dict__[n.removeprefix("in_")] = nc.dram_tensor(n, a.shape, F32, kind="ExternalInput").ap()
    g.out = nc.dram_tensor("out", [1, T, D], F32, kind="ExternalOutput").ap()
    program(nc, g)
    r = run_bass_kernel_spmd(nc, [arrays], core_ids=[0])
    return r.results[0]["out"]
```
